# Optimizing a Trainium2 kernel written in Bass

```python
import jax, jax.numpy as jnp
from jax import lax
import numpy as np

D_MODEL = 1024
BATCH = 1
SEQ = 512
DEPTH = 1
DEC_BATCH = 8
DEC_SEQ = 1
PAST_LEN = 4096
PAGE_SIZE = 128

D_MIX = D_MODEL
W_A = D_MIX // 2
W_B = D_MIX - W_A
HGRN_HEAD_DIM = 128
H_A = W_A // HGRN_HEAD_DIM
DK = HGRN_HEAD_DIM
DV = HGRN_HEAD_DIM
CHUNK = 64
LRU_BLOCKS = 8
LRU_BLOCK_DIM = W_B // LRU_BLOCKS
CONV_W = 4
LRU_C = 8.0
N_GROUPS = 4
EXPERTS_PER_GROUP = 8
N_EXPERTS = N_GROUPS * EXPERTS_PER_GROUP
TOP_K_IN_GROUP = 2
D_EXPERT = D_MODEL // 4
IN_COLS = 4 * W_A + 2 * W_B
EPS = 1e-6

kernel_name = "hymba_style_hgrn2_rglru_hiermoe_step"

F32 = jnp.float32

def _rmsnorm(x, g):
    xf = x.astype(F32)
    y = xf * lax.rsqrt(jnp.mean(xf * xf, axis=-1, keepdims=True) + EPS) * g.astype(F32)
    return y.astype(x.dtype)

def _hgrn_chunk(S, inp):
    q, k, v, logf = inp
    C = q.shape[2]
    b = jnp.cumsum(logf, axis=2)
    causal = jnp.tril(jnp.ones((C, C), bool))[None, None, :, :, None]
    diff = b[:, :, :, None, :] - b[:, :, None, :, :]
    decay = jnp.where(causal, jnp.exp(jnp.where(causal, diff, 0.0)), 0.0)
    scores = jnp.sum(q[:, :, :, None, :] * k[:, :, None, :, :] * decay, axis=-1)
    o = (jnp.einsum('bhts,bhse->bhte', scores, v)
         + jnp.einsum('bhtd,bhde->bhte', q * jnp.exp(b), S))
    b_last = b[:, :, -1:, :]
    S_new = (jnp.exp(b_last[:, :, 0, :])[..., None] * S
             + jnp.einsum('bhsd,bhse->bhde', k * jnp.exp(b_last - b), v))
    return S_new, o

def _hgrn2(q, k, v, logf, S0):
    B, L = q.shape[0], q.shape[1]
    c = min(CHUNK, L)
    n = -(-L // c)
    pad = n * c - L

    def blocks(t):
        t = jnp.pad(t, ((0, 0), (0, pad), (0, 0), (0, 0)))
        return t.reshape(B, n, c, H_A, t.shape[-1]).transpose(1, 0, 3, 2, 4)

    S, o = lax.scan(_hgrn_chunk, S0, (blocks(q), blocks(k), blocks(v), blocks(logf)))
    o = o.transpose(1, 0, 3, 2, 4).reshape(B, n * c, H_A, DV)[:, :L]
    return o, S

def _causal_conv(x, buf, w, b):
    L = x.shape[1]
    xx = jnp.concatenate([buf.astype(x.dtype), x], axis=1)
    y = b + sum(xx[:, i:i + L] * w[i] for i in range(CONV_W))
    return y, xx[:, -(CONV_W - 1):]

def _linear_scan(a, u, h0):
    u = u.at[:, 0].add(a[:, 0] * h0)

    def comb(l, r):
        al, bl = l
        ar, br = r
        return al * ar, ar * bl + br

    _, h = lax.associative_scan(comb, (a, u), axis=1)
    return h

def _rglru(xc, h0, fresh, wx, bx, wa, ba, lam):
    B, L, _ = xc.shape
    xf = xc.astype(F32)
    xb = xf.reshape(B, L, LRU_BLOCKS, LRU_BLOCK_DIM)
    gate_x = jax.nn.sigmoid(jnp.einsum('blnc,ncd->blnd', xb, wx.astype(F32)).reshape(B, L, W_B) + bx.astype(F32))
    gate_a = jax.nn.sigmoid(jnp.einsum('blnc,ncd->blnd', xb, wa.astype(F32)).reshape(B, L, W_B) + ba.astype(F32))
    log_a = -LRU_C * gate_a * jax.nn.softplus(-lam.astype(F32))
    a = jnp.exp(log_a)
    mult = jnp.sqrt(-jnp.expm1(2.0 * log_a))
    if fresh:
        reset = (jnp.arange(L) == 0)[None, :, None]
        mult = jnp.where(reset, 1.0, mult)
        a = jnp.where(reset, 0.0, a)
    h = _linear_scan(a, gate_x * xf * mult, h0.astype(F32))
    return h, h[:, -1]

def _mixer(xn, S0, h0, buf0, fresh, lb, w_in, hg_g, conv_w, conv_b, wx, bx, wa, ba, lam, w_out):
    B, L, _ = xn.shape
    proj = xn @ w_in
    q, fx, v, g, xr, gr = jnp.split(
        proj, [W_A, 2 * W_A, 3 * W_A, 4 * W_A, 4 * W_A + W_B], axis=-1)
    f = lb + (1.0 - lb) * jax.nn.sigmoid(fx.astype(F32))
    logf = jnp.log(f)
    k = 1.0 - f
    hs = lambda t: t.astype(F32).reshape(B, L, H_A, -1)
    o, S_new = _hgrn2(hs(q), hs(k), hs(v), hs(logf), S0.astype(F32))
    o = o * lax.rsqrt(jnp.mean(o * o, axis=-1, keepdims=True) + EPS) * hg_g.astype(F32).reshape(H_A, DV)
    ya = (o.reshape(B, L, W_A) * jax.nn.silu(g.astype(F32))).astype(xn.dtype)
    xc, buf_new = _causal_conv(xr, buf0, conv_w, conv_b)
    h, h_last = _rglru(xc, h0, fresh, wx, bx, wa, ba, lam)
    yb = (h * jax.nn.gelu(gr.astype(F32))).astype(xn.dtype)
    out = jnp.concatenate([ya, yb], axis=-1) @ w_out
    return out, S_new, h_last, buf_new

def _hier_moe(xn, wg, bg, we, be, w1, w3, w2):
    B, L, D = xn.shape
    xt = xn.reshape(B * L, D)
    xf = xt.astype(F32)
    p_group = jax.nn.softmax(xf @ wg.astype(F32) + bg.astype(F32), axis=-1)
    p_top, g_idx = lax.top_k(p_group, 1)
    logits = jnp.einsum('td,gde->tge', xf, we.astype(F32)) + be.astype(F32)
    sel = jnp.take_along_axis(logits, g_idx[:, :, None], axis=1)[:, 0]
    top_l, e_idx = lax.top_k(sel, TOP_K_IN_GROUP)
    w = jax.nn.softmax(top_l, axis=-1) * p_top
    flat = g_idx * EXPERTS_PER_GROUP + e_idx
    gates = jnp.sum(jax.nn.one_hot(flat, N_EXPERTS, dtype=F32) * w[..., None], axis=1)
    h = jax.nn.silu(jnp.einsum('td,edf->tef', xt, w1)) * jnp.einsum('td,edf->tef', xt, w3)
    h = h * gates[:, :, None].astype(h.dtype)
    y = jnp.einsum('tef,efd->td', h, w2)
    return y.reshape(B, L, D).astype(xn.dtype)

def _trunk(x, S0, h0, buf0, fresh, p):
    (lower_bounds, ln1_g, w_in, hgrn_norm_g, conv_w, conv_b, lru_wx, lru_bx, lru_wa, lru_ba,
     lru_lambda, w_out, ln2_g, router_wg, router_bg, router_we, router_be,
     exp_w1, exp_w3, exp_w2, final_g) = p
    lbs = jnp.cumsum(jax.nn.softmax(lower_bounds.astype(F32), axis=0), axis=0)
    Ss, hs, bufs = [], [], []
    for l in range(DEPTH):
        xn = _rmsnorm(x, ln1_g[l])
        mix, S, h, buf = _mixer(xn, S0[l], h0[l], buf0[l], fresh, lbs[l], w_in[l], hgrn_norm_g[l],
                                conv_w[l], conv_b[l], lru_wx[l], lru_bx[l], lru_wa[l], lru_ba[l],
                                lru_lambda[l], w_out[l])
        x = x + mix
        x = x + _hier_moe(_rmsnorm(x, ln2_g[l]), router_wg[l], router_bg[l], router_we[l],
                          router_be[l], exp_w1[l], exp_w3[l], exp_w2[l])
        Ss.append(S)
        hs.append(h)
        bufs.append(buf)
    return _rmsnorm(x, final_g), jnp.stack(Ss), jnp.stack(hs), jnp.stack(bufs)

def setup_inputs(seed: int = 0) -> dict:
    key = jax.random.key(seed)
    ks = jax.random.split(key, 32)
    nrm = lambda k, shape, s: jax.random.normal(k, shape, F32) * s
    a0 = jax.random.uniform(ks[0], (DEPTH, W_B), F32, 0.9, 0.999)
    s = a0 ** (1.0 / LRU_C)
    lam = jnp.log(s) - jnp.log1p(-s)
    return {
        "x_prompt": nrm(ks[1], (BATCH, SEQ, D_MODEL), 1.0),
        "x_sample": nrm(ks[2], (DEC_BATCH, DEC_SEQ, D_MODEL), 1.0),
        "state_hgrn": nrm(ks[3], (DEPTH, DEC_BATCH, H_A, DK, DV), 0.5),
        "state_rglru": nrm(ks[4], (DEPTH, DEC_BATCH, W_B), 0.5),
        "state_conv": nrm(ks[5], (DEPTH, DEC_BATCH, CONV_W - 1, W_B), 1.0),
        "lower_bounds": nrm(ks[6], (DEPTH + 1, W_A), 0.1),
        "ln1_g": 1.0 + nrm(ks[7], (DEPTH, D_MODEL), 0.02),
        "w_in": nrm(ks[8], (DEPTH, D_MODEL, IN_COLS), D_MODEL ** -0.5),
        "hgrn_norm_g": 1.0 + nrm(ks[9], (DEPTH, W_A), 0.02),
        "conv_w": nrm(ks[10], (DEPTH, CONV_W, W_B), CONV_W ** -0.5),
        "conv_b": nrm(ks[11], (DEPTH, W_B), 0.01),
        "lru_wx": nrm(ks[12], (DEPTH, LRU_BLOCKS, LRU_BLOCK_DIM, LRU_BLOCK_DIM), LRU_BLOCK_DIM ** -0.5),
        "lru_bx": nrm(ks[13], (DEPTH, W_B), 0.01),
        "lru_wa": nrm(ks[14], (DEPTH, LRU_BLOCKS, LRU_BLOCK_DIM, LRU_BLOCK_DIM), LRU_BLOCK_DIM ** -0.5),
        "lru_ba": nrm(ks[15], (DEPTH, W_B), 0.01),
        "lru_lambda": lam,
        "w_out": nrm(ks[16], (DEPTH, D_MIX, D_MODEL), D_MIX ** -0.5),
        "ln2_g": 1.0 + nrm(ks[17], (DEPTH, D_MODEL), 0.02),
        "router_wg": nrm(ks[18], (DEPTH, D_MODEL, N_GROUPS), D_MODEL ** -0.5),
        "router_bg": nrm(ks[19], (DEPTH, N_GROUPS), 0.01),
        "router_we": nrm(ks[20], (DEPTH, N_GROUPS, D_MODEL, EXPERTS_PER_GROUP), D_MODEL ** -0.5),
        "router_be": nrm(ks[21], (DEPTH, N_GROUPS, EXPERTS_PER_GROUP), 0.01),
        "exp_w1": nrm(ks[22], (DEPTH, N_EXPERTS, D_MODEL, D_EXPERT), D_MODEL ** -0.5),
        "exp_w3": nrm(ks[23], (DEPTH, N_EXPERTS, D_MODEL, D_EXPERT), D_MODEL ** -0.5),
        "exp_w2": nrm(ks[24], (DEPTH, N_EXPERTS, D_EXPERT, D_MODEL), D_EXPERT ** -0.5),
        "final_g": 1.0 + nrm(ks[25], (D_MODEL,), 0.02),
    }

def reference(x_prompt, x_sample, state_hgrn, state_rglru, state_conv, lower_bounds, ln1_g, w_in,
              hgrn_norm_g, conv_w, conv_b, lru_wx, lru_bx, lru_wa, lru_ba, lru_lambda, w_out, ln2_g,
              router_wg, router_bg, router_we, router_be, exp_w1, exp_w3, exp_w2, final_g):
    p = (lower_bounds, ln1_g, w_in, hgrn_norm_g, conv_w, conv_b, lru_wx, lru_bx, lru_wa, lru_ba,
         lru_lambda, w_out, ln2_g, router_wg, router_bg, router_we, router_be,
         exp_w1, exp_w3, exp_w2, final_g)
    S0p = jnp.zeros((DEPTH, BATCH, H_A, DK, DV), F32)
    h0p = jnp.zeros((DEPTH, BATCH, W_B), F32)
    b0p = jnp.zeros((DEPTH, BATCH, CONV_W - 1, W_B), x_prompt.dtype)
    y_prompt, hg_p, lru_p, conv_p = _trunk(x_prompt, S0p, h0p, b0p, True, p)
    y_sample, hg_s, lru_s, conv_s = _trunk(x_sample, state_hgrn, state_rglru, state_conv, False, p)
    return (y_prompt, y_sample,
            hg_p.astype(state_hgrn.dtype), lru_p.astype(state_rglru.dtype), conv_p.astype(state_conv.dtype),
            hg_s.astype(state_hgrn.dtype), lru_s.astype(state_rglru.dtype), conv_s.astype(state_conv.dtype))


_drawn_inputs = setup_inputs


def setup_inputs(seed=0):
    import zlib

    import numpy as np

    out = dict(_drawn_inputs(seed))
    spreads = {}
    factors = {'lru_bx': 15.476,
     'lru_ba': 24.003,
     'router_bg': 17.35,
     'router_be': 21.442,
     'final_g': 22.01,
     'hgrn_norm_g': 4.159,
     'ln2_g': 4.829}
    for name, (base, spread) in spreads.items():
        noise = np.random.default_rng([zlib.crc32(name.encode()), seed]).standard_normal(out[name].shape)
        drawn = base * np.exp(spread * noise) if base else spread * noise
        out[name] = __import__('jax').numpy.asarray(drawn.astype(out[name].dtype))
    for name, factor in factors.items():
        out[name] = (out[name] * factor).astype(out[name].dtype)
    return out
```

```python
from contextlib import ExitStack
from math import pi, sqrt

import concourse.bass as bass
from concourse import mybir

F32 = mybir.dt.float32
I32 = mybir.dt.int32
U32 = mybir.dt.uint32
ALU = mybir.AluOpType
ACT = mybir.ActivationFunctionType
AX_X = mybir.AxisListType.X

P = 128
D = 1024
SEQ, NS = 512, 8
TOK = SEQ + NS
HALF = TOK // 2
KD = D // P
NH = 4
CH = SEQ // P
NT = CH + 1
ROWS = [P] * CH + [NS]
GROUPS, PER_GROUP = 4, 8
NE = GROUPS * PER_GROUP
FE = 256
NR = 3
BIG = 4096
EPS = 1e-6
SUB = 32

LB, HGG, CW, CB, BX, BA, LAM, H0 = 0, 8, 12, 28, 32, 36, 40, 44
NPAR = H0 + NS * NH
V_FA, V_FB, V_NFB, V_C, V_NC, V_BX, V_BA, V_HG, V_T0, V_T1, V_T2, V_T3 = range(0, 48, 4)

XR, FX, Q, V, GR, G = 4, 1, 0, 2, 5, 3
ORDER = [XR, FX, Q, V, GR, G]


def rotation():
    r = []
    for i in range(NT):
        r += [("xt", i, 0), ("xt", i, 1)]
    r += [("par", 0), ("par", 1)]
    for name in ("xr", "fx"):
        r += [(name, m, h) for m in range(NH) for h in range(2)]
    for m in range(NH):
        r += [("q", m, 0), ("q", m, 1)]
        r += [(g, m, h) for g in ("gx", "ga") for h in range(2)]
    r += [("v", c) for c in range(NT)]
    r += [("xtail",)]
    for s in range(8):
        r += [("gr" if s < 4 else "g", s % 4, 0), ("gr" if s < 4 else "g", s % 4, 1)]
        if s % 2 and s >= 3:
            r += [("mean", (s - 3) // 2)]
        r += [("vb", s)]
    r += [("mean", 3), ("mean", 4), ("htail",)]
    for c in range(NT + 1):
        if c < NT:
            r += [("op", c, 0), ("op", c, 1)]
        if c > 0:
            r += [("x2t", c - 1, 0), ("x2t", c - 1, 1), ("lg", c - 1)]
    r += [("pos",)]
    return {name: (n % NR, n // NR) for n, name in enumerate(r)}


ROT = rotation()


def build(nc, x_prompt, x_sample, state_hgrn, state_rglru, state_conv, lower_bounds, ln1_g, w_in,
          hgrn_norm_g, conv_w, conv_b, lru_wx, lru_bx, lru_wa, lru_ba, lru_lambda, w_out, ln2_g,
          router_wg, router_bg, router_we, router_be, exp_w1, exp_w3, exp_w2, final_g,
          y_prompt, y_sample, hgrn_p, rglru_p, conv_p, hgrn_s, rglru_s, conv_s):
    xn_dram = nc.dram_tensor("xn_rows", (TOK, D), F32).ap()
    ye_dram = nc.dram_tensor("expert_rows", (2 * TOK, D), F32).ap()

    def x_rows(i):
        return x_prompt[0, i * P:(i + 1) * P, :] if i < CH else x_sample.rearrange("b s d -> (b s) d")

    def y_rows(i):
        return y_prompt[0, i * P:(i + 1) * P, :] if i < CH else y_sample.rearrange("b s d -> (b s) d")

    with ExitStack() as ctx:
        def sb(name, shape, dt=F32):
            return ctx.enter_context(nc.sbuf_tensor(name, shape, dt))

        def sem(name):
            return ctx.enter_context(nc.semaphore(name))

        X = sb("X", [P, NT, D])
        XS = sb("XS", [P, 2, D])
        XNT = sb("XNT", [P, KD, TOK])
        WC = sb("WC", [P, 2, KD, 512])
        SLOT0 = sb("SLOT0", [P, 6144])
        GXt = SLOT0[:, 0:NH * TOK].rearrange("p (m t) -> p m t", m=NH)
        GAt = SLOT0[:, NH * TOK:2 * NH * TOK].rearrange("p (m t) -> p m t", m=NH)
        XCt = sb("XCt", [P, NH, TOK])
        SLOT1 = sb("SLOT1", [P, 3 * NH * TOK])
        Ft = SLOT1[:, 0:NH * TOK].rearrange("p (m t) -> p m t", m=NH)
        Kt = SLOT1[:, NH * TOK:2 * NH * TOK].rearrange("p (m t) -> p m t", m=NH)
        Qt = SLOT1[:, 2 * NH * TOK:3 * NH * TOK].rearrange("p (m t) -> p m t", m=NH)
        XRt = sb("XRt", [P, NH, TOK + 3])
        GY = sb("GY", [P, 2 * NH, TOK])
        Vt = sb("Vt", [P, CH, 512])
        Vs = sb("Vs", [NS, 512])
        T = sb("T", [P, 2, 6, 512])
        TN = T[:, 0, 0:5, :].rearrange("p a t -> p (a t)")[:, 0:NH * TOK].rearrange("p (m t) -> p m t", m=NH)
        A2 = T[:, 1, 0:5, :].rearrange("p a t -> p (a t)")[:, 0:NH * TOK].rearrange("p (m t) -> p m t", m=NH)
        SC = SLOT0[:, 0:1024].rearrange("p (a c t) -> p a c t", a=2, c=CH)
        S = SLOT0[:, 1024:2048].rearrange("p (a c t) -> p a c t", a=2, c=CH)
        KT = SLOT0[:, 2048:2560].rearrange("p (c t) -> p c t", c=CH)
        NB = SLOT0[:, 2560:3072]
        SST = XS[:, 1, :].rearrange("p (a t) -> p a t", a=2)
        SKV = XS[:, 0, 0:512]
        OS = sb("OS", [P, NH * NS])
        OSB = sb("OSB", [P, NH * NS])
        AC = sb("AC", [P, NH, CH])
        PROW = sb("PROW", [NPAR, P])
        CROW = sb("CROW", [NS * 3 * NH, P])
        PARAM = sb("PARAM", [P, NPAR])
        CVT = sb("CVT", [P, NS * 3 * NH])
        VEC = sb("VEC", [P, 48])
        G1 = sb("G1", [P, KD])
        G2 = sb("G2", [P, KD])
        BDX = sb("BDX", [P, NH, P])
        BDA = sb("BDA", [P, NH, P])
        TAIL = BDX[0:11, :, :].rearrange("p m t -> p (m t)")
        HTAIL = BDA[0:9, :, :].rearrange("p m t -> p (m t)")
        SSQ = sb("SSQ", [P, NT])
        RSTD = sb("RSTD", [P, NT])
        EPSC = sb("EPSC", [P, 1])
        IDENT = sb("IDENT", [P, P])
        MEAN128 = sb("MEAN128", [P, P])
        ONES = sb("ONES", [P, P])
        LTRI = sb("LTRI", [P, P])
        CMASK = sb("CMASK", [P, P])
        RESET = sb("RESET", [P, CH, P])
        SCR = sb("SCR", [P, 8, NS])
        V_FLAT = Vt[:, :, :].rearrange("p c t -> p (c t)")
        used = [0]

        def over_v(shape):
            n = 1
            for x in shape[1:]:
                n *= x
            v = V_FLAT[:, used[0]:used[0] + n]
            used[0] += n
            if len(shape) == 3:
                return v.rearrange("p (a b) -> p a b", a=shape[1])
            return v.rearrange("p (k a b) -> p k a b", k=shape[1], a=shape[2])

        WGt = sb("WGt", [P, KD * GROUPS])
        WEt = sb("WEt", [P, GROUPS, KD * PER_GROUP])
        WR = sb("WR", [P, KD, GROUPS + NE])
        RB = sb("RB", [P, GROUPS + NE])
        LG = over_v([P, NT, GROUPS + NE])
        L8 = over_v([P, NT, 8])
        TOP = over_v([P, NT, 8])
        TIX = sb("TIX", [P, NT, 8], U32)
        GIX = sb("GIX", [P, NT])
        GEX = over_v([P, NT, GROUPS])
        PTOP = sb("PTOP", [P, NT])
        LSEL = over_v([P, NT, NE])
        LMSK = over_v([P, NT, NE])
        EIX = sb("EIX", [P, NT, 2])
        OH = over_v([P, 2, NT, NE])
        OHV = over_v([P, 2, NT, NE])
        RANK = sb("RANK", [P, 2, NT])
        WK = sb("WK", [P, 2, NT])
        CNT = sb("CNT", [P, 2])
        NRND = sb("NRND", [P, 1], I32)
        IOI = SLOT1[:, 2 * NH * TOK:2 * NH * TOK + 2 * NE + P + 2 * NT].bitcast(I32)
        IOF = sb("IOF", [P, NE + NE + P + 2 * NT])
        iota_e, iota_g = IOF[:, 0:NE], IOF[:, NE:2 * NE]
        iota_s = IOF[:, 2 * NE:2 * NE + P]
        token_code = IOF[:, 2 * NE + P:].rearrange("p (i k) -> p k i", k=2)
        PM = over_v([P, 2, P])
        DSTI = sb("DSTI", [P, NE + 1], I32)
        SRCI = sb("SRCI", [P, NE + 1], I32)
        GIDX = sb("GIDX", [P, 2, 1], I32)
        SIDX = sb("SIDX", [P, 2, 1], I32)
        XG = [T[:, j, 0:2, :].rearrange("p a t -> p (a t)") for j in range(2)]
        YO = [T[:, j, 2:4, :].rearrange("p a t -> p (a t)") for j in range(2)]
        GYF = GY[:, :, :].rearrange("p m t -> p (m t)")
        XGT = [GYF[:, 1024 * j:1024 * (j + 1)].rearrange("p (k t) -> p k t", k=KD) for j in range(2)]
        HS = [GYF[:, 2048 + FE * j:2048 + FE * (j + 1)] for j in range(2)]
        HG = [GYF[:, 2560 + FE * j:2560 + FE * (j + 1)] for j in range(2)]
        HT = [GYF[:, 3072 + FE * j:3072 + FE * (j + 1)].rearrange("p (j t) -> p j t", j=2) for j in range(2)]
        W1 = [s[:, 0:2048].rearrange("p (k f) -> p k f", k=KD) for s in (SLOT0, SLOT1)]
        W3 = [s[:, 2048:4096].rearrange("p (k f) -> p k f", k=KD) for s in (SLOT0, SLOT1)]
        W2 = [s[:, 4096:6144].rearrange("p (j d) -> p j d", j=2) for s in (SLOT0, SLOT1)]
        YE = [XNT[:, 0:4, 0:512], XNT[:, 4:8, 0:512]]
        FGB = WC[:, 0, 0:2, :].rearrange("p a t -> p (a t)")
        OUT = [WC[:, 0, 2:4, :].rearrange("p a t -> p (a t)"), WC[:, 0, 4:6, :].rearrange("p a t -> p (a t)")]

        PS = [ctx.enter_context(nc.psum_tensor(f"ps{b}", [P, 512], F32)) for b in range(8)]
        B_OS, B_SD, B_SL, B_KV, B_O = 3, 4, 5, 6, 7

        s_x = [sem(f"x_in{i}") for i in range(NT)]
        s_wc = [sem(f"wc_in{i}") for i in range(2)]
        s_wc_free = sem("wc_free")
        s_par = sem("param_rows_in")
        s_gain = sem("gains_in")
        s_bd = sem("gate_weights_in")
        s_rt = sem("router_weights_in")
        s_written = [sem(f"rot_written{i}") for i in range(NR)]
        s_read = [sem(f"rot_read{i}") for i in range(NR)]
        s_const = sem("constants_made")
        s_init = sem("scratch_initialised")
        s_pool = sem("pool_step")
        s_zero = sem("zeroed")
        s_zero_sc = sem("scores_zeroed")
        s_ssq = sem("squares_summed")
        s_rstd = sem("rstd_step")
        s_xs = sem("rows_scaled")
        s_xst = sem("rows_transposed")
        s_param = sem("param_ready")
        s_vec = sem("vec_step")
        s_vexp = sem("vec_exp")
        s_conv = sem("conv_step")
        s_xc = sem("xc_ready")
        s_f = sem("f_ready")
        s_gt = sem("gate_tanh_ready")
        s_a = sem("decay_a_ready")
        s_m2 = sem("mult_squared_ready")
        s_mu = sem("mult_ready")
        s_u = sem("u_step")
        s_h = sem("h_ready")
        s_k = sem("k_ready")
        s_lf = sem("logf_ready")
        s_b = sem("cumulated_ready")
        s_d = sem("exponents_ready")
        s_e = sem("decays_ready")
        s_ac = sem("chunk_decay_ready")
        s_qk = sem("decayed_qk_ready")
        s_scores = sem("scores_written")
        s_kt_ps = sem("kt_written")
        s_kt = sem("kt_ready")
        s_sc = sem("scores_ready")
        s_kv = sem("kv_written")
        s_s = sem("states_ready")
        s_o = sem("o_written")
        s_osq = sem("o_squared")
        s_rs = sem("head_rstd_step")
        s_yn = sem("y_normed")
        s_gel = sem("gelu_step")
        s_gela = sem("gelu_act")
        s_yb = sem("y_b_ready")
        s_tg = sem("g_tanh_ready")
        s_sg = sem("silu_ready")
        s_y = sem("y_a_ready")
        s_skv = sem("sample_kv_step")
        s_sst = sem("sample_state_ready")
        s_sin = [sem(f"sample_state_in{i}") for i in range(2)]
        s_sout = [sem(f"sample_state_out{i}") for i in range(2)]
        s_osw = sem("sample_o_written")
        s_oss = sem("sample_o_step")
        s_tail = sem("tails_ready")
        s_small_out = sem("small_outputs_written")
        s_hp = sem("hgrn_state_written")
        s_xn = [sem(f"xn_rows_written{i}") for i in range(2)]
        s_lg = sem("logits_ready")
        s_r = sem("router_step")
        s_rexp = sem("router_exp")
        s_oh = sem("onehots_ready")
        s_rnd = sem("rounds_known")
        s_pm = sem("slot_onehot_ready")
        s_pmu = sem("slot_onehot_used")
        s_tab = sem("table_written")
        s_tabr = sem("table_ready")
        s_tabs = sem("table_step")
        s_turn = sem("pool_turns")
        s_gi = sem("gather_index_copied")
        s_si = sem("scatter_index_copied")
        s_xg = [sem(f"rows_gathered{i}") for i in range(2)]
        s_ys = [sem(f"rows_scattered{i}") for i in range(2)]
        s_w13 = [sem(f"w13_in{i}") for i in range(2)]
        s_w2 = [sem(f"w2_in{i}") for i in range(2)]
        s_tw = sem("xg_transposed")
        s_xgt = sem("xgt_ready")
        s_hw = sem("h_written")
        s_silu = sem("silu_done")
        s_hg = sem("h_gated")
        s_htw = sem("h_transposed")
        s_ht = sem("ht_ready")
        s_yw = sem("y_written")
        s_ya = sem("y_half_a_read")
        s_yd = sem("y_half_b_read")
        s_rdone = sem("round_done")
        s_fg = sem("final_gain_in")
        s_ye = [sem(f"expert_rows_in{i}") for i in range(2)]
        s_cmb = sem("combine_step")
        s_fr = sem("final_rstd_step")
        s_fin = sem("final_ready")
        s_out = [sem(f"y_out{i}") for i in range(2)]

        def claim(pe, name):
            bank, use = ROT[name]
            if use > 0:
                pe.wait_ge(s_read[bank], use)
            return PS[bank]

        def written(ins, name):
            ins.then_inc(s_written[ROT[name][0]], 1)

        def await_ps(eng, name):
            bank, use = ROT[name]
            eng.wait_ge(s_written[bank], use + 1)
            return PS[bank]

        def read(ins, name):
            ins.then_inc(s_read[ROT[name][0]], 1)

        def await_read(eng, name):
            eng.wait_ge(s_read[ROT[name][0]], ROT[name][1] + 1)

        def bc(ap, axis, n):
            ap = ap.unsqueeze(axis)
            shape = list(ap.shape)
            shape[axis] = n
            return ap.to_broadcast(shape)

        def col(v, m):
            return VEC[:, v + m:v + m + 1]

        block = ctx.enter_context(nc.Block())

        @block.sync
        def _(sp):
            sp.dma_start(X[:, 0, :], x_rows(0)).then_inc(s_x[0], 16)
            for i in range(1, NT):
                sp.dma_start(X[0:ROWS[i], i, :], x_rows(i)).then_inc(s_x[i], 16)
            w_in_v = w_in[0].rearrange("(p k) n -> p k n", k=KD)
            w_out_v = w_out[0].rearrange("(m p) n -> p m n", p=P)
            for j in range(8):
                if j >= 2:
                    sp.wait_ge(s_wc_free, j - 1)
                src = w_in_v[:, :, ORDER[j] * 512:(ORDER[j] + 1) * 512] if j < 6 else w_out_v[:, :, (j - 6) * 512:(j - 5) * 512]
                sp.dma_start(WC[:, j % 2, :, :], src).then_inc(s_wc[j % 2], 16)

            def load_w13(e, p):
                sp.dma_start(W1[p], exp_w1[0, e].rearrange("(p k) f -> p k f", k=KD)).then_inc(s_w13[p], 16)
                sp.dma_start(W3[p], exp_w3[0, e].rearrange("(p k) f -> p k f", k=KD)).then_inc(s_w13[p], 16)

            def load_w2(e, p):
                sp.dma_start(W2[p], exp_w2[0, e].rearrange("(p j) d -> p j d", j=2)).then_inc(s_w2[p], 16)

            def first(p):
                load_w13(p, p)
                load_w2(p, p)

            sp.wait_ge(s_y, NH + 1)
            sp.wait_ge(s_hp, 16 * NH)
            first(0)
            first(1)

            for c in range(NT):
                sp.wait_ge(s_xs, NT + c + 1)
                sp.dma_start(xn_dram[c * P:c * P + ROWS[c], :], XS[0:ROWS[c], c % 2, :]).then_inc(s_xn[c % 2], 16)

            sp.wait_ge(s_rnd, 1)
            rounds = sp.value_load(NRND[0:1, 0:1], min_val=1, max_val=5)
            with sp.Fori(0, rounds) as r:
                with sp.If(r > 0):
                    for p in range(2):
                        sp.wait_ge(s_hw, r * NE)
                        load_w13(p, p)
                        sp.wait_ge(s_yw, r * NE)
                        load_w2(p, p)
                with sp.Fori(0, NE // 2 - 1) as i:
                    for p in range(2):
                        n = r * NE + i * 2 + p
                        e = i * 2 + p + 2
                        sp.wait_ge(s_hw, n + 1)
                        load_w13(e, p)
                        sp.wait_ge(s_yw, n + 1)
                        load_w2(e, p)

            sp.dma_start(FGB, final_g.rearrange("(a d) -> a d", a=1).partition_broadcast(P)).then_inc(s_fg, 16)
            sp.wait_ge(s_rdone, rounds + 1)
            ye_v = ye_dram.rearrange("(t k) d -> t (k d)", k=2)
            for c in range(NT):
                if c >= 2:
                    sp.wait_ge(s_cmb, 2 * (c - 1))
                sp.dma_start(YE[c % 2][0:ROWS[c]], ye_v[c * P:c * P + ROWS[c], :].rearrange("t (a d) -> t a d", a=4)).then_inc(s_ye[c % 2], 16)
                if c >= 1:
                    sp.wait_ge(s_fin, c)
                    sp.dma_start(y_rows(c - 1), OUT[(c - 1) % 2][0:ROWS[c - 1]]).then_inc(s_out[(c - 1) % 2], 16)
            sp.wait_ge(s_fin, NT)
            sp.dma_start(y_rows(NT - 1), OUT[(NT - 1) % 2][0:NS]).then_inc(s_out[(NT - 1) % 2], 16)
            sp.wait_ge(s_out[0], 16 * 3)
            sp.wait_ge(s_out[1], 16 * 2)

        @block.gpsimd
        def _(pool):
            step = [0]

            def chain(ins):
                step[0] += 1
                ins.then_inc(s_pool, 1)
                pool.wait_ge(s_pool, step[0])

            chain(pool.memset(IDENT[:], 0.0))
            pool.affine_select(out=IDENT[:], in_=IDENT[:], compare_op=ALU.not_equal, fill=1.0, base=0,
                               pattern=[[-1, P]], channel_multiplier=1).then_inc(s_const, 1)
            chain(pool.memset(BDX[:], 0.0))
            chain(pool.memset(BDA[:], 0.0))
            for bd, w in ((BDX, lru_wx), (BDA, lru_wa)):
                wv = w[0].rearrange("(m two) c d -> two c m d", two=2)
                for two in range(2):
                    pool.dma_start(bd[64 * two:64 * two + 64, :, 64 * two:64 * two + 64], wv[two]).then_inc(s_bd, 16)
            st_v = state_hgrn[0].rearrange("b h d e -> b d h e")
            so_v = hgrn_s[0].rearrange("b h d e -> b d h e")

            def load_state(b):
                pool.dma_start(SST[:, b % 2, :].rearrange("p (h e) -> p h e", h=NH), st_v[b]).then_inc(s_sin[b % 2], 16)

            pool.memset(ONES[:], 1.0).then_inc(s_pool, 1)
            pool.memset(MEAN128[:], 1.0 / P).then_inc(s_pool, 1)
            pool.memset(LTRI[:], 1.0).then_inc(s_pool, 1)
            pool.memset(CMASK[:], 1.0).then_inc(s_pool, 1)
            step[0] += 4
            pool.wait_ge(s_pool, step[0])
            chain(pool.affine_select(out=LTRI[:], in_=LTRI[:], compare_op=ALU.is_gt, fill=0.0, base=0,
                                     pattern=[[1, P]], channel_multiplier=-1))
            chain(pool.affine_select(out=CMASK[:], in_=CMASK[:], compare_op=ALU.is_ge, fill=0.0, base=0,
                                     pattern=[[1, P]], channel_multiplier=-1))
            for blk in range(P // SUB):
                part = CMASK[SUB * blk:SUB * (blk + 1), :]
                chain(pool.affine_select(out=part, in_=part, compare_op=ALU.is_ge, fill=0.0, base=SUB * (blk + 1) - 1,
                                         pattern=[[-1, P]], channel_multiplier=0))
            chain(pool.iota(IOI[:, 0:NE], [[1, NE]], base=0, channel_multiplier=0))
            chain(pool.iota(IOI[:, NE:2 * NE], [[1, GROUPS], [0, PER_GROUP]], base=0, channel_multiplier=0))
            chain(pool.iota(IOI[:, 2 * NE:2 * NE + P], [[1, P]], base=0, channel_multiplier=0))
            pool.iota(IOI[:, 2 * NE + P:], [[2 * P, NT], [1, 2]], base=-BIG, channel_multiplier=2).then_inc(s_const, 1)

            pool.wait_ge(s_xst, NT)
            load_state(0)
            load_state(1)

            pool.dma_start(conv_s[0, :, 0:2, :], state_conv[0, :, 1:3, :]).then_inc(s_small_out, 16)
            pool.wait_ge(s_tail, 1)
            pool.dma_start(conv_p[0, 0], TAIL[0:3, :]).then_inc(s_small_out, 16)
            pool.dma_start(conv_s[0, :, 2, :], TAIL[3:11, :]).then_inc(s_small_out, 16)
            for b in range(NS):
                pool.wait_ge(s_sst, b + 1)
                pool.dma_start(so_v[b], SST[:, b % 2, :].rearrange("p (h e) -> p h e", h=NH)).then_inc(s_sout[b % 2], 16)
                if b + 2 < NS:
                    pool.wait_ge(s_sout[b % 2], 16 * (b // 2 + 1))
                    pool.wait_ge(s_osw, b + 1)
                    load_state(b + 2)
                if b % 2 == 1:
                    h = b // 2
                    pool.wait_ge(s_s, CH * (h + 1))
                    pool.dma_start(hgrn_p[0, 0, h], S[:, h % 2, CH - 1, :]).then_inc(s_hp, 16)
            pool.wait_ge(s_tail, 2)
            pool.dma_start(rglru_p[0], HTAIL[0:1, :]).then_inc(s_ys[0], 16)
            pool.dma_start(rglru_s[0], HTAIL[1:9, :]).then_inc(s_ys[1], 16)

            pool.wait_ge(s_hp, 16 * NH)
            pool.wait_ge(s_y, NH + 1)
            pool.memset(XG[0], 0.0).then_inc(s_zero, 1)
            pool.memset(XG[1], 0.0).then_inc(s_zero, 1)
            pool.wait_ge(s_zero, 2)
            pool.wait_ge(s_xn[0], 16 * 3)
            pool.wait_ge(s_xn[1], 16 * 2)
            pool.wait_ge(s_rnd, 1)
            rounds = pool.value_load(NRND[0:1, 0:1], min_val=1, max_val=5)

            def gather(n, e, p):
                pool.wait_ge(s_tw, n - 1)
                pool.sem_inc(s_turn, 1)
                pool.tensor_copy(GIDX[:, p, :], SRCI[:, e]).then_inc(s_gi, 1)
                pool.wait_ge(s_gi, n + 1)
                pool.sem_inc(s_turn, 1)
                pool.indirect_dma_start(out=XG[p], out_offset=None, in_=xn_dram,
                                        in_offset=bass.IndirectOffsetOnAxis(ap=GIDX[:, p, :].bitcast(U32), axis=0),
                                        bounds_check=TOK - 1, oob_is_err=False).then_inc(s_xg[p], 16)

            def scatter(n, e, p, use):
                pool.wait_ge(s_ys[p], 16 * use + 16)
                pool.sem_inc(s_turn, 1)
                pool.tensor_copy(SIDX[:, p, :], DSTI[:, e]).then_inc(s_si, 1)
                pool.wait_ge(s_si, n + 1)
                pool.wait_ge(s_ya, n + 2)
                pool.wait_ge(s_yd, n + 2)
                pool.sem_inc(s_turn, 1)
                pool.indirect_dma_start(out=ye_dram, out_offset=bass.IndirectOffsetOnAxis(ap=SIDX[:, p, :].bitcast(U32), axis=0),
                                        in_=YO[p], in_offset=None,
                                        bounds_check=2 * TOK - 1, oob_is_err=False).then_inc(s_ys[p], 16)

            pool.sem_inc(s_rdone, 1)
            with pool.Fori(0, rounds) as r:
                base = r * NE
                pool.wait_ge(s_tabr, r + 1)
                pool.sem_inc(s_turn, 1)
                for e in range(2):
                    pool.tensor_copy(GIDX[:, e, :], SRCI[:, e:e + 1]).then_inc(s_gi, 1)
                    pool.wait_ge(s_gi, base + e + 1)
                    pool.sem_inc(s_turn, 1)
                    pool.indirect_dma_start(out=XG[e], out_offset=None, in_=xn_dram,
                                            in_offset=bass.IndirectOffsetOnAxis(ap=GIDX[:, e, :].bitcast(U32), axis=0),
                                            bounds_check=TOK - 1, oob_is_err=False).then_inc(s_xg[e], 16)
                with pool.Fori(0, NE // 2 - 1) as i:
                    for p in range(2):
                        e = i * 2 + p
                        gather(base + e + 2, bass.ds(e + 2, 1), p)
                        scatter(base + e, bass.ds(e, 1), p, r * (NE // 2) + i)
                for p in range(2):
                    e = NE - 2 + p
                    scatter(base + e, slice(e, e + 1), p, r * (NE // 2) + NE // 2 - 1)
                pool.wait_ge(s_ys[0], (r + 1) * (NE // 2 * 16) + 16)
                pool.wait_ge(s_ys[1], (r + 1) * (NE // 2 * 16) + 16)
                pool.sem_inc(s_rdone, 1)
            pool.wait_ge(s_small_out, 16 * 3)
            pool.wait_ge(s_sout[0], 16 * 4)
            pool.wait_ge(s_sout[1], 16 * 4)

        @block.scalar
        def _(act):
            rows = [(lower_bounds, LB, 8), (hgrn_norm_g, HGG, 4), (conv_w[0], CW, 16), (conv_b, CB, 4), (lru_bx, BX, 4),
                    (lru_ba, BA, 4), (lru_lambda, LAM, 4), (state_rglru[0], H0, NS * NH)]
            act.dma_start(G1[:], ln1_g[0].rearrange("(p k) -> p k", k=KD)).then_inc(s_gain, 16)
            for src, at, n in rows:
                act.dma_start(PROW[at:at + n, :], src.rearrange("a (m p) -> (a m) p", p=P)).then_inc(s_par, 16)
            act.dma_start(CROW[:], state_conv[0].rearrange("b w (m p) -> (b w m) p", p=P)).then_inc(s_par, 16)
            act.dma_start(G2[:], ln2_g[0].rearrange("(p k) -> p k", k=KD)).then_inc(s_gain, 16)
            act.dma_start(WGt[:], router_wg[0].rearrange("(p k) g -> p (k g)", k=KD)).then_inc(s_rt, 16)
            act.dma_start(WEt[:], router_we[0].rearrange("g (p k) e -> p g (k e)", k=KD)).then_inc(s_rt, 16)
            act.dma_start(RB[:, 0:GROUPS], router_bg[0:1, :].to_broadcast([P, GROUPS])).then_inc(s_rt, 16)
            act.dma_start(RB[:, GROUPS:], router_be.rearrange("a g e -> a (g e)").to_broadcast([P, NE])).then_inc(s_rt, 16)

            act.wait_ge(s_init, 3)
            for i in range(NT):
                act.wait_ge(s_x[i], 16)
                if i >= 2:
                    act.wait_ge(s_ssq, i - 1)
                act.activation(XS[0:ROWS[i], i % 2, :], X[0:ROWS[i], i, :], ACT.Square,
                               accum_out=SSQ[0:ROWS[i], i:i + 1]).then_inc(s_ssq, 1)
            act.wait_ge(s_ssq, NT)
            act.activation(RSTD[:], SSQ[:], ACT.Ln, scale=1.0 / D, bias=EPSC[:]).then_inc(s_rstd, 1)
            act.wait_ge(s_rstd, 1)
            act.activation(RSTD[:], RSTD[:], ACT.Exp, scale=-0.5).then_inc(s_rstd, 1)
            act.wait_ge(s_rstd, 2)
            for i in range(NT):
                if i >= 2:
                    act.wait_ge(s_xst, i - 1)
                act.activation(XS[0:ROWS[i], i % 2, :], X[0:ROWS[i], i, :], ACT.Copy,
                               scale=RSTD[0:ROWS[i], i:i + 1]).then_inc(s_xs, 1)

            act.wait_ge(s_vec, 2)
            act.activation(VEC[:, V_T0:V_T0 + 8], VEC[:, V_T0:V_T0 + 8], ACT.Exp).then_inc(s_vexp, 1)

            def halves(name, m, dst, off, func, **kw):
                for h in range(2):
                    ps = await_ps(act, (name, m, h))
                    read(act.activation(dst[:, m, off + h * HALF:off + (h + 1) * HALF], ps[:, 0:HALF], func, **kw),
                         (name, m, h))

            for m in range(NH):
                halves("xr", m, XRt, 3, ACT.Copy)
            for m in range(NH):
                halves("fx", m, Kt, 0, ACT.Tanh, scale=0.5)
            act.wait_ge(s_param, 1)
            for m in range(NH):
                halves("gx", m, GXt, 0, ACT.Tanh, scale=0.5, bias=col(V_BX, m))
                halves("ga", m, GAt, 0, ACT.Tanh, scale=0.5, bias=col(V_BA, m))
                await_read(act, ("ga", m, 1))
                act.activation(TN[:, m, :], GAt[:, m, :], ACT.Tanh, scale=col(V_NC, m), bias=col(V_NC, m)).then_inc(s_gt, 1)
                act.activation(GAt[:, m, :], GAt[:, m, :], ACT.Exp, scale=col(V_C, m), bias=col(V_C, m)).then_inc(s_a, 1)
                act.wait_ge(s_a, m + 1)
                act.activation(A2[:, m, :], GAt[:, m, :], ACT.Square).then_inc(s_gt, 1)
            for m in range(NH):
                act.wait_ge(s_m2, 2 * (m + 1))
                act.activation(TN[:, m, :], TN[:, m, :], ACT.Ln, scale=0.25).then_inc(s_mu, 1)
                act.wait_ge(s_mu, 2 * m + 1)
                act.activation(TN[:, m, :], TN[:, m, :], ACT.Exp, scale=0.5).then_inc(s_mu, 1)
            act.wait_ge(s_f, NH)
            for h in range(NH):
                act.activation(Ft[:, h, 0:SEQ], Ft[:, h, 0:SEQ], ACT.Ln).then_inc(s_lf, 1)

            def decays(h):
                t = T[:, h % 2]
                act.wait_ge(s_d, 4 * (h + 1))
                for j, half in ((0, 64), (1, 32)):
                    v = t[:, j, :].rearrange("p (n two l) -> p n two l", two=2, l=half)
                    act.activation(v[:, :, 1, :], v[:, :, 1, :], ACT.Exp).then_inc(s_e, 1)
                    act.activation(v[:, :, 0, :], v[:, :, 0, :], ACT.Exp, scale=-1.0).then_inc(s_e, 1)
                act.activation(t[:, 4, :], t[:, 2, :], ACT.Exp).then_inc(s_e, 1)
                act.activation(t[:, 2, :], t[:, 2, :], ACT.Exp, scale=-1.0).then_inc(s_e, 1)
                act.activation(t[:, 5, :], Ft[:, h, 0:SEQ], ACT.Exp).then_inc(s_e, 1)
                act.activation(t[:, 3, :], t[:, 3, :], ACT.Exp).then_inc(s_e, 1)
                act.activation(AC[:, h, :], Ft[:, h, 0:SEQ].rearrange("p (c t) -> p c t", c=CH)[:, :, P - 1], ACT.Exp).then_inc(s_ac, 1)

            def square_o(h):
                act.wait_ge(s_o, h + 1)
                if h >= 1:
                    act.wait_ge(s_rs, 2 * h)
                    act.wait_ge(s_yn, h)
                act.activation(NB, PS[B_O][:, :], ACT.Square).then_inc(s_osq, 1)

            def head_rstd(h):
                ps = await_ps(act, ("mean", h))
                read(act.activation(NB, ps[:, :], ACT.Ln, bias=EPSC[:]), ("mean", h))
                await_read(act, ("mean", h))
                act.activation(NB, NB, ACT.Exp, scale=-0.5).then_inc(s_rs, 2)

            decays(0)
            for s in range(8):
                name, m = ("gr" if s < 4 else "g"), s % 4
                halves(name, m, GY[:, NH:, :] if s < 4 else GY[:, 0:NH, :], 0, ACT.Copy)
                if s < 4:
                    await_read(act, (name, m, 1))
                    act.wait_ge(s_tail, 1)
                    act.activation(XRt[:, m, 0:TOK], GY[:, NH + m, :], ACT.Square).then_inc(s_gela, 1)
                if s % 2 == 0:
                    h = s // 2
                    act.wait_ge(s_kt_ps, h + 1)
                    if h >= 1:
                        act.wait_ge(s_kv, h)
                    act.activation(KT, PS[B_KV][:, :].rearrange("p (c t) -> p c t", c=CH), ACT.Copy).then_inc(s_kt, 1)
                    if h >= 1:
                        square_o(h - 1)
                    if h + 1 < NH:
                        decays(h + 1)
                elif s >= 3:
                    head_rstd((s - 3) // 2)
                if s == 5:
                    for m2 in range(NH):
                        act.wait_ge(s_gel, 2 * (m2 + 1))
                        act.activation(XRt[:, m2, 0:TOK], XRt[:, m2, 0:TOK], ACT.Tanh, scale=sqrt(2 / pi)).then_inc(s_gela, 1)
            for m in range(NH):
                await_read(act, ("g", m, 1))
                act.wait_ge(s_yb, m + 1)
                act.activation(XRt[:, m, 0:TOK], GY[:, m, :], ACT.Tanh, scale=0.5).then_inc(s_tg, 1)
            square_o(NH - 1)
            head_rstd(NH - 1)
            act.wait_ge(s_oss, 1)
            act.activation(OSB[:], OS[:], ACT.Square).then_inc(s_oss, 1)
            ps = await_ps(act, ("mean", 4))
            act.wait_ge(s_oss, 2)
            read(act.activation(OSB[:], ps[:, 0:NH * NS], ACT.Ln, bias=EPSC[:]), ("mean", 4))
            await_read(act, ("mean", 4))
            act.activation(OSB[:], OSB[:], ACT.Exp, scale=-0.5).then_inc(s_oss, 1)

            for c in range(NT):
                n = ROWS[c]
                await_read(act, ("op", c, 1))
                if c == 0:
                    act.wait_ge(s_sout[0], 16 * 4)
                    act.wait_ge(s_sout[1], 16 * 4)
                if c >= 2:
                    act.wait_ge(s_xst, NT + c - 1)
                    act.wait_ge(s_xn[c % 2], 16 * (c // 2))
                act.activation(XS[0:n, c % 2, :], X[0:n, c, :], ACT.Square, accum_out=SSQ[0:n, c:c + 1]).then_inc(s_ssq, 1)
                act.wait_ge(s_ssq, NT + c + 1)
                act.activation(RSTD[0:n, c:c + 1], SSQ[0:n, c:c + 1], ACT.Ln, scale=1.0 / D, bias=EPSC[0:n, :]).then_inc(s_rstd, 1)
                act.wait_ge(s_rstd, 3 + 2 * c)
                act.activation(RSTD[0:n, c:c + 1], RSTD[0:n, c:c + 1], ACT.Exp, scale=-0.5).then_inc(s_rstd, 1)
                act.wait_ge(s_rstd, 4 + 2 * c)
                act.activation(XS[0:n, c % 2, :], X[0:n, c, :], ACT.Copy, scale=RSTD[0:n, c:c + 1]).then_inc(s_xs, 1)

            act.wait_ge(s_rexp, 1)
            act.activation(GEX[:], GEX[:], ACT.Exp).then_inc(s_rexp, 1)
            act.wait_ge(s_rexp, 3)
            act.activation(WK[:, 1, :], WK[:, 1, :], ACT.Exp).then_inc(s_rexp, 1)

            act.wait_ge(s_rnd, 1)
            rounds = act.value_load(NRND[0:1, 0:1], min_val=1, max_val=5)

            def silu(n, p):
                act.wait_ge(s_hw, n + 1)
                act.activation(HS[p], PS[2 + p][:, 0:FE], ACT.Silu).then_inc(s_silu, 1)

            def ht_copy(n, p):
                act.wait_ge(s_htw, n + 1)
                act.activation(HT[p], PS[4][:, 0:2 * P].rearrange("p (j t) -> p j t", j=2), ACT.Copy).then_inc(s_ht, 1)

            def y_copy(n, p, scattered):
                act.wait_ge(s_yw, n + 1)
                act.wait_ge(s_ys[p], 16 * scattered + 16)
                act.activation(YO[p][:, 0:512], PS[5][:, :], ACT.Copy).then_inc(s_ya, 1)

            act.sem_inc(s_ht, 1)
            act.sem_inc(s_ya, 1)
            with act.Fori(0, rounds) as r:
                base = r * NE
                silu(base, 0)
                ht_copy(base, 0)
                with act.Fori(0, NE // 2 - 1) as i:
                    for j in range(2):
                        e = base + i * 2 + 1 + j
                        p = 1 - j
                        silu(e, p)
                        y_copy(e - 1, 1 - p, r * (NE // 2) + i)
                        ht_copy(e, p)
                e = base + NE - 1
                silu(e, 1)
                y_copy(e - 1, 0, r * (NE // 2) + NE // 2 - 1)
                ht_copy(e, 1)
                y_copy(e, 1, r * (NE // 2) + NE // 2 - 1)

            for c in range(NT):
                n = ROWS[c]
                act.wait_ge(s_cmb, 2 * (c + 1))
                if c >= 2:
                    act.wait_ge(s_out[c % 2], 16 * (c // 2))
                act.activation(OUT[c % 2][0:n], X[0:n, c, :], ACT.Square, accum_out=SSQ[0:n, c:c + 1]).then_inc(s_fr, 1)
                act.wait_ge(s_fr, 3 * c + 1)
                act.activation(RSTD[0:n, c:c + 1], SSQ[0:n, c:c + 1], ACT.Ln, scale=1.0 / D, bias=EPSC[0:n, :]).then_inc(s_fr, 1)
                act.wait_ge(s_fr, 3 * c + 2)
                act.activation(RSTD[0:n, c:c + 1], RSTD[0:n, c:c + 1], ACT.Exp, scale=-0.5).then_inc(s_fr, 1)

        @block.vector
        def _(dve):
            vec = [0]

            def vstep(ins):
                vec[0] += 1
                ins.then_inc(s_vec, 1)
                dve.wait_ge(s_vec, vec[0])

            dve.memset(EPSC[:], EPS).then_inc(s_init, 1)
            dve.memset(SSQ[:], 1.0).then_inc(s_init, 1)
            dve.memset(RSTD[:], 1.0).then_inc(s_init, 1)
            dve.memset(XRt[:, :, 0:3], 0.0).then_inc(s_init, 1)
            dve.memset(RESET[:], 1.0).then_inc(s_init, 1)
            dve.wait_ge(s_init, 5)
            dve.memset(RESET[:, :, 0:1], 0.0).then_inc(s_init, 1)

            def evac_xt(name, i, gain):
                n = ROWS[i]
                for j in range(2):
                    ps = await_ps(dve, (name, i, j))
                    src = ps[:, :].rearrange("p (k t) -> p k t", k=4)[:, :, 0:n]
                    read(dve.tensor_tensor(XNT[:, 4 * j:4 * j + 4, i * P:i * P + n], src, bc(gain[:, 4 * j:4 * j + 4], 2, n), ALU.mult),
                         (name, i, j))

            dve.wait_ge(s_gain, 32)
            for i in range(NT):
                evac_xt("xt", i, G1)
            ps = await_ps(dve, ("par", 0))
            read(dve.tensor_copy(PARAM[:], ps[:, 0:NPAR]), ("par", 0))
            ps = await_ps(dve, ("par", 1))
            read(dve.tensor_copy(CVT[:], ps[:, 0:NS * 3 * NH]), ("par", 1))
            await_read(dve, ("par", 0))
            await_read(dve, ("par", 1))
            dve.wait_ge(s_const, 2)
            dve.tensor_copy(IOF[:], IOI[:, :]).then_inc(s_init, 1)

            def v4(at):
                return VEC[:, at:at + 4]

            def p4(at):
                return PARAM[:, at:at + 4]

            vstep(dve.tensor_tensor(v4(V_T0), p4(LB + 4), p4(LB), ALU.subtract))
            vstep(dve.scalar_tensor_tensor(out=v4(V_T1), in0=p4(LAM), scalar=-1.0, in1=p4(LAM), op0=ALU.mult, op1=ALU.min))
            dve.wait_ge(s_vexp, 1)
            vstep(dve.tensor_scalar(v4(V_T0), v4(V_T0), 1.0, None, ALU.add))
            vstep(dve.reciprocal(v4(V_T0), v4(V_T0)))
            vstep(dve.tensor_scalar(v4(V_FB), v4(V_T0), -0.5, 0.5, ALU.mult, ALU.add))
            vstep(dve.tensor_scalar(v4(V_NFB), v4(V_FB), -1.0, None, ALU.mult))
            vstep(dve.tensor_tensor(v4(V_FA), v4(V_T0), v4(V_FB), ALU.add))
            vstep(dve.tensor_scalar(v4(V_T2), v4(V_T1), 2.0, None, ALU.add))
            vstep(dve.reciprocal(v4(V_T2), v4(V_T2)))
            vstep(dve.tensor_tensor(v4(V_T1), v4(V_T1), v4(V_T2), ALU.mult))
            vstep(dve.tensor_tensor(v4(V_T2), v4(V_T1), v4(V_T1), ALU.mult))
            vstep(dve.tensor_scalar(v4(V_T3), v4(V_T2), 1.0 / 17, None, ALU.mult))
            for odd in (15, 13, 11, 9, 7, 5, 3):
                vstep(dve.scalar_tensor_tensor(out=v4(V_T3), in0=v4(V_T3), scalar=1.0 / odd, in1=v4(V_T2), op0=ALU.add, op1=ALU.mult))
            vstep(dve.scalar_tensor_tensor(out=v4(V_T3), in0=v4(V_T3), scalar=1.0, in1=v4(V_T1), op0=ALU.add, op1=ALU.mult))
            vstep(dve.tensor_scalar(v4(V_T1), p4(LAM), -1.0, 0.0, ALU.mult, ALU.max))
            vstep(dve.scalar_tensor_tensor(out=v4(V_T3), in0=v4(V_T3), scalar=2.0, in1=v4(V_T1), op0=ALU.mult, op1=ALU.add))
            vstep(dve.tensor_scalar(v4(V_C), v4(V_T3), -4.0, None, ALU.mult))
            vstep(dve.tensor_scalar(v4(V_NC), v4(V_T3), 4.0, None, ALU.mult))
            vstep(dve.tensor_scalar(v4(V_BX), p4(BX), 0.5, None, ALU.mult))
            vstep(dve.tensor_scalar(v4(V_BA), p4(BA), 0.5, None, ALU.mult))
            dve.tensor_scalar(v4(V_HG), p4(HGG), 0.5, None, ALU.mult).then_inc(s_param, 1)

            conv = [0]

            def cstep(ins):
                conv[0] += 1
                ins.then_inc(s_conv, 1)
                dve.wait_ge(s_conv, conv[0])

            dve.wait_ge(s_param, 1)
            for m in range(NH):
                await_read(dve, ("xr", m, 1))
                cstep(dve.tensor_scalar(XCt[:, m, 0:SEQ], XRt[:, m, 0:SEQ], PARAM[:, CW + m:CW + m + 1],
                                        PARAM[:, CB + m:CB + m + 1], ALU.mult, ALU.add))
                for w in range(1, 4):
                    cstep(dve.scalar_tensor_tensor(out=XCt[:, m, 0:SEQ], in0=XRt[:, m, w:w + SEQ],
                                                   scalar=PARAM[:, CW + 4 * w + m:CW + 4 * w + m + 1],
                                                   in1=XCt[:, m, 0:SEQ], op0=ALU.mult, op1=ALU.add))
            xs_c = XCt[:, :, SEQ:TOK]
            hist = CVT[:, :].rearrange("p (b w m) -> p w m b", b=NS, w=3)
            cstep(dve.tensor_tensor(xs_c, XRt[:, :, SEQ + 3:TOK + 3], bc(p4(CW + 12), 2, NS), ALU.mult))
            cstep(dve.tensor_tensor(xs_c, xs_c, bc(p4(CB), 2, NS), ALU.add))
            for w in range(3):
                cstep(dve.tensor_tensor(SCR[:, 0:NH, :], hist[:, w], bc(p4(CW + 4 * w), 2, NS), ALU.mult))
                cstep(dve.tensor_tensor(xs_c, xs_c, SCR[:, 0:NH, :], ALU.add))
            n_conv = conv[0]

            for h in range(NH):
                await_read(dve, ("fx", h, 1))
                dve.tensor_scalar(Ft[:, h, :], Kt[:, h, :], col(V_FB, h), col(V_FA, h), ALU.mult, ALU.add).then_inc(s_f, 1)
                dve.tensor_scalar(Kt[:, h, :], Kt[:, h, :], col(V_NFB, h), col(V_FB, h), ALU.mult, ALU.add).then_inc(s_k, 1)

            def mult_squared(m):
                dve.wait_ge(s_gt, 2 * (m + 1))
                dve.scalar_tensor_tensor(out=TN[:, m, :], in0=A2[:, m, :], scalar=1.0, in1=TN[:, m, :],
                                         op0=ALU.add, op1=ALU.mult).then_inc(s_m2, 1)
                dve.wait_ge(s_m2, 2 * m + 1)
                dve.tensor_scalar(TN[:, m, :], TN[:, m, :], 1e-18, None, ALU.max).then_inc(s_m2, 1)

            for m in range(NH):
                for hf in range(2):
                    ps = await_ps(dve, ("q", m, hf))
                    read(dve.tensor_copy(Qt[:, m, hf * HALF:(hf + 1) * HALF], ps[:, 0:HALF]), ("q", m, hf))
                if m >= 1:
                    mult_squared(m - 1)
            mult_squared(NH - 1)
            for c in range(NT):
                ps = await_ps(dve, ("v", c))
                dst = Vt[:, c, :] if c < CH else Vs[:]
                read(dve.tensor_copy(dst, ps[0:ROWS[c], :]), ("v", c))
            ps = await_ps(dve, ("xtail",))
            read(dve.tensor_copy(TAIL[:], ps[0:11, :]), ("xtail",))
            await_read(dve, ("xtail",))
            dve.sem_inc(s_tail, 1)

            ustep_n = [0]

            def ustep(ins):
                ustep_n[0] += 1
                ins.then_inc(s_u, 1)
                dve.wait_ge(s_u, ustep_n[0])

            dve.wait_ge(s_mu, 2 * NH)
            ustep(dve.memset(TN[:, :, 0:1], 0.5))
            for m in range(NH):
                ustep(dve.scalar_tensor_tensor(out=GXt[:, m, :], in0=GXt[:, m, :], scalar=1.0, in1=XCt[:, m, :],
                                               op0=ALU.add, op1=ALU.mult))
                ustep(dve.tensor_tensor(GXt[:, m, :], GXt[:, m, :], TN[:, m, :], ALU.mult))
                dve.tensor_tensor_scan(XCt[:, m, 0:SEQ], GAt[:, m, 0:SEQ], GXt[:, m, 0:SEQ], 0.0, ALU.mult, ALU.add).then_inc(s_h, 1)
            h0 = PARAM[:, H0:NPAR].rearrange("p (b m) -> p m b", b=NS)
            ustep(dve.tensor_tensor(SCR[:, 0:NH, :], GAt[:, :, SEQ:TOK], h0, ALU.mult))
            dve.tensor_tensor(XCt[:, :, SEQ:TOK], SCR[:, 0:NH, :], GXt[:, :, SEQ:TOK], ALU.add).then_inc(s_h, 1)

            def exponents(h):
                t = T[:, h % 2]
                if h >= 2:
                    dve.wait_ge(s_o, h - 1)
                dve.wait_ge(s_lf, h + 1)
                b = Ft[:, h, 0:SEQ]
                dve.tensor_tensor_scan(b, RESET[:, :, :].rearrange("p c t -> p (c t)"), b, 0.0, ALU.mult, ALU.add).then_inc(s_b, 1)
                dve.wait_ge(s_b, h + 1)
                for j, size, at in ((0, P, 63), (1, 64, 31), (2, SUB, SUB // 2 - 1)):
                    bv = b.rearrange("p (n l) -> p n l", l=size)
                    tv = t[:, j, :].rearrange("p (n l) -> p n l", l=size)
                    dve.tensor_tensor(tv, bv, bc(bv[:, :, at], 2, size), ALU.subtract).then_inc(s_d, 1)
                bv = b.rearrange("p (n l) -> p n l", l=P)
                dve.tensor_tensor(t[:, 3, :].rearrange("p (n l) -> p n l", l=P), bc(bv[:, :, P - 1], 2, P), bv,
                                  ALU.subtract).then_inc(s_d, 1)

            def decayed_qk(h):
                t = T[:, h % 2]
                dve.wait_ge(s_e, 8 * (h + 1))
                q, k = Qt[:, h, 0:SEQ], Kt[:, h, 0:SEQ]
                for j, half in ((0, 64), (1, 32)):
                    tv = t[:, j, :].rearrange("p (n two l) -> p n two l", two=2, l=half)
                    for two, x in ((1, q), (0, k)):
                        xv = x.rearrange("p (n two l) -> p n two l", two=2, l=half)
                        dve.tensor_tensor(tv[:, :, two, :], tv[:, :, two, :], xv[:, :, two, :], ALU.mult).then_inc(s_qk, 1)
                for j, x in ((4, q), (2, k), (5, q), (3, k)):
                    dve.tensor_tensor(t[:, j, :], t[:, j, :], x, ALU.mult).then_inc(s_qk, 1)

            def scores(h):
                dve.wait_ge(s_scores, h + 1)
                if h >= 2:
                    dve.wait_ge(s_o, h - 1)
                sc = SC[:, h % 2]
                sd = PS[B_SD][:, :].rearrange("p (c t) -> p c t", c=CH)
                sl = PS[B_SL][:, :].rearrange("p (c t) -> p c t", c=CH)
                dve.copy_predicated(sc, bc(CMASK[:].bitcast(I32), 1, CH), sd).then_inc(s_sc, 1)
                dve.wait_ge(s_sc, 4 * h + 1)
                for s0, n in ((0, 64), (0, 32), (64, 32)):
                    dve.tensor_copy(sc[s0:s0 + n, :, s0 + n:s0 + 2 * n], sl[s0:s0 + n, :, s0 + n:s0 + 2 * n]).then_inc(s_sc, 1)

            def states(h):
                dve.wait_ge(s_kv, h + 1)
                dve.wait_ge(s_ac, h + 1)
                if h >= 2:
                    dve.wait_ge(s_hp, 16 * (h - 1))
                    dve.wait_ge(s_o, h - 1)
                kv = PS[B_KV][:, :].rearrange("p (c t) -> p c t", c=CH)
                dve.tensor_copy(S[:, h % 2, 0, :], kv[:, 0, :]).then_inc(s_s, 1)
                for c in range(1, CH):
                    dve.wait_ge(s_s, CH * h + c)
                    dve.scalar_tensor_tensor(out=S[:, h % 2, c, :], in0=S[:, h % 2, c - 1, :], scalar=AC[:, h, c:c + 1],
                                             in1=kv[:, c, :], op0=ALU.mult, op1=ALU.add).then_inc(s_s, 1)

            def normed(h):
                dve.wait_ge(s_rs, 2 * (h + 1))
                dve.scalar_tensor_tensor(out=Kt[:, h, 0:SEQ], in0=PS[B_O][:, :], scalar=col(V_HG, h), in1=NB,
                                         op0=ALU.mult, op1=ALU.mult).then_inc(s_yn, 1)

            def sample_state(b):
                ps = await_ps(dve, ("vb", b))
                kv = SKV[:, :].rearrange("p (h e) -> p h e", h=NH)
                read(dve.tensor_tensor(kv, ps[:, :].rearrange("p (h e) -> p h e", h=NH), bc(Kt[:, :, SEQ + b], 2, P), ALU.mult),
                     ("vb", b))
                dve.wait_ge(s_sin[b % 2], 16 * (b // 2 + 1))
                st = SST[:, b % 2, :].rearrange("p (h e) -> p h e", h=NH)
                dve.tensor_tensor(st, st, bc(Ft[:, :, SEQ + b], 2, P), ALU.mult).then_inc(s_skv, 1)
                dve.wait_ge(s_skv, b + 1)
                await_read(dve, ("vb", b))
                dve.tensor_tensor(st, st, kv, ALU.add).then_inc(s_sst, 1)

            gel = [0]

            def gelu_argument(m):
                dve.wait_ge(s_gela, m + 1)
                dve.tensor_scalar(XRt[:, m, 0:TOK], XRt[:, m, 0:TOK], 0.044715, 1.0, ALU.mult, ALU.add).then_inc(s_gel, 1)
                dve.wait_ge(s_gel, 2 * m + 1)
                dve.tensor_tensor(XRt[:, m, 0:TOK], XRt[:, m, 0:TOK], GY[:, NH + m, :], ALU.mult).then_inc(s_gel, 1)

            dve.wait_ge(s_h, NH + 1)
            dve.memset(SC, 0.0).then_inc(s_zero_sc, 1)
            dve.wait_ge(s_zero_sc, 1)
            exponents(0)
            decayed_qk(0)
            dve.wait_ge(s_const, 2)
            for s in range(8):
                h = s // 2
                if s % 2 == 0:
                    scores(h)
                else:
                    states(h)
                    if s >= 3:
                        normed((s - 3) // 2)
                sample_state(s)
                if s % 2 == 0 and h + 1 < NH:
                    exponents(h + 1)
                    decayed_qk(h + 1)
                if s < 4:
                    gelu_argument(s)
                if s == 6:
                    for m in range(NH):
                        dve.wait_ge(s_gela, NH + m + 1)
                        yb = GY[:, NH + m, :]
                        dve.scalar_tensor_tensor(out=yb, in0=XRt[:, m, 0:TOK], scalar=1.0, in1=yb,
                                                 op0=ALU.add, op1=ALU.mult).then_inc(s_gel, 1)
                        dve.wait_ge(s_gel, 2 * NH + m + 1)
                        dve.scalar_tensor_tensor(out=yb, in0=yb, scalar=0.5, in1=XCt[:, m, :],
                                                 op0=ALU.mult, op1=ALU.mult).then_inc(s_yb, 1)
            dve.wait_ge(s_osw, NS)
            dve.tensor_copy(OS[:], PS[B_OS][:, 0:NH * NS]).then_inc(s_oss, 1)
            for m in range(NH):
                dve.wait_ge(s_tg, m + 1)
                dve.scalar_tensor_tensor(out=GY[:, m, :], in0=XRt[:, m, 0:TOK], scalar=1.0, in1=GY[:, m, :],
                                         op0=ALU.add, op1=ALU.mult).then_inc(s_sg, 1)
            normed(NH - 1)
            dve.wait_ge(s_sg, NH)
            for h in range(NH):
                dve.wait_ge(s_yn, h + 1)
                dve.tensor_tensor(GY[:, h, 0:SEQ], GY[:, h, 0:SEQ], Kt[:, h, 0:SEQ], ALU.mult).then_inc(s_y, 1)
            dve.wait_ge(s_oss, 3)
            dve.tensor_tensor(OS[:], OS[:], OSB[:], ALU.mult).then_inc(s_oss, 1)
            dve.wait_ge(s_oss, 4)
            os_v = OS[:, :].rearrange("p (h b) -> p h b", h=NH)
            dve.tensor_tensor(os_v, os_v, bc(v4(V_HG), 2, NS), ALU.mult).then_inc(s_oss, 1)
            dve.wait_ge(s_oss, 5)
            dve.tensor_tensor(GY[:, 0:NH, SEQ:TOK], GY[:, 0:NH, SEQ:TOK], os_v, ALU.mult).then_inc(s_y, 1)
            ps = await_ps(dve, ("htail",))
            read(dve.tensor_copy(HTAIL[:], ps[0:9, :]), ("htail",))
            await_read(dve, ("htail",))
            dve.sem_inc(s_tail, 1)

            rt = [0]

            def rstep(ins):
                rt[0] += 1
                ins.then_inc(s_r, 1)
                dve.wait_ge(s_r, rt[0])

            dve.wait_ge(s_rt, 16 * 4)
            dve.tensor_copy(WR[:, :, 0:GROUPS], WGt[:, :].rearrange("p (k g) -> p k g", k=KD)).then_inc(s_r, 1)
            for g in range(GROUPS):
                dve.tensor_copy(WR[:, :, GROUPS + PER_GROUP * g:GROUPS + PER_GROUP * (g + 1)],
                                WEt[:, g, :].rearrange("p (k e) -> p k e", k=KD)).then_inc(s_r, 1)
            dve.memset(LG[:], 0.0).then_inc(s_r, 1)
            dve.memset(L8[:], -3e38).then_inc(s_r, 1)
            rt[0] += 3 + GROUPS
            dve.wait_ge(s_r, rt[0])

            for c in range(NT + 1):
                if c < NT:
                    for n in range(2):
                        ps = await_ps(dve, ("op", c, n))
                        x = X[0:ROWS[c], c, n * 512:(n + 1) * 512]
                        read(dve.tensor_tensor(x, ps[0:ROWS[c], :], x, ALU.add), ("op", c, n))
                if c > 0:
                    evac_xt("x2t", c - 1, G2)
                    ps = await_ps(dve, ("lg", c - 1))
                    n = ROWS[c - 1]
                    read(dve.tensor_tensor(LG[0:n, c - 1, :], ps[0:n, 0:GROUPS + NE], RB[0:n, :], ALU.add), ("lg", c - 1))
            await_read(dve, ("lg", NT - 1))

            rstep(dve.tensor_copy(L8[:, :, 0:GROUPS], LG[:, :, 0:GROUPS]))
            for i in range(NT):
                rstep(dve.max(TOP[:, i, :], L8[:, i, :]))
                rstep(dve.max_index(TIX[:, i, :], TOP[:, i, :], L8[:, i, :]))
            rstep(dve.tensor_copy(GIX[:], TIX[:, :, 0]))
            dve.tensor_tensor(GEX[:], LG[:, :, 0:GROUPS], bc(TOP[:, :, 0], 2, GROUPS), ALU.subtract).then_inc(s_rexp, 1)
            rstep(dve.tensor_tensor(LMSK[:], bc(iota_g, 1, NT), bc(GIX[:], 2, NE), ALU.is_equal))
            rstep(dve.tensor_tensor(LSEL[:], LG[:, :, GROUPS:], LMSK[:], ALU.mult))
            rstep(dve.tensor_scalar(LMSK[:], LMSK[:], 3e38, -3e38, ALU.mult, ALU.add))
            rstep(dve.tensor_tensor(LSEL[:], LSEL[:], LMSK[:], ALU.add))
            for i in range(NT):
                rstep(dve.max(TOP[:, i, :], LSEL[:, i, :]))
                rstep(dve.max_index(TIX[:, i, :], TOP[:, i, :], LSEL[:, i, :]))
            rstep(dve.tensor_copy(EIX[:], TIX[:, :, 0:2]))
            dve.wait_ge(s_rexp, 2)
            dve.tensor_tensor(WK[:, 1, :], TOP[:, :, 1], TOP[:, :, 0], ALU.subtract).then_inc(s_rexp, 1)
            for k in range(2):
                rstep(dve.tensor_tensor(OH[:, k], bc(iota_e, 1, NT), bc(EIX[:, :, k], 2, NE), ALU.is_equal))
                rstep(dve.tensor_tensor(OHV[:, k], OH[:, k], bc(token_code[:, k], 2, NE), ALU.mult))
            dve.tensor_tensor(LMSK[:], OH[:, 0], OH[:, 1], ALU.add).then_inc(s_oh, 1)
            rstep(dve.reduce_sum(PTOP[:], GEX[:], AX_X))
            rstep(dve.reciprocal(PTOP[:], PTOP[:]))
            dve.wait_ge(s_rexp, 4)
            rstep(dve.tensor_scalar(WK[:, 0, :], WK[:, 1, :], 1.0, None, ALU.add))
            rstep(dve.reciprocal(WK[:, 0, :], WK[:, 0, :]))
            rstep(dve.tensor_tensor(WK[:, 0, :], WK[:, 0, :], PTOP[:], ALU.mult))
            rstep(dve.tensor_tensor(WK[:, 1, :], WK[:, 1, :], WK[:, 0, :], ALU.mult))
            ps = await_ps(dve, ("pos",))
            pos = ps[:, 0:NT * NE].rearrange("p (i e) -> p i e", i=NT)
            for k in range(2):
                rstep(dve.tensor_tensor(LSEL[:], pos, OH[:, k], ALU.mult))
                rstep(dve.reduce_sum(RANK[:, k, :], LSEL[:], AX_X))
            rstep(dve.reduce_max(CNT[:, 0:1], ps[:, NT * NE:(NT + 1) * NE], AX_X))
            rstep(dve.tensor_scalar(NRND[:], CNT[:, 0:1], P - 1.0, None, ALU.add))
            dve.tensor_scalar(NRND[:], NRND[:], 7, None, ALU.arith_shift_right).then_inc(s_rnd, 1)
            dve.wait_ge(s_rnd, 1)
            rounds = dve.value_load(NRND[0:1, 0:1], min_val=1, max_val=5)

            def xgt(n, p):
                dve.wait_ge(s_tw, n + 1)
                for j in range(2):
                    dve.tensor_tensor(XGT[p][:, 4 * j:4 * j + 4, :], PS[j][:, :].rearrange("p (k t) -> p k t", k=4),
                                      bc(G2[:, 4 * j:4 * j + 4], 2, P), ALU.mult).then_inc(s_xgt, 1)

            def gated(n, p):
                dve.wait_ge(s_silu, n + 1)
                dve.tensor_tensor(HG[p], PS[2 + p][:, FE:2 * FE], HS[p], ALU.mult).then_inc(s_hg, 1)

            def y_copy(n, p, scattered):
                dve.wait_ge(s_yw, n + 1)
                dve.wait_ge(s_ys[p], 16 * scattered + 16)
                dve.tensor_copy(YO[p][:, 512:1024], PS[6][:, :]).then_inc(s_yd, 1)

            dve.wait_ge(s_hp, 16 * NH)
            dve.sem_inc(s_xgt, 1)
            dve.sem_inc(s_yd, 1)
            with dve.Fori(0, rounds) as r:
                base = r * NE
                dve.wait_ge(s_rdone, r + 1)
                for j in range(2 * NT):
                    i, k = j // 2, j % 2
                    dve.wait_ge(s_pmu, r * (2 * NT) + max(j - 1, 0) + 1)
                    dve.tensor_scalar(PM[:, j % 2, :], iota_s, RANK[:, k, i:i + 1], None, ALU.is_equal).then_inc(s_pm, 1)
                dve.wait_ge(s_tab, r + 1)
                dve.tensor_scalar(DSTI[:, 0:NE], PS[B_O][:, 0:NE], float(BIG), None, ALU.add).then_inc(s_tabs, 1)
                dve.tensor_scalar(RANK[:], RANK[:], float(-P), None, ALU.add).then_inc(s_tabs, 1)
                dve.wait_ge(s_tabs, 2 * r + 2)
                dve.tensor_scalar(SRCI[:, 0:NE], DSTI[:, 0:NE], 1, None, ALU.arith_shift_right).then_inc(s_tabr, 1)
                xgt(base, 0)
                xgt(base + 1, 1)
                gated(base, 0)
                with dve.Fori(0, NE // 2 - 1) as i:
                    for j in range(2):
                        e = base + i * 2 + 1 + j
                        p = 1 - j
                        xgt(e + 1, 1 - p)
                        gated(e, p)
                        y_copy(e - 1, 1 - p, r * (NE // 2) + i)
                e = base + NE - 1
                gated(e, 1)
                y_copy(e - 1, 0, r * (NE // 2) + NE // 2 - 1)
                y_copy(e, 1, r * (NE // 2) + NE // 2 - 1)

            dve.wait_ge(s_fg, 16)
            for c in range(NT + 1):
                if c < NT:
                    n = ROWS[c]
                    dve.wait_ge(s_ye[c % 2], 16 * (c // 2 + 1))
                    for k in range(2):
                        x = X[0:n, c, :].rearrange("p (a d) -> p a d", a=2)
                        dve.scalar_tensor_tensor(out=x, in0=YE[c % 2][0:n, 2 * k:2 * k + 2, :], scalar=WK[0:n, k, c:c + 1],
                                                 in1=x, op0=ALU.mult, op1=ALU.add).then_inc(s_cmb, 1)
                        dve.wait_ge(s_cmb, 2 * c + k + 1)
                if c > 0:
                    n = ROWS[c - 1]
                    dve.wait_ge(s_fr, 3 * c)
                    dve.scalar_tensor_tensor(out=OUT[(c - 1) % 2][0:n], in0=X[0:n, c - 1, :], scalar=RSTD[0:n, c - 1:c],
                                             in1=FGB[0:n], op0=ALU.mult, op1=ALU.mult).then_inc(s_fin, 1)

        @block.tensor
        def _(pe):
            pe.wait_ge(s_const, 1)

            def transpose_rows(name, c):
                n = ROWS[c]
                xv = XS[0:n, c % 2, :].rearrange("t (p k) -> t k p", k=KD)
                for j in range(2):
                    ps = claim(pe, (name, c, j))
                    for k in range(4):
                        ins = pe.transpose(ps[:, k * P:k * P + n], xv[:, 4 * j + k, :], IDENT[0:n, 0:n])
                    written(ins, (name, c, j))

            for i in range(NT):
                pe.wait_ge(s_xs, i + 1)
                transpose_rows("xt", i)
                bank, use = ROT[("xt", i, 1)]
                pe.wait_ge(s_written[bank], use + 1)
                pe.sem_inc(s_xst, 1)
            pe.wait_ge(s_par, 16 * 9)
            ps = claim(pe, ("par", 0))
            written(pe.transpose(ps[:, 0:NPAR], PROW[:], IDENT[0:NPAR, 0:NPAR]), ("par", 0))
            ps = claim(pe, ("par", 1))
            written(pe.transpose(ps[:, 0:NS * 3 * NH], CROW[:], IDENT[0:NS * 3 * NH, 0:NS * 3 * NH]), ("par", 1))
            await_read(pe, ("xt", NT - 1, 1))

            def project(name, j, m):
                for hf in range(2):
                    ps = claim(pe, (name, m, hf))
                    for k in range(KD):
                        ins = pe.matmul(ps[:, 0:HALF], WC[:, j % 2, k, m * P:(m + 1) * P],
                                        XNT[:, k, hf * HALF:(hf + 1) * HALF], start=(k == 0), stop=(k == KD - 1))
                    written(ins, (name, m, hf))

            def chunk(j):
                pe.wait_ge(s_wc[j % 2], 16 * (j // 2 + 1))

            def chunk_done(name):
                b, u = ROT[name]
                pe.wait_ge(s_written[b], u + 1)
                pe.sem_inc(s_wc_free, 1)

            for j, name in ((0, "xr"), (1, "fx")):
                chunk(j)
                for m in range(NH):
                    project(name, j, m)
                chunk_done((name, NH - 1, 1))
            chunk(2)
            pe.wait_ge(s_bd, 16 * 4)
            for m in range(NH):
                project("q", 2, m)
                if m == 0:
                    pe.wait_ge(s_conv, 16 + 8)
                for name, w in (("gx", BDX), ("ga", BDA)):
                    for hf in range(2):
                        ps = claim(pe, (name, m, hf))
                        written(pe.matmul(ps[:, 0:HALF], w[:, m, :], XCt[:, m, hf * HALF:(hf + 1) * HALF],
                                          start=True, stop=True), (name, m, hf))
            chunk_done(("q", NH - 1, 1))
            chunk(3)
            for c in range(NT):
                ps = claim(pe, ("v", c))
                for k in range(KD):
                    ins = pe.matmul(ps[0:ROWS[c], :], XNT[:, k, c * P:c * P + ROWS[c]], WC[:, 1, k, :],
                                    start=(k == 0), stop=(k == KD - 1))
                written(ins, ("v", c))
            chunk_done(("v", NT - 1))
            ps = claim(pe, ("xtail",))
            for m in range(NH):
                ins = pe.transpose(ps[0:11, m * P:(m + 1) * P], XRt[:, m, SEQ:TOK + 3], IDENT[:])
            written(ins, ("xtail",))

            def head_scores(h):
                t = T[:, h % 2]
                pe.wait_ge(s_qk, 8 * (h + 1))
                if h >= 1:
                    pe.wait_ge(s_sc, 4 * h)
                for c in range(CH):
                    at = c * P
                    pe.matmul(PS[B_SD][:, at:at + P], t[:, 2, at:at + P], t[:, 4, at:at + P], start=True, stop=True)
                for c in range(CH):
                    at = c * P
                    for j, s0, n in ((0, 0, 64), (1, 0, 32), (1, 64, 32)):
                        ins = pe.matmul(PS[B_SL][s0:s0 + n, at + s0 + n:at + s0 + 2 * n], t[:, j, at + s0:at + s0 + n],
                                        t[:, j, at + s0 + n:at + s0 + 2 * n], start=True, stop=True,
                                        tile_position=(0, s0), skip_group_check=True)
                ins.then_inc(s_scores, 1)
                if h >= 1:
                    pe.wait_ge(s_s, CH * h)
                for c in range(CH):
                    ins = pe.transpose(PS[B_KV][:, c * P:(c + 1) * P], t[:, 3, c * P:(c + 1) * P], IDENT[:])
                ins.then_inc(s_kt_ps, 1)

            def head_kv(h):
                pe.wait_ge(s_kt, h + 1)
                for c in range(CH):
                    ins = pe.matmul(PS[B_KV][:, c * P:(c + 1) * P], KT[:, c, :], Vt[:, c, h * P:(h + 1) * P], start=True, stop=True)
                ins.then_inc(s_kv, 1)

            def head_o(h):
                pe.wait_ge(s_sc, 4 * (h + 1))
                pe.wait_ge(s_s, CH * (h + 1))
                if h >= 1:
                    pe.wait_ge(s_yn, h)
                for c in range(CH):
                    o = PS[B_O][:, c * P:(c + 1) * P]
                    ins = pe.matmul(o, Vt[:, c, h * P:(h + 1) * P], SC[:, h % 2, c, :], start=True, stop=(c == 0))
                    if c > 0:
                        ins = pe.matmul(o, S[:, h % 2, c - 1, :], T[:, h % 2, 5, c * P:(c + 1) * P], start=False, stop=True)
                ins.then_inc(s_o, 1)

            def head_mean(h):
                ps = claim(pe, ("mean", h))
                pe.wait_ge(s_osq, h + 1)
                written(pe.matmul(ps[:, :], MEAN128[:], NB, start=True, stop=True), ("mean", h))

            def sample_o(b):
                pe.wait_ge(s_sst, b + 1)
                for h in range(NH):
                    at = h * NS + b
                    ins = pe.matmul(PS[B_OS][:, at:at + 1], SST[:, b % 2, h * P:(h + 1) * P], Qt[:, h, SEQ + b:SEQ + b + 1],
                                    start=True, stop=True)
                ins.then_inc(s_osw, 1)

            pe.wait_ge(s_const, 2)
            for s in range(8):
                h = s // 2
                if s % 4 == 0:
                    chunk(4 + s // 4)
                name = "gr" if s < 4 else "g"
                project(name, 4 + s // 4, s % 4)
                if s % 2 == 0:
                    head_scores(h)
                    if h >= 1:
                        head_o(h - 1)
                else:
                    head_kv(h)
                    if s >= 3:
                        head_mean((s - 3) // 2)
                if s >= 1:
                    sample_o(s - 1)
                ps = claim(pe, ("vb", s))
                written(pe.matmul(ps[:, :], IDENT[0:NS, s:s + 1].to_broadcast([NS, P]), Vs[:], start=True, stop=True), ("vb", s))
                if s % 4 == 3:
                    chunk_done((name, NH - 1, 1))
            head_o(NH - 1)
            sample_o(NS - 1)
            head_mean(NH - 1)
            ps = claim(pe, ("mean", 4))
            pe.wait_ge(s_oss, 2)
            written(pe.matmul(ps[:, 0:NH * NS], MEAN128[:], OSB[:], start=True, stop=True), ("mean", 4))
            ps = claim(pe, ("htail",))
            pe.wait_ge(s_h, NH + 1)
            for m in range(NH):
                ins = pe.transpose(ps[0:9, m * P:(m + 1) * P], XCt[:, m, SEQ - 1:TOK], IDENT[:])
            written(ins, ("htail",))

            chunk(6)
            chunk(7)
            pe.wait_ge(s_yb, NH)
            pe.wait_ge(s_y, NH + 1)
            for c in range(NT + 1):
                if c < NT:
                    n = ROWS[c]
                    for half in range(2):
                        ps = claim(pe, ("op", c, half))
                        for j in range(2 * NH):
                            m = (j + NH) % (2 * NH)
                            ins = pe.matmul(ps[0:n, :], GY[:, m, c * P:c * P + n], WC[:, half, m, :],
                                            start=(j == 0), stop=(j == 2 * NH - 1))
                        written(ins, ("op", c, half))
                if c > 0:
                    pe.wait_ge(s_xs, NT + c)
                    transpose_rows("x2t", c - 1)
                    b, u = ROT[("x2t", c - 1, 1)]
                    pe.wait_ge(s_written[b], u + 1)
                    pe.sem_inc(s_xst, 1)
                    n = ROWS[c - 1]
                    ps = claim(pe, ("lg", c - 1))
                    await_read(pe, ("x2t", c - 1, 1))
                    for k in range(KD):
                        ins = pe.matmul(ps[0:n, 0:GROUPS + NE], XNT[:, k, (c - 1) * P:(c - 1) * P + n], WR[:, k, :],
                                        start=(k == 0), stop=(k == KD - 1))
                    written(ins, ("lg", c - 1))

            ps = claim(pe, ("pos",))
            pe.wait_ge(s_oh, 1)
            for i in range(NT + 1):
                out = ps[:, i * NE:(i + 1) * NE]
                for j in range(min(i + 1, NT)):
                    lhs = LTRI if j == i else ONES
                    last = j == min(i, NT - 1)
                    ins = pe.matmul(out, lhs[0:ROWS[j], :], LMSK[0:ROWS[j], j, :], start=(j == 0), stop=last)
            written(ins, ("pos",))
            pe.wait_ge(s_rnd, 1)
            rounds = pe.value_load(NRND[0:1, 0:1], min_val=1, max_val=5)

            def turn(n, p, use):
                pe.wait_ge(s_xg[p], 16 * (use + 1))
                pe.wait_ge(s_xgt, 2 * n + 1)
                xv = XG[p].rearrange("t (p k) -> t k p", k=KD)
                for k in range(KD):
                    ins = pe.transpose(PS[k // 4][:, (k % 4) * P:(k % 4 + 1) * P], xv[:, k, :], IDENT[:])
                ins.then_inc(s_tw, 1)

            def up(n, p, use):
                pe.wait_ge(s_xgt, 2 * n + 3)
                pe.wait_ge(s_w13[p], 32 * (use + 1))
                for j, w in ((0, W1[p]), (1, W3[p])):
                    for k in range(KD):
                        ins = pe.matmul(PS[2 + p][:, j * FE:(j + 1) * FE], XGT[p][:, k, :], w[:, k, :],
                                        start=(k == 0), stop=(k == KD - 1))
                ins.then_inc(s_hw, 1)

            def turn_h(n, p):
                pe.wait_ge(s_hg, n + 1)
                pe.wait_ge(s_ht, n + 1)
                hv = HG[p].rearrange("t (p j) -> t j p", j=2)
                for j in range(2):
                    ins = pe.transpose(PS[4][:, j * P:(j + 1) * P], hv[:, j, :], IDENT[:])
                ins.then_inc(s_htw, 1)

            def down(n, p, use):
                pe.wait_ge(s_ht, n + 2)
                pe.wait_ge(s_w2[p], 16 * (use + 1))
                pe.wait_ge(s_ya, n + 1)
                pe.wait_ge(s_yd, n + 1)
                for half in range(2):
                    for j in range(2):
                        ins = pe.matmul(PS[5 + half][:, :], HT[p][:, j, :], W2[p][:, j, half * 512:(half + 1) * 512],
                                        start=(j == 0), stop=(j == 1))
                ins.then_inc(s_yw, 1)

            pe.sem_inc(s_pmu, 1)
            with pe.Fori(0, rounds) as r:
                base = r * NE
                for j in range(2 * NT):
                    i, k = j // 2, j % 2
                    pe.wait_ge(s_pm, r * (2 * NT) + j + 1)
                    ins = pe.matmul(PS[B_O][:, 0:NE], PM[0:ROWS[i], j % 2, :], OHV[0:ROWS[i], k, i, :],
                                    start=(j == 0), stop=(j == 2 * NT - 1))
                    if j < 2 * NT - 1:
                        ins.then_inc(s_pmu, 1)
                ins.then_inc(s_tab, 1)
                pe.wait_ge(s_tab, r + 1)
                pe.sem_inc(s_pmu, 1)
                half_n = r * (NE // 2)
                turn(base, 0, half_n)
                turn(base + 1, 1, half_n)
                up(base, 0, half_n)
                turn_h(base, 0)
                with pe.Fori(0, NE // 2 - 1) as i:
                    for j in range(2):
                        e = base + i * 2 + 1 + j
                        p = 1 - j
                        turn(e + 1, 1 - p, half_n + i + 1)
                        up(e, p, half_n + i + j)
                        down(e - 1, 1 - p, half_n + i)
                        turn_h(e, p)
                e = base + NE - 1
                up(e, 1, half_n + NE // 2 - 1)
                down(e - 1, 0, half_n + NE // 2 - 1)
                turn_h(e, 1)
                down(e, 1, half_n + NE // 2 - 1)


_INS = ["x_prompt", "x_sample", "state_hgrn", "state_rglru", "state_conv", "lower_bounds", "ln1_g", "w_in",
        "hgrn_norm_g", "conv_w", "conv_b", "lru_wx", "lru_bx", "lru_wa", "lru_ba", "lru_lambda", "w_out", "ln2_g",
        "router_wg", "router_bg", "router_we", "router_be", "exp_w1", "exp_w3", "exp_w2", "final_g"]
_OUTS = [(1, SEQ, D), (NS, 1, D), (1, 1, NH, P, P), (1, 1, 512), (1, 1, 3, 512),
         (1, NS, NH, P, P), (1, NS, 512), (1, NS, 3, 512)]


def kernel(**inputs):
    import numpy as _np
    import concourse.bacc as _bacc
    from concourse.bass_utils import run_bass_kernel_spmd as _run

    nc = _bacc.Bacc("TRN2", target_bir_lowering=False, num_devices=1)
    arrays, args = {}, []
    for name in _INS:
        a = _np.ascontiguousarray(inputs[name])
        arrays[f"in_{name}"] = a
        args.append(nc.dram_tensor(f"in_{name}", a.shape, F32, kind="ExternalInput").ap())
    for i, shape in enumerate(_OUTS):
        args.append(nc.dram_tensor(f"out_{i}", shape, F32, kind="ExternalOutput").ap())
    build(nc, *args)
    r = _run(nc, [arrays], core_ids=[0])
    return tuple(r.results[0][f"out_{i}"] for i in range(len(_OUTS)))
```

```python
from contextlib import ExitStack
from math import pi, sqrt

import concourse.bass as bass
from concourse import mybir

F32 = mybir.dt.float32
I32 = mybir.dt.int32
U32 = mybir.dt.uint32
ALU = mybir.AluOpType
ACT = mybir.ActivationFunctionType
AX_X = mybir.AxisListType.X

P = 128
D = 1024
SEQ, NS = 512, 8
TOK = SEQ + NS
HALF = TOK // 2
KD = D // P
NH = 4
CH = SEQ // P
NT = CH + 1
ROWS = [P] * CH + [NS]
GROUPS, PER_GROUP = 4, 8
NE = GROUPS * PER_GROUP
FE = 256
CAP = 64
NPAIR = NE // 2
MAX_ROUNDS = -(-TOK // CAP)
NPM = 4
NR = 3
BIG = 4096
EPS = 1e-6
SUB = 32

LB, HGG, CW, CB, BX, BA, LAM, H0 = 0, 8, 12, 28, 32, 36, 40, 44
NPAR = H0 + NS * NH
V_FA, V_FB, V_NFB, V_C, V_NC, V_BX, V_BA, V_HG, V_T0, V_T1, V_T2, V_T3 = range(0, 48, 4)

XR, FX, Q, V, GR, G = 4, 1, 0, 2, 5, 3
ORDER = [XR, FX, Q, V, GR, G]


def rotation():
    r = []
    for i in range(NT):
        r += [("xt", i, 0), ("xt", i, 1)]
    r += [("par", 0), ("par", 1)]
    for name in ("xr", "fx"):
        r += [(name, m, h) for m in range(NH) for h in range(2)]
    for m in range(NH):
        r += [("q", m, 0), ("q", m, 1)]
        r += [(g, m, h) for g in ("gx", "ga") for h in range(2)]
    r += [("v", c) for c in range(NT)]
    r += [("xtail",)]
    for s in range(8):
        r += [("gr" if s < 4 else "g", s % 4, 0), ("gr" if s < 4 else "g", s % 4, 1)]
        if s % 2 and s >= 3:
            r += [("mean", (s - 3) // 2)]
        r += [("vb", s)]
    r += [("mean", 3), ("mean", 4), ("htail",)]
    for c in range(NT + 1):
        if c < NT:
            r += [("op", c, 0), ("op", c, 1)]
        if c > 0:
            r += [("x2t", c - 1, 0), ("x2t", c - 1, 1), ("lg", c - 1)]
    r += [("pos",)]
    return {name: (n % NR, n // NR) for n, name in enumerate(r)}


ROT = rotation()


def build(nc, x_prompt, x_sample, state_hgrn, state_rglru, state_conv, lower_bounds, ln1_g, w_in,
          hgrn_norm_g, conv_w, conv_b, lru_wx, lru_bx, lru_wa, lru_ba, lru_lambda, w_out, ln2_g,
          router_wg, router_bg, router_we, router_be, exp_w1, exp_w3, exp_w2, final_g,
          y_prompt, y_sample, hgrn_p, rglru_p, conv_p, hgrn_s, rglru_s, conv_s):
    xn_dram = nc.dram_tensor("xn_rows", (TOK, D), F32).ap()
    ye_dram = nc.dram_tensor("expert_rows", (2 * TOK, D), F32).ap()

    def x_rows(i):
        return x_prompt[0, i * P:(i + 1) * P, :] if i < CH else x_sample.rearrange("b s d -> (b s) d")

    def y_rows(i):
        return y_prompt[0, i * P:(i + 1) * P, :] if i < CH else y_sample.rearrange("b s d -> (b s) d")

    with ExitStack() as ctx:
        def sb(name, shape, dt=F32):
            return ctx.enter_context(nc.sbuf_tensor(name, shape, dt))

        def sem(name):
            return ctx.enter_context(nc.semaphore(name))

        X = sb("X", [P, NT, D])
        XS = sb("XS", [P, 2, D])
        XNT = sb("XNT", [P, KD, TOK])
        WC = sb("WC", [P, 2, KD, 512])
        SLOT0 = sb("SLOT0", [P, 6144])
        GXt = SLOT0[:, 0:NH * TOK].rearrange("p (m t) -> p m t", m=NH)
        GAt = SLOT0[:, NH * TOK:2 * NH * TOK].rearrange("p (m t) -> p m t", m=NH)
        XRC = sb("XRC", [P, NH * (2 * TOK + 3)])
        XRt = XRC[:, 0:NH * (TOK + 3)].rearrange("p (m t) -> p m t", m=NH)
        XCt = XRC[:, NH * (TOK + 3):].rearrange("p (m t) -> p m t", m=NH)
        SLOT1 = sb("SLOT1", [P, 3 * NH * TOK])
        Ft = SLOT1[:, 0:NH * TOK].rearrange("p (m t) -> p m t", m=NH)
        Kt = SLOT1[:, NH * TOK:2 * NH * TOK].rearrange("p (m t) -> p m t", m=NH)
        Qt = SLOT1[:, 2 * NH * TOK:3 * NH * TOK].rearrange("p (m t) -> p m t", m=NH)
        GY = sb("GY", [P, 2 * NH, TOK])
        Vt = sb("Vt", [P, CH, 512])
        Vs = sb("Vs", [NS, 512])
        T = sb("T", [P, 2, 6, 512])
        TN = T[:, 0, 0:5, :].rearrange("p a t -> p (a t)")[:, 0:NH * TOK].rearrange("p (m t) -> p m t", m=NH)
        A2 = T[:, 1, 0:5, :].rearrange("p a t -> p (a t)")[:, 0:NH * TOK].rearrange("p (m t) -> p m t", m=NH)
        SC = SLOT0[:, 0:1024].rearrange("p (a c t) -> p a c t", a=2, c=CH)
        S = SLOT0[:, 1024:2048].rearrange("p (a c t) -> p a c t", a=2, c=CH)
        KT = SLOT0[:, 2048:2560].rearrange("p (c t) -> p c t", c=CH)
        NB = SLOT0[:, 2560:3072]
        SST = XS[:, 1, :].rearrange("p (a t) -> p a t", a=2)
        SKV = XS[:, 0, 0:512]
        OS = sb("OS", [P, NH * NS])
        OSB = sb("OSB", [P, NH * NS])
        AC = sb("AC", [P, NH, CH])
        PROW = sb("PROW", [NPAR, P])
        CROW = sb("CROW", [NS * 3 * NH, P])
        PARAM = sb("PARAM", [P, NPAR])
        CVT = sb("CVT", [P, NS * 3 * NH])
        VEC = sb("VEC", [P, 48])
        G1 = sb("G1", [P, KD])
        G2 = sb("G2", [P, KD])
        BDX = sb("BDX", [P, NH, P])
        BDA = sb("BDA", [P, NH, P])
        TAIL = BDX[0:11, :, :].rearrange("p m t -> p (m t)")
        HTAIL = BDA[0:9, :, :].rearrange("p m t -> p (m t)")
        SSQ = sb("SSQ", [P, NT])
        RSTD = sb("RSTD", [P, NT])
        EPSC = sb("EPSC", [P, 1])
        IDENT = sb("IDENT", [P, P])
        MEAN128 = sb("MEAN128", [P, P])
        ONES = sb("ONES", [P, P])
        LTRI = sb("LTRI", [P, P])
        CMASK = sb("CMASK", [P, P])
        RESET = sb("RESET", [P, CH, P])
        SCR = sb("SCR", [P, 8, NS])
        V_FLAT = Vt[:, :, :].rearrange("p c t -> p (c t)")
        used = [0]

        def over_v(shape):
            n = 1
            for x in shape[1:]:
                n *= x
            v = V_FLAT[:, used[0]:used[0] + n]
            used[0] += n
            if len(shape) == 3:
                return v.rearrange("p (a b) -> p a b", a=shape[1])
            return v.rearrange("p (k a b) -> p k a b", k=shape[1], a=shape[2])

        WGt = sb("WGt", [P, KD * GROUPS])
        WEt = sb("WEt", [P, GROUPS, KD * PER_GROUP])
        WR = sb("WR", [P, KD, GROUPS + NE])
        RB = sb("RB", [P, GROUPS + NE])
        LG = over_v([P, NT, GROUPS + NE])
        L8 = over_v([P, NT, 8])
        TOP = over_v([P, NT, 8])
        TIX = sb("TIX", [P, NT, 8], U32)
        GIX = sb("GIX", [P, NT])
        GEX = over_v([P, NT, GROUPS])
        PTOP = sb("PTOP", [P, NT])
        LSEL = over_v([P, NT, NE])
        LMSK = over_v([P, 1, NE])
        CHO = over_v([P, NT + 1, NE])
        CUM = over_v([P, NT + 1, NE])
        EIX = sb("EIX", [P, NT, 2])
        OH = over_v([P, 2, NT, NE])
        OHV = over_v([P, 2, NT, NE])
        RANK = sb("RANK", [P, 2, NT])
        WK = sb("WK", [P, 2, NT])
        CNT = sb("CNT", [P, 2])
        NRND = sb("NRND", [P, 1], I32)
        IOI = SLOT1[:, 2 * NH * TOK:2 * NH * TOK + 2 * NE + P + 2 * NT].bitcast(I32)
        IOF = sb("IOF", [P, NE + NE + P + 2 * NT])
        iota_e, iota_g = IOF[:, 0:NE], IOF[:, NE:2 * NE]
        iota_s = IOF[:, 2 * NE:2 * NE + P]
        token_code = IOF[:, 2 * NE + P:].rearrange("p (i k) -> p k i", k=2)
        PM = over_v([P, NPM, P])
        DSTI = sb("DSTI", [P, NPAIR], I32)
        SRCI = sb("SRCI", [P, NPAIR], I32)
        GIDX = sb("GIDX", [P, 2, 1], I32)
        SIDX = sb("SIDX", [P, 2, 1], I32)
        XG = [T[:, j, 0:2, :].rearrange("p a t -> p (a t)") for j in range(2)]
        YO = [T[:, j, 2:4, :].rearrange("p a t -> p (a t)") for j in range(2)]
        XGT = [XRC[:, 1024 * j:1024 * (j + 1)].rearrange("p (k t) -> p k t", k=KD) for j in range(2)]
        HS = [XRC[:, 2048 + FE * j:2048 + FE * (j + 1)] for j in range(2)]
        HG = [XRC[:, 2560 + FE * j:2560 + FE * (j + 1)] for j in range(2)]
        HT = [XRC[:, 3072 + FE * j:3072 + FE * (j + 1)].rearrange("p (j t) -> p j t", j=2) for j in range(2)]
        GYF = GY[:, :, :].rearrange("p m t -> p (m t)")
        WCF = WC[:, :, :, :].rearrange("p a k t -> p (a k t)")
        W13 = [s[:, 0:4096].rearrange("p (k f) -> p k f", k=KD) for s in (SLOT0, SLOT1, WCF, GYF)]
        W2 = [s.rearrange("p (j d) -> p j d", j=2)
              for s in (SLOT0[:, 4096:6144], SLOT1[:, 4096:6144], WCF[:, 4096:6144], WCF[:, 6144:8192])]
        XNF = XNT[:, :, :].rearrange("p k t -> p (k t)")
        YE = [b.rearrange("p (k d) -> p k d", k=2) for b in
              (XNF[:, 0:2048], XNF[:, 2048:4096], SLOT0[:, 0:2048], SLOT0[:, 2048:4096], SLOT0[:, 4096:6144])]
        OUT = [SLOT1[:, D * c:D * (c + 1)] for c in range(NT)]
        FGB = T[:, 0, 4:6, :].rearrange("p a t -> p (a t)")

        PS = [ctx.enter_context(nc.psum_tensor(f"ps{b}", [P, 512], F32)) for b in range(8)]
        B_OS, B_SD, B_SL, B_KV, B_O = 3, 4, 5, 6, 7

        s_x = [sem(f"x_in{i}") for i in range(NT)]
        s_wc = [sem(f"wc_in{i}") for i in range(2)]
        s_wc_free = sem("wc_free")
        s_par = sem("param_rows_in")
        s_gain = sem("gains_in")
        s_bd = sem("gate_weights_in")
        s_rt = sem("router_weights_in")
        s_written = [sem(f"rot_written{i}") for i in range(NR)]
        s_read = [sem(f"rot_read{i}") for i in range(NR)]
        s_const = sem("constants_made")
        s_init = sem("scratch_initialised")
        s_pool = sem("pool_step")
        s_zero = sem("zeroed")
        s_zero_sc = sem("scores_zeroed")
        s_ssq = sem("squares_summed")
        s_rstd = sem("rstd_step")
        s_xs = sem("rows_scaled")
        s_xst = sem("rows_transposed")
        s_param = sem("param_ready")
        s_vec = sem("vec_step")
        s_vexp = sem("vec_exp")
        s_conv = sem("conv_step")
        s_xc = sem("xc_ready")
        s_f = sem("f_ready")
        s_gt = sem("gate_tanh_ready")
        s_a = sem("decay_a_ready")
        s_m2 = sem("mult_squared_ready")
        s_mu = sem("mult_ready")
        s_u = sem("u_step")
        s_h = sem("h_ready")
        s_k = sem("k_ready")
        s_lf = sem("logf_ready")
        s_b = sem("cumulated_ready")
        s_d = sem("exponents_ready")
        s_e = sem("decays_ready")
        s_ac = sem("chunk_decay_ready")
        s_qk = sem("decayed_qk_ready")
        s_scores = sem("scores_written")
        s_kt_ps = sem("kt_written")
        s_kt = sem("kt_ready")
        s_sc = sem("scores_ready")
        s_kv = sem("kv_written")
        s_s = sem("states_ready")
        s_o = sem("o_written")
        s_osq = sem("o_squared")
        s_rs = sem("head_rstd_step")
        s_yn = sem("y_normed")
        s_gel = sem("gelu_step")
        s_gela = sem("gelu_act")
        s_yb = sem("y_b_ready")
        s_tg = sem("g_tanh_ready")
        s_sg = sem("silu_ready")
        s_y = sem("y_a_ready")
        s_skv = sem("sample_kv_step")
        s_sst = sem("sample_state_ready")
        s_sin = [sem(f"sample_state_in{i}") for i in range(2)]
        s_sout = [sem(f"sample_state_out{i}") for i in range(2)]
        s_osw = sem("sample_o_written")
        s_oss = sem("sample_o_step")
        s_tail = sem("tails_ready")
        s_small_out = sem("small_outputs_written")
        s_hp = sem("hgrn_state_written")
        s_xn = [sem(f"xn_rows_written{i}") for i in range(2)]
        s_lg = sem("logits_ready")
        s_r = sem("router_step")
        s_rexp = sem("router_exp")
        s_oh = sem("onehots_ready")
        s_rnd = sem("rounds_known")
        s_pm = sem("slot_onehot_ready")
        s_pmu = sem("slot_onehot_used")
        s_tab = sem("table_written")
        s_tabr = sem("table_ready")
        s_tabs = sem("table_step")
        s_turn = sem("pool_turns")
        s_gi = sem("gather_index_copied")
        s_si = sem("scatter_index_copied")
        s_xg = [sem(f"rows_gathered{i}") for i in range(2)]
        s_ys = [sem(f"rows_scattered{i}") for i in range(2)]
        s_w13 = [sem(f"w13_in{i}") for i in range(4)]
        s_w2 = [sem(f"w2_in{i}") for i in range(4)]
        s_tw = sem("xg_transposed")
        s_xgt = sem("xgt_ready")
        s_hw = sem("h_written")
        s_silu = sem("silu_done")
        s_hg = sem("h_gated")
        s_htw = sem("h_transposed")
        s_ht = sem("ht_ready")
        s_yw = sem("y_written")
        s_ya = sem("y_half_a_read")
        s_yd = sem("y_half_b_read")
        s_rdone = sem("round_done")
        s_fg = sem("final_gain_in")
        s_ye = [sem(f"expert_rows_in{i}") for i in range(NT)]
        s_cmb = sem("combine_step")
        s_fr = sem("final_squares_summed")
        s_froot = sem("final_root_ready")
        s_frstd = sem("final_rstd_ready")
        s_fin = sem("final_ready")
        s_out = sem("y_out")

        def claim(pe, name):
            bank, use = ROT[name]
            if use > 0:
                pe.wait_ge(s_read[bank], use)
            return PS[bank]

        def written(ins, name):
            ins.then_inc(s_written[ROT[name][0]], 1)

        def await_ps(eng, name):
            bank, use = ROT[name]
            eng.wait_ge(s_written[bank], use + 1)
            return PS[bank]

        def read(ins, name):
            ins.then_inc(s_read[ROT[name][0]], 1)

        def await_read(eng, name):
            eng.wait_ge(s_read[ROT[name][0]], ROT[name][1] + 1)

        def bc(ap, axis, n):
            ap = ap.unsqueeze(axis)
            shape = list(ap.shape)
            shape[axis] = n
            return ap.to_broadcast(shape)

        def col(v, m):
            return VEC[:, v + m:v + m + 1]

        def load_w2(eng, e, slot):
            eng.dma_start(W2[slot], exp_w2[0, e].rearrange("(p j) d -> p j d", j=2)).then_inc(s_w2[slot], 16)

        block = ctx.enter_context(nc.Block())

        @block.sync
        def _(sp):
            sp.dma_start(X[:, 0, :], x_rows(0)).then_inc(s_x[0], 16)
            for i in range(1, NT):
                sp.dma_start(X[0:ROWS[i], i, :], x_rows(i)).then_inc(s_x[i], 16)
            w_in_v = w_in[0].rearrange("(p k) n -> p k n", k=KD)
            w_out_v = w_out[0].rearrange("(m p) n -> p m n", p=P)
            for j in range(8):
                if j >= 2:
                    sp.wait_ge(s_wc_free, j - 1)
                src = w_in_v[:, :, ORDER[j] * 512:(ORDER[j] + 1) * 512] if j < 6 else w_out_v[:, :, (j - 6) * 512:(j - 5) * 512]
                sp.dma_start(WC[:, j % 2, :, :], src).then_inc(s_wc[j % 2], 16)

            def load_w13(e, slot):
                for half, w in enumerate((exp_w1, exp_w3)):
                    sp.dma_start(W13[slot][:, :, half * FE:(half + 1) * FE],
                                 w[0, e].rearrange("(p k) f -> p k f", k=KD)).then_inc(s_w13[slot], 16)

            sp.wait_ge(s_y, NH + 1)
            sp.wait_ge(s_hp, 16 * NH)
            for e in range(2):
                load_w13(e, e)
                load_w2(sp, e, e)

            for c in range(NT):
                sp.wait_ge(s_xs, NT + c + 1)
                sp.dma_start(xn_dram[c * P:c * P + ROWS[c], :], XS[0:ROWS[c], c % 2, :]).then_inc(s_xn[c % 2], 16)
            sp.dma_start(FGB, final_g.rearrange("(a d) -> a d", a=1).partition_broadcast(P)).then_inc(s_fg, 16)

            await_read(sp, ("op", NT - 1, 1))
            for e in range(2, 4):
                load_w13(e, e)
                load_w2(sp, e, e)

            sp.wait_ge(s_rnd, 1)
            rounds = sp.value_load(NRND[0:1, 0:1], min_val=1, max_val=MAX_ROUNDS)
            with sp.Fori(0, rounds) as r:
                with sp.If(r > 0):
                    sp.wait_ge(s_yw, r * NE)
                    for e in range(4):
                        load_w13(e, e)
                        load_w2(sp, e, e)
                with sp.Fori(0, NE // 4 - 1) as i:
                    for slot in range(4):
                        sp.wait_ge(s_hw, r * NE + i * 4 + slot + 1)
                        load_w13(i * 4 + slot + 4, slot)

            sp.wait_ge(s_rdone, rounds + 1)
            ye_v = ye_dram.rearrange("(t k) d -> t k d", k=2)
            for c in range(NT):
                sp.dma_start(YE[c][0:ROWS[c]], ye_v[c * P:c * P + ROWS[c]]).then_inc(s_ye[c], 16)
            for c in range(NT):
                sp.wait_ge(s_fin, c + 1)
                sp.dma_start(y_rows(c), OUT[c][0:ROWS[c]]).then_inc(s_out, 16)
            sp.wait_ge(s_out, 16 * NT)

        @block.gpsimd
        def _(pool):
            step = [0]

            def chain(ins):
                step[0] += 1
                ins.then_inc(s_pool, 1)
                pool.wait_ge(s_pool, step[0])

            chain(pool.memset(IDENT[:], 0.0))
            pool.affine_select(out=IDENT[:], in_=IDENT[:], compare_op=ALU.not_equal, fill=1.0, base=0,
                               pattern=[[-1, P]], channel_multiplier=1).then_inc(s_const, 1)
            chain(pool.memset(BDX[:], 0.0))
            chain(pool.memset(BDA[:], 0.0))
            for bd, w in ((BDX, lru_wx), (BDA, lru_wa)):
                wv = w[0].rearrange("(m two) c d -> two c m d", two=2)
                for two in range(2):
                    pool.dma_start(bd[64 * two:64 * two + 64, :, 64 * two:64 * two + 64], wv[two]).then_inc(s_bd, 16)
            st_v = state_hgrn[0].rearrange("b h d e -> b d h e")
            so_v = hgrn_s[0].rearrange("b h d e -> b d h e")

            def load_state(b):
                pool.dma_start(SST[:, b % 2, :].rearrange("p (h e) -> p h e", h=NH), st_v[b]).then_inc(s_sin[b % 2], 16)

            pool.memset(ONES[:], 1.0).then_inc(s_pool, 1)
            pool.memset(MEAN128[:], 1.0 / P).then_inc(s_pool, 1)
            pool.memset(LTRI[:], 1.0).then_inc(s_pool, 1)
            pool.memset(CMASK[:], 1.0).then_inc(s_pool, 1)
            step[0] += 4
            pool.wait_ge(s_pool, step[0])
            chain(pool.affine_select(out=LTRI[:], in_=LTRI[:], compare_op=ALU.is_gt, fill=0.0, base=0,
                                     pattern=[[1, P]], channel_multiplier=-1))
            chain(pool.affine_select(out=CMASK[:], in_=CMASK[:], compare_op=ALU.is_ge, fill=0.0, base=0,
                                     pattern=[[1, P]], channel_multiplier=-1))
            for blk in range(P // SUB):
                part = CMASK[SUB * blk:SUB * (blk + 1), :]
                chain(pool.affine_select(out=part, in_=part, compare_op=ALU.is_ge, fill=0.0, base=SUB * (blk + 1) - 1,
                                         pattern=[[-1, P]], channel_multiplier=0))
            chain(pool.iota(IOI[:, 0:NE], [[1, NE]], base=0, channel_multiplier=0))
            chain(pool.iota(IOI[:, NE:2 * NE], [[1, GROUPS], [0, PER_GROUP]], base=0, channel_multiplier=0))
            chain(pool.iota(IOI[:, 2 * NE:2 * NE + P], [[0, P // CAP], [1, CAP]], base=0, channel_multiplier=0))
            pool.iota(IOI[:, 2 * NE + P:], [[2 * P, NT], [1, 2]], base=-BIG, channel_multiplier=2).then_inc(s_const, 1)

            pool.wait_ge(s_xst, NT)
            load_state(0)
            load_state(1)

            pool.dma_start(conv_s[0, :, 0:2, :], state_conv[0, :, 1:3, :]).then_inc(s_small_out, 16)
            pool.wait_ge(s_tail, 1)
            pool.dma_start(conv_p[0, 0], TAIL[0:3, :]).then_inc(s_small_out, 16)
            pool.dma_start(conv_s[0, :, 2, :], TAIL[3:11, :]).then_inc(s_small_out, 16)
            for b in range(NS):
                pool.wait_ge(s_sst, b + 1)
                pool.dma_start(so_v[b], SST[:, b % 2, :].rearrange("p (h e) -> p h e", h=NH)).then_inc(s_sout[b % 2], 16)
                if b + 2 < NS:
                    pool.wait_ge(s_sout[b % 2], 16 * (b // 2 + 1))
                    pool.wait_ge(s_osw, b + 1)
                    load_state(b + 2)
                if b % 2 == 1:
                    h = b // 2
                    pool.wait_ge(s_s, CH * (h + 1))
                    pool.dma_start(hgrn_p[0, 0, h], S[:, h % 2, CH - 1, :]).then_inc(s_hp, 16)
            pool.wait_ge(s_tail, 2)
            pool.dma_start(rglru_p[0], HTAIL[0:1, :]).then_inc(s_ys[0], 16)
            pool.dma_start(rglru_s[0], HTAIL[1:9, :]).then_inc(s_ys[1], 16)

            pool.wait_ge(s_hp, 16 * NH)
            pool.wait_ge(s_y, NH + 1)
            pool.memset(XG[0], 0.0).then_inc(s_zero, 1)
            pool.memset(XG[1], 0.0).then_inc(s_zero, 1)
            pool.wait_ge(s_zero, 2)
            pool.wait_ge(s_xn[0], 16 * 3)
            pool.wait_ge(s_xn[1], 16 * 2)
            pool.wait_ge(s_rnd, 1)
            rounds = pool.value_load(NRND[0:1, 0:1], min_val=1, max_val=MAX_ROUNDS)

            def gather(n, q, p):
                pool.wait_ge(s_tw, n - 1)
                pool.sem_inc(s_turn, 1)
                pool.tensor_copy(GIDX[:, p, :], SRCI[:, q]).then_inc(s_gi, 1)
                pool.wait_ge(s_gi, n + 1)
                pool.sem_inc(s_turn, 1)
                pool.indirect_dma_start(out=XG[p], out_offset=None, in_=xn_dram,
                                        in_offset=bass.IndirectOffsetOnAxis(ap=GIDX[:, p, :].bitcast(U32), axis=0),
                                        bounds_check=TOK - 1, oob_is_err=False).then_inc(s_xg[p], 16)

            def scatter(n, q, p, use):
                pool.wait_ge(s_ys[p], 16 * use + 16)
                pool.sem_inc(s_turn, 1)
                pool.tensor_copy(SIDX[:, p, :], DSTI[:, q]).then_inc(s_si, 1)
                pool.wait_ge(s_si, n + 1)
                pool.wait_ge(s_ya, n + 2)
                pool.wait_ge(s_yd, n + 2)
                pool.sem_inc(s_turn, 1)
                pool.indirect_dma_start(out=ye_dram, out_offset=bass.IndirectOffsetOnAxis(ap=SIDX[:, p, :].bitcast(U32), axis=0),
                                        in_=YO[p], in_offset=None,
                                        bounds_check=2 * TOK - 1, oob_is_err=False).then_inc(s_ys[p], 16)

            pool.sem_inc(s_rdone, 1)
            with pool.Fori(0, rounds) as r:
                base = r * NPAIR
                pool.wait_ge(s_tabr, r + 1)
                pool.sem_inc(s_turn, 1)
                for q in range(2):
                    pool.tensor_copy(GIDX[:, q, :], SRCI[:, q:q + 1]).then_inc(s_gi, 1)
                    pool.wait_ge(s_gi, base + q + 1)
                    pool.sem_inc(s_turn, 1)
                    pool.indirect_dma_start(out=XG[q], out_offset=None, in_=xn_dram,
                                            in_offset=bass.IndirectOffsetOnAxis(ap=GIDX[:, q, :].bitcast(U32), axis=0),
                                            bounds_check=TOK - 1, oob_is_err=False).then_inc(s_xg[q], 16)
                gather(base + 2, slice(2, 3), 0)
                with pool.Fori(0, NPAIR // 2 - 2) as i:
                    for p in range(2):
                        q = i * 2 + p
                        gather(base + q + 3, bass.ds(q + 3, 1), 1 - p)
                        scatter(base + q, bass.ds(q, 1), p, r * (NPAIR // 2) + i)
                gather(base + NPAIR - 1, slice(NPAIR - 1, NPAIR), 1)
                for q in range(NPAIR - 4, NPAIR):
                    scatter(base + q, slice(q, q + 1), q % 2, r * (NPAIR // 2) + q // 2)
                pool.wait_ge(s_ys[0], (r + 1) * (NPAIR // 2 * 16) + 16)
                pool.wait_ge(s_ys[1], (r + 1) * (NPAIR // 2 * 16) + 16)
                pool.sem_inc(s_rdone, 1)
            pool.wait_ge(s_small_out, 16 * 3)
            pool.wait_ge(s_sout[0], 16 * 4)
            pool.wait_ge(s_sout[1], 16 * 4)

        @block.scalar
        def _(act):
            rows = [(lower_bounds, LB, 8), (hgrn_norm_g, HGG, 4), (conv_w[0], CW, 16), (conv_b, CB, 4), (lru_bx, BX, 4),
                    (lru_ba, BA, 4), (lru_lambda, LAM, 4), (state_rglru[0], H0, NS * NH)]
            act.dma_start(G1[:], ln1_g[0].rearrange("(p k) -> p k", k=KD)).then_inc(s_gain, 16)
            for src, at, n in rows:
                act.dma_start(PROW[at:at + n, :], src.rearrange("a (m p) -> (a m) p", p=P)).then_inc(s_par, 16)
            act.dma_start(CROW[:], state_conv[0].rearrange("b w (m p) -> (b w m) p", p=P)).then_inc(s_par, 16)
            act.dma_start(G2[:], ln2_g[0].rearrange("(p k) -> p k", k=KD)).then_inc(s_gain, 16)
            act.dma_start(WGt[:], router_wg[0].rearrange("(p k) g -> p (k g)", k=KD)).then_inc(s_rt, 16)
            act.dma_start(WEt[:], router_we[0].rearrange("g (p k) e -> p g (k e)", k=KD)).then_inc(s_rt, 16)
            act.dma_start(RB[:, 0:GROUPS], router_bg[0:1, :].to_broadcast([P, GROUPS])).then_inc(s_rt, 16)
            act.dma_start(RB[:, GROUPS:], router_be.rearrange("a g e -> a (g e)").to_broadcast([P, NE])).then_inc(s_rt, 16)

            act.wait_ge(s_init, 3)
            for i in range(NT):
                act.wait_ge(s_x[i], 16)
                if i >= 2:
                    act.wait_ge(s_ssq, i - 1)
                act.activation(XS[0:ROWS[i], i % 2, :], X[0:ROWS[i], i, :], ACT.Square,
                               accum_out=SSQ[0:ROWS[i], i:i + 1]).then_inc(s_ssq, 1)
            act.wait_ge(s_ssq, NT)
            act.activation(RSTD[:], SSQ[:], ACT.Sqrt, scale=1.0 / D, bias=EPSC[:]).then_inc(s_rstd, 1)
            act.wait_ge(s_rstd, 2)
            for i in range(NT):
                if i >= 2:
                    act.wait_ge(s_xst, i - 1)
                act.activation(XS[0:ROWS[i], i % 2, :], X[0:ROWS[i], i, :], ACT.Copy,
                               scale=RSTD[0:ROWS[i], i:i + 1]).then_inc(s_xs, 1)

            act.wait_ge(s_vec, 2)
            act.activation(VEC[:, V_T0:V_T0 + 8], VEC[:, V_T0:V_T0 + 8], ACT.Exp).then_inc(s_vexp, 1)

            def halves(name, m, dst, off, func, **kw):
                for h in range(2):
                    ps = await_ps(act, (name, m, h))
                    read(act.activation(dst[:, m, off + h * HALF:off + (h + 1) * HALF], ps[:, 0:HALF], func, **kw),
                         (name, m, h))

            for m in range(NH):
                halves("xr", m, XRt, 3, ACT.Copy)
            for m in range(NH):
                halves("fx", m, Kt, 0, ACT.Tanh, scale=0.5)
            act.wait_ge(s_param, 1)
            for m in range(NH):
                halves("gx", m, GXt, 0, ACT.Tanh, scale=0.5, bias=col(V_BX, m))
                halves("ga", m, GAt, 0, ACT.Tanh, scale=0.5, bias=col(V_BA, m))
                await_read(act, ("ga", m, 1))
                act.activation(TN[:, m, :], GAt[:, m, :], ACT.Tanh, scale=col(V_NC, m), bias=col(V_NC, m)).then_inc(s_gt, 1)
                act.activation(GAt[:, m, :], GAt[:, m, :], ACT.Exp, scale=col(V_C, m), bias=col(V_C, m)).then_inc(s_a, 1)
                act.wait_ge(s_a, m + 1)
                act.activation(A2[:, m, :], GAt[:, m, :], ACT.Square).then_inc(s_gt, 1)
            for m in range(NH):
                act.wait_ge(s_m2, 2 * (m + 1))
                act.activation(TN[:, m, :], TN[:, m, :], ACT.Ln, scale=0.25).then_inc(s_mu, 1)
                act.wait_ge(s_mu, 2 * m + 1)
                act.activation(TN[:, m, :], TN[:, m, :], ACT.Exp, scale=0.5).then_inc(s_mu, 1)
            act.wait_ge(s_f, NH)
            for h in range(NH):
                act.activation(Ft[:, h, 0:SEQ], Ft[:, h, 0:SEQ], ACT.Ln).then_inc(s_lf, 1)

            def decays(h):
                t = T[:, h % 2]
                act.wait_ge(s_d, 4 * (h + 1))
                for j, half in ((0, 64), (1, 32)):
                    v = t[:, j, :].rearrange("p (n two l) -> p n two l", two=2, l=half)
                    act.activation(v[:, :, 1, :], v[:, :, 1, :], ACT.Exp).then_inc(s_e, 1)
                    act.activation(v[:, :, 0, :], v[:, :, 0, :], ACT.Exp, scale=-1.0).then_inc(s_e, 1)
                act.activation(t[:, 4, :], t[:, 2, :], ACT.Exp).then_inc(s_e, 1)
                act.activation(t[:, 2, :], t[:, 2, :], ACT.Exp, scale=-1.0).then_inc(s_e, 1)
                act.activation(t[:, 5, :], Ft[:, h, 0:SEQ], ACT.Exp).then_inc(s_e, 1)
                act.activation(t[:, 3, :], t[:, 3, :], ACT.Exp).then_inc(s_e, 1)
                act.activation(AC[:, h, :], Ft[:, h, 0:SEQ].rearrange("p (c t) -> p c t", c=CH)[:, :, P - 1], ACT.Exp).then_inc(s_ac, 1)

            def square_o(h):
                act.wait_ge(s_o, h + 1)
                if h >= 1:
                    act.wait_ge(s_rs, 2 * h)
                    act.wait_ge(s_yn, h)
                act.activation(NB, PS[B_O][:, :], ACT.Square).then_inc(s_osq, 1)

            def head_rstd(h):
                ps = await_ps(act, ("mean", h))
                read(act.activation(NB, ps[:, :], ACT.Ln, bias=EPSC[:]), ("mean", h))
                await_read(act, ("mean", h))
                act.activation(NB, NB, ACT.Exp, scale=-0.5).then_inc(s_rs, 2)

            decays(0)
            for s in range(8):
                name, m = ("gr" if s < 4 else "g"), s % 4
                halves(name, m, GY[:, NH:, :] if s < 4 else GY[:, 0:NH, :], 0, ACT.Copy)
                if s < 4:
                    await_read(act, (name, m, 1))
                    act.wait_ge(s_tail, 1)
                    act.activation(XRt[:, m, 0:TOK], GY[:, NH + m, :], ACT.Square).then_inc(s_gela, 1)
                if s % 2 == 0:
                    h = s // 2
                    act.wait_ge(s_kt_ps, h + 1)
                    if h >= 1:
                        act.wait_ge(s_kv, h)
                    act.activation(KT, PS[B_KV][:, :].rearrange("p (c t) -> p c t", c=CH), ACT.Copy).then_inc(s_kt, 1)
                    if h >= 1:
                        square_o(h - 1)
                    if h + 1 < NH:
                        decays(h + 1)
                elif s >= 3:
                    head_rstd((s - 3) // 2)
                if s == 5:
                    for m2 in range(NH):
                        act.wait_ge(s_gel, 2 * (m2 + 1))
                        act.activation(XRt[:, m2, 0:TOK], XRt[:, m2, 0:TOK], ACT.Tanh, scale=sqrt(2 / pi)).then_inc(s_gela, 1)
            for m in range(NH):
                await_read(act, ("g", m, 1))
                act.wait_ge(s_yb, m + 1)
                act.activation(XRt[:, m, 0:TOK], GY[:, m, :], ACT.Tanh, scale=0.5).then_inc(s_tg, 1)
            square_o(NH - 1)
            head_rstd(NH - 1)
            act.wait_ge(s_oss, 1)
            act.activation(OSB[:], OS[:], ACT.Square).then_inc(s_oss, 1)
            ps = await_ps(act, ("mean", 4))
            act.wait_ge(s_oss, 2)
            read(act.activation(OSB[:], ps[:, 0:NH * NS], ACT.Ln, bias=EPSC[:]), ("mean", 4))
            await_read(act, ("mean", 4))
            act.activation(OSB[:], OSB[:], ACT.Exp, scale=-0.5).then_inc(s_oss, 1)

            for c in range(NT):
                n = ROWS[c]
                await_read(act, ("op", c, 1))
                if c == 0:
                    act.wait_ge(s_sout[0], 16 * 4)
                    act.wait_ge(s_sout[1], 16 * 4)
                if c >= 2:
                    act.wait_ge(s_xst, NT + c - 1)
                    act.wait_ge(s_xn[c % 2], 16 * (c // 2))
                act.activation(XS[0:n, c % 2, :], X[0:n, c, :], ACT.Square, accum_out=SSQ[0:n, c:c + 1]).then_inc(s_ssq, 1)
                act.wait_ge(s_ssq, NT + c + 1)
                act.activation(RSTD[0:n, c:c + 1], SSQ[0:n, c:c + 1], ACT.Sqrt, scale=1.0 / D, bias=EPSC[0:n, :]).then_inc(s_rstd, 1)
                act.wait_ge(s_rstd, 4 + 2 * c)
                act.activation(XS[0:n, c % 2, :], X[0:n, c, :], ACT.Copy, scale=RSTD[0:n, c:c + 1]).then_inc(s_xs, 1)

            act.wait_ge(s_rexp, 2 * NT)
            act.activation(GEX[:], GEX[:], ACT.Exp).then_inc(s_rexp, 1)
            act.activation(WK[:, 1, :], WK[:, 1, :], ACT.Exp).then_inc(s_rexp, 1)

            act.wait_ge(s_rnd, 1)
            rounds = act.value_load(NRND[0:1, 0:1], min_val=1, max_val=MAX_ROUNDS)

            def silu(n, p):
                act.wait_ge(s_hw, 2 * n + 2)
                act.activation(HS[p], PS[2 + p][:, 0:FE], ACT.Silu).then_inc(s_silu, 1)

            def ht_copy(n, p):
                act.wait_ge(s_htw, n + 1)
                act.activation(HT[p], PS[4][:, 0:2 * P].rearrange("p (j t) -> p j t", j=2), ACT.Copy).then_inc(s_ht, 1)

            def y_copy(n, p, scattered, load=None):
                act.wait_ge(s_yw, 2 * n + 2)
                if load is not None:
                    for slot in (2 * p, 2 * p + 1):
                        load_w2(act, load + slot, slot)
                act.wait_ge(s_ys[p], 16 * scattered + 16)
                act.activation(YO[p][:, 0:512], PS[5][:, :], ACT.Copy).then_inc(s_ya, 1)

            act.sem_inc(s_ht, 1)
            act.sem_inc(s_ya, 1)
            with act.Fori(0, rounds) as r:
                base = r * NPAIR
                silu(base, 0)
                ht_copy(base, 0)
                with act.Fori(0, NPAIR // 2 - 1) as i:
                    for j in range(2):
                        q = base + i * 2 + 1 + j
                        p = 1 - j
                        silu(q, p)
                        y_copy(q - 1, 1 - p, r * (NPAIR // 2) + i, load=i * 4 + 4)
                        ht_copy(q, p)
                q = base + NPAIR - 1
                silu(q, 1)
                y_copy(q - 1, 0, r * (NPAIR // 2) + NPAIR // 2 - 1)
                ht_copy(q, 1)
                y_copy(q, 1, r * (NPAIR // 2) + NPAIR // 2 - 1)

            for c in range(NT):
                n = ROWS[c]
                act.wait_ge(s_cmb, 2 * (c + 1))
                act.activation(OUT[c][0:n], X[0:n, c, :], ACT.Square, accum_out=SSQ[0:n, c:c + 1]).then_inc(s_fr, 1)
                act.wait_ge(s_fr, c + 1)
                act.activation(RSTD[0:n, c:c + 1], SSQ[0:n, c:c + 1], ACT.Sqrt, scale=1.0 / D, bias=EPSC[0:n, :]).then_inc(s_froot, 1)

        @block.vector
        def _(dve):
            vec = [0]

            def vstep(ins):
                vec[0] += 1
                ins.then_inc(s_vec, 1)
                dve.wait_ge(s_vec, vec[0])

            dve.memset(EPSC[:], EPS).then_inc(s_init, 1)
            dve.memset(SSQ[:], 1.0).then_inc(s_init, 1)
            dve.memset(RSTD[:], 1.0).then_inc(s_init, 1)
            dve.memset(XRt[:, :, 0:3], 0.0).then_inc(s_init, 1)
            dve.memset(RESET[:], 1.0).then_inc(s_init, 1)
            dve.wait_ge(s_init, 5)
            dve.memset(RESET[:, :, 0:1], 0.0).then_inc(s_init, 1)

            def evac_xt(name, i, gain):
                n = ROWS[i]
                for j in range(2):
                    ps = await_ps(dve, (name, i, j))
                    src = ps[:, :].rearrange("p (k t) -> p k t", k=4)[:, :, 0:n]
                    read(dve.tensor_tensor(XNT[:, 4 * j:4 * j + 4, i * P:i * P + n], src, bc(gain[:, 4 * j:4 * j + 4], 2, n), ALU.mult),
                         (name, i, j))

            dve.wait_ge(s_rstd, 1)
            dve.reciprocal(RSTD[:], RSTD[:]).then_inc(s_rstd, 1)
            dve.wait_ge(s_gain, 32)
            for i in range(NT):
                evac_xt("xt", i, G1)
            ps = await_ps(dve, ("par", 0))
            read(dve.tensor_copy(PARAM[:], ps[:, 0:NPAR]), ("par", 0))
            ps = await_ps(dve, ("par", 1))
            read(dve.tensor_copy(CVT[:], ps[:, 0:NS * 3 * NH]), ("par", 1))
            await_read(dve, ("par", 0))
            await_read(dve, ("par", 1))
            dve.wait_ge(s_const, 2)
            dve.tensor_copy(IOF[:], IOI[:, :]).then_inc(s_init, 1)

            def v4(at):
                return VEC[:, at:at + 4]

            def p4(at):
                return PARAM[:, at:at + 4]

            vstep(dve.tensor_tensor(v4(V_T0), p4(LB + 4), p4(LB), ALU.subtract))
            vstep(dve.scalar_tensor_tensor(out=v4(V_T1), in0=p4(LAM), scalar=-1.0, in1=p4(LAM), op0=ALU.mult, op1=ALU.min))
            dve.wait_ge(s_vexp, 1)
            vstep(dve.tensor_scalar(v4(V_T0), v4(V_T0), 1.0, None, ALU.add))
            vstep(dve.reciprocal(v4(V_T0), v4(V_T0)))
            vstep(dve.tensor_scalar(v4(V_FB), v4(V_T0), -0.5, 0.5, ALU.mult, ALU.add))
            vstep(dve.tensor_scalar(v4(V_NFB), v4(V_FB), -1.0, None, ALU.mult))
            vstep(dve.tensor_tensor(v4(V_FA), v4(V_T0), v4(V_FB), ALU.add))
            vstep(dve.tensor_scalar(v4(V_T2), v4(V_T1), 2.0, None, ALU.add))
            vstep(dve.reciprocal(v4(V_T2), v4(V_T2)))
            vstep(dve.tensor_tensor(v4(V_T1), v4(V_T1), v4(V_T2), ALU.mult))
            vstep(dve.tensor_tensor(v4(V_T2), v4(V_T1), v4(V_T1), ALU.mult))
            vstep(dve.tensor_scalar(v4(V_T3), v4(V_T2), 1.0 / 17, None, ALU.mult))
            for odd in (15, 13, 11, 9, 7, 5, 3):
                vstep(dve.scalar_tensor_tensor(out=v4(V_T3), in0=v4(V_T3), scalar=1.0 / odd, in1=v4(V_T2), op0=ALU.add, op1=ALU.mult))
            vstep(dve.scalar_tensor_tensor(out=v4(V_T3), in0=v4(V_T3), scalar=1.0, in1=v4(V_T1), op0=ALU.add, op1=ALU.mult))
            vstep(dve.tensor_scalar(v4(V_T1), p4(LAM), -1.0, 0.0, ALU.mult, ALU.max))
            vstep(dve.scalar_tensor_tensor(out=v4(V_T3), in0=v4(V_T3), scalar=2.0, in1=v4(V_T1), op0=ALU.mult, op1=ALU.add))
            vstep(dve.tensor_scalar(v4(V_C), v4(V_T3), -4.0, None, ALU.mult))
            vstep(dve.tensor_scalar(v4(V_NC), v4(V_T3), 4.0, None, ALU.mult))
            vstep(dve.tensor_scalar(v4(V_BX), p4(BX), 0.5, None, ALU.mult))
            vstep(dve.tensor_scalar(v4(V_BA), p4(BA), 0.5, None, ALU.mult))
            dve.tensor_scalar(v4(V_HG), p4(HGG), 0.5, None, ALU.mult).then_inc(s_param, 1)

            conv = [0]

            def cstep(ins):
                conv[0] += 1
                ins.then_inc(s_conv, 1)
                dve.wait_ge(s_conv, conv[0])

            dve.wait_ge(s_param, 1)
            for m in range(NH):
                await_read(dve, ("xr", m, 1))
                cstep(dve.tensor_scalar(XCt[:, m, 0:SEQ], XRt[:, m, 0:SEQ], PARAM[:, CW + m:CW + m + 1],
                                        PARAM[:, CB + m:CB + m + 1], ALU.mult, ALU.add))
                for w in range(1, 4):
                    cstep(dve.scalar_tensor_tensor(out=XCt[:, m, 0:SEQ], in0=XRt[:, m, w:w + SEQ],
                                                   scalar=PARAM[:, CW + 4 * w + m:CW + 4 * w + m + 1],
                                                   in1=XCt[:, m, 0:SEQ], op0=ALU.mult, op1=ALU.add))
            xs_c = XCt[:, :, SEQ:TOK]
            hist = CVT[:, :].rearrange("p (b w m) -> p w m b", b=NS, w=3)
            cstep(dve.tensor_tensor(xs_c, XRt[:, :, SEQ + 3:TOK + 3], bc(p4(CW + 12), 2, NS), ALU.mult))
            cstep(dve.tensor_tensor(xs_c, xs_c, bc(p4(CB), 2, NS), ALU.add))
            for w in range(3):
                cstep(dve.tensor_tensor(SCR[:, 0:NH, :], hist[:, w], bc(p4(CW + 4 * w), 2, NS), ALU.mult))
                cstep(dve.tensor_tensor(xs_c, xs_c, SCR[:, 0:NH, :], ALU.add))
            n_conv = conv[0]

            for h in range(NH):
                await_read(dve, ("fx", h, 1))
                dve.tensor_scalar(Ft[:, h, :], Kt[:, h, :], col(V_FB, h), col(V_FA, h), ALU.mult, ALU.add).then_inc(s_f, 1)
                dve.tensor_scalar(Kt[:, h, :], Kt[:, h, :], col(V_NFB, h), col(V_FB, h), ALU.mult, ALU.add).then_inc(s_k, 1)

            def mult_squared(m):
                dve.wait_ge(s_gt, 2 * (m + 1))
                dve.scalar_tensor_tensor(out=TN[:, m, :], in0=A2[:, m, :], scalar=1.0, in1=TN[:, m, :],
                                         op0=ALU.add, op1=ALU.mult).then_inc(s_m2, 1)
                dve.wait_ge(s_m2, 2 * m + 1)
                dve.tensor_scalar(TN[:, m, :], TN[:, m, :], 1e-18, None, ALU.max).then_inc(s_m2, 1)

            for m in range(NH):
                for hf in range(2):
                    ps = await_ps(dve, ("q", m, hf))
                    read(dve.tensor_copy(Qt[:, m, hf * HALF:(hf + 1) * HALF], ps[:, 0:HALF]), ("q", m, hf))
                if m >= 1:
                    mult_squared(m - 1)
            mult_squared(NH - 1)
            for c in range(NT):
                ps = await_ps(dve, ("v", c))
                dst = Vt[:, c, :] if c < CH else Vs[:]
                read(dve.tensor_copy(dst, ps[0:ROWS[c], :]), ("v", c))
            ps = await_ps(dve, ("xtail",))
            read(dve.tensor_copy(TAIL[:], ps[0:11, :]), ("xtail",))
            await_read(dve, ("xtail",))
            dve.sem_inc(s_tail, 1)

            ustep_n = [0]

            def ustep(ins):
                ustep_n[0] += 1
                ins.then_inc(s_u, 1)
                dve.wait_ge(s_u, ustep_n[0])

            dve.wait_ge(s_mu, 2 * NH)
            ustep(dve.memset(TN[:, :, 0:1], 0.5))
            for m in range(NH):
                ustep(dve.scalar_tensor_tensor(out=GXt[:, m, :], in0=GXt[:, m, :], scalar=1.0, in1=XCt[:, m, :],
                                               op0=ALU.add, op1=ALU.mult))
                ustep(dve.tensor_tensor(GXt[:, m, :], GXt[:, m, :], TN[:, m, :], ALU.mult))
                dve.tensor_tensor_scan(XCt[:, m, 0:SEQ], GAt[:, m, 0:SEQ], GXt[:, m, 0:SEQ], 0.0, ALU.mult, ALU.add).then_inc(s_h, 1)
            h0 = PARAM[:, H0:NPAR].rearrange("p (b m) -> p m b", b=NS)
            ustep(dve.tensor_tensor(SCR[:, 0:NH, :], GAt[:, :, SEQ:TOK], h0, ALU.mult))
            dve.tensor_tensor(XCt[:, :, SEQ:TOK], SCR[:, 0:NH, :], GXt[:, :, SEQ:TOK], ALU.add).then_inc(s_h, 1)

            def exponents(h):
                t = T[:, h % 2]
                if h >= 2:
                    dve.wait_ge(s_o, h - 1)
                dve.wait_ge(s_lf, h + 1)
                b = Ft[:, h, 0:SEQ]
                dve.tensor_tensor_scan(b, RESET[:, :, :].rearrange("p c t -> p (c t)"), b, 0.0, ALU.mult, ALU.add).then_inc(s_b, 1)
                dve.wait_ge(s_b, h + 1)
                for j, size, at in ((0, P, 63), (1, 64, 31), (2, SUB, SUB // 2 - 1)):
                    bv = b.rearrange("p (n l) -> p n l", l=size)
                    tv = t[:, j, :].rearrange("p (n l) -> p n l", l=size)
                    dve.tensor_tensor(tv, bv, bc(bv[:, :, at], 2, size), ALU.subtract).then_inc(s_d, 1)
                bv = b.rearrange("p (n l) -> p n l", l=P)
                dve.tensor_tensor(t[:, 3, :].rearrange("p (n l) -> p n l", l=P), bc(bv[:, :, P - 1], 2, P), bv,
                                  ALU.subtract).then_inc(s_d, 1)

            def decayed_qk(h):
                t = T[:, h % 2]
                dve.wait_ge(s_e, 8 * (h + 1))
                q, k = Qt[:, h, 0:SEQ], Kt[:, h, 0:SEQ]
                for j, half in ((0, 64), (1, 32)):
                    tv = t[:, j, :].rearrange("p (n two l) -> p n two l", two=2, l=half)
                    for two, x in ((1, q), (0, k)):
                        xv = x.rearrange("p (n two l) -> p n two l", two=2, l=half)
                        dve.tensor_tensor(tv[:, :, two, :], tv[:, :, two, :], xv[:, :, two, :], ALU.mult).then_inc(s_qk, 1)
                for j, x in ((4, q), (2, k), (5, q), (3, k)):
                    dve.tensor_tensor(t[:, j, :], t[:, j, :], x, ALU.mult).then_inc(s_qk, 1)

            def scores(h):
                dve.wait_ge(s_scores, h + 1)
                if h >= 2:
                    dve.wait_ge(s_o, h - 1)
                sc = SC[:, h % 2]
                sd = PS[B_SD][:, :].rearrange("p (c t) -> p c t", c=CH)
                sl = PS[B_SL][:, :].rearrange("p (c t) -> p c t", c=CH)
                dve.copy_predicated(sc, bc(CMASK[:].bitcast(I32), 1, CH), sd).then_inc(s_sc, 1)
                dve.wait_ge(s_sc, 4 * h + 1)
                for s0, n in ((0, 64), (0, 32), (64, 32)):
                    dve.tensor_copy(sc[s0:s0 + n, :, s0 + n:s0 + 2 * n], sl[s0:s0 + n, :, s0 + n:s0 + 2 * n]).then_inc(s_sc, 1)

            def states(h):
                dve.wait_ge(s_kv, h + 1)
                dve.wait_ge(s_ac, h + 1)
                if h >= 2:
                    dve.wait_ge(s_hp, 16 * (h - 1))
                    dve.wait_ge(s_o, h - 1)
                kv = PS[B_KV][:, :].rearrange("p (c t) -> p c t", c=CH)
                dve.tensor_copy(S[:, h % 2, 0, :], kv[:, 0, :]).then_inc(s_s, 1)
                for c in range(1, CH):
                    dve.wait_ge(s_s, CH * h + c)
                    dve.scalar_tensor_tensor(out=S[:, h % 2, c, :], in0=S[:, h % 2, c - 1, :], scalar=AC[:, h, c:c + 1],
                                             in1=kv[:, c, :], op0=ALU.mult, op1=ALU.add).then_inc(s_s, 1)

            def normed(h):
                dve.wait_ge(s_rs, 2 * (h + 1))
                dve.scalar_tensor_tensor(out=Kt[:, h, 0:SEQ], in0=PS[B_O][:, :], scalar=col(V_HG, h), in1=NB,
                                         op0=ALU.mult, op1=ALU.mult).then_inc(s_yn, 1)

            def sample_state(b):
                ps = await_ps(dve, ("vb", b))
                kv = SKV[:, :].rearrange("p (h e) -> p h e", h=NH)
                read(dve.tensor_tensor(kv, ps[:, :].rearrange("p (h e) -> p h e", h=NH), bc(Kt[:, :, SEQ + b], 2, P), ALU.mult),
                     ("vb", b))
                dve.wait_ge(s_sin[b % 2], 16 * (b // 2 + 1))
                st = SST[:, b % 2, :].rearrange("p (h e) -> p h e", h=NH)
                dve.tensor_tensor(st, st, bc(Ft[:, :, SEQ + b], 2, P), ALU.mult).then_inc(s_skv, 1)
                dve.wait_ge(s_skv, b + 1)
                await_read(dve, ("vb", b))
                dve.tensor_tensor(st, st, kv, ALU.add).then_inc(s_sst, 1)

            gel = [0]

            def gelu_argument(m):
                dve.wait_ge(s_gela, m + 1)
                dve.tensor_scalar(XRt[:, m, 0:TOK], XRt[:, m, 0:TOK], 0.044715, 1.0, ALU.mult, ALU.add).then_inc(s_gel, 1)
                dve.wait_ge(s_gel, 2 * m + 1)
                dve.tensor_tensor(XRt[:, m, 0:TOK], XRt[:, m, 0:TOK], GY[:, NH + m, :], ALU.mult).then_inc(s_gel, 1)

            dve.wait_ge(s_h, NH + 1)
            dve.memset(SC, 0.0).then_inc(s_zero_sc, 1)
            dve.wait_ge(s_zero_sc, 1)
            exponents(0)
            decayed_qk(0)
            dve.wait_ge(s_const, 2)
            for s in range(8):
                h = s // 2
                if s % 2 == 0:
                    scores(h)
                else:
                    states(h)
                    if s >= 3:
                        normed((s - 3) // 2)
                sample_state(s)
                if s % 2 == 0 and h + 1 < NH:
                    exponents(h + 1)
                    decayed_qk(h + 1)
                if s < 4:
                    gelu_argument(s)
                if s == 6:
                    for m in range(NH):
                        dve.wait_ge(s_gela, NH + m + 1)
                        yb = GY[:, NH + m, :]
                        dve.scalar_tensor_tensor(out=yb, in0=XRt[:, m, 0:TOK], scalar=1.0, in1=yb,
                                                 op0=ALU.add, op1=ALU.mult).then_inc(s_gel, 1)
                        dve.wait_ge(s_gel, 2 * NH + m + 1)
                        dve.scalar_tensor_tensor(out=yb, in0=yb, scalar=0.5, in1=XCt[:, m, :],
                                                 op0=ALU.mult, op1=ALU.mult).then_inc(s_yb, 1)
            dve.wait_ge(s_osw, NS)
            dve.tensor_copy(OS[:], PS[B_OS][:, 0:NH * NS]).then_inc(s_oss, 1)
            for m in range(NH):
                dve.wait_ge(s_tg, m + 1)
                dve.scalar_tensor_tensor(out=GY[:, m, :], in0=XRt[:, m, 0:TOK], scalar=1.0, in1=GY[:, m, :],
                                         op0=ALU.add, op1=ALU.mult).then_inc(s_sg, 1)
            normed(NH - 1)
            dve.wait_ge(s_sg, NH)
            for h in range(NH):
                dve.wait_ge(s_yn, h + 1)
                dve.tensor_tensor(GY[:, h, 0:SEQ], GY[:, h, 0:SEQ], Kt[:, h, 0:SEQ], ALU.mult).then_inc(s_y, 1)
            dve.wait_ge(s_oss, 3)
            dve.tensor_tensor(OS[:], OS[:], OSB[:], ALU.mult).then_inc(s_oss, 1)
            dve.wait_ge(s_oss, 4)
            os_v = OS[:, :].rearrange("p (h b) -> p h b", h=NH)
            dve.tensor_tensor(os_v, os_v, bc(v4(V_HG), 2, NS), ALU.mult).then_inc(s_oss, 1)
            dve.wait_ge(s_oss, 5)
            dve.tensor_tensor(GY[:, 0:NH, SEQ:TOK], GY[:, 0:NH, SEQ:TOK], os_v, ALU.mult).then_inc(s_y, 1)
            ps = await_ps(dve, ("htail",))
            read(dve.tensor_copy(HTAIL[:], ps[0:9, :]), ("htail",))
            await_read(dve, ("htail",))
            dve.sem_inc(s_tail, 1)

            rt = [0]

            def rstep(ins):
                rt[0] += 1
                ins.then_inc(s_r, 1)
                dve.wait_ge(s_r, rt[0])

            dve.wait_ge(s_rt, 16 * 4)
            dve.tensor_copy(WR[:, :, 0:GROUPS], WGt[:, :].rearrange("p (k g) -> p k g", k=KD)).then_inc(s_r, 1)
            for g in range(GROUPS):
                dve.tensor_copy(WR[:, :, GROUPS + PER_GROUP * g:GROUPS + PER_GROUP * (g + 1)],
                                WEt[:, g, :].rearrange("p (k e) -> p k e", k=KD)).then_inc(s_r, 1)
            dve.memset(LG[:], 0.0).then_inc(s_r, 1)
            dve.memset(L8[:], -3e38).then_inc(s_r, 1)
            dve.memset(CHO[:, NT, :], 0.0).then_inc(s_r, 1)
            dve.memset(CUM[:, 0, :], 0.0).then_inc(s_r, 1)
            rt[0] += 5 + GROUPS
            dve.wait_ge(s_r, rt[0])

            def route(c):
                rstep(dve.tensor_copy(L8[:, c, 0:GROUPS], LG[:, c, 0:GROUPS]))
                rstep(dve.max(TOP[:, c, :], L8[:, c, :]))
                rstep(dve.max_index(TIX[:, c, :], TOP[:, c, :], L8[:, c, :]))
                rstep(dve.tensor_copy(GIX[:, c:c + 1], TIX[:, c, 0:1]))
                dve.tensor_tensor(GEX[:, c, :], LG[:, c, 0:GROUPS], TOP[:, c, 0:1].to_broadcast([P, GROUPS]),
                                  ALU.subtract).then_inc(s_rexp, 1)
                rstep(dve.tensor_scalar(LMSK[:, 0, :], iota_g, GIX[:, c:c + 1], 3e38, ALU.is_equal, ALU.mult))
                rstep(dve.scalar_tensor_tensor(out=LSEL[:, c, :], in0=LMSK[:, 0, :], scalar=-3e38, in1=LG[:, c, GROUPS:],
                                               op0=ALU.add, op1=ALU.add))
                dve.wait_ge(s_rexp, 2 * c + 1)
                rstep(dve.max(TOP[:, c, :], LSEL[:, c, :]))
                rstep(dve.max_index(TIX[:, c, :], TOP[:, c, :], LSEL[:, c, :]))
                rstep(dve.tensor_copy(EIX[:, c, :], TIX[:, c, 0:2]))
                dve.tensor_tensor(WK[:, 1, c:c + 1], TOP[:, c, 1:2], TOP[:, c, 0:1], ALU.subtract).then_inc(s_rexp, 1)
                for k in range(2):
                    dve.tensor_scalar(OH[:, k, c, :], iota_e, EIX[:, c, k:k + 1], None, ALU.is_equal).then_inc(s_r, 1)
                    dve.tensor_scalar(OHV[:, k, c, :], iota_e, EIX[:, c, k:k + 1], token_code[:, k, c:c + 1],
                                      ALU.is_equal, ALU.mult).then_inc(s_r, 1)
                rt[0] += 4
                dve.wait_ge(s_r, rt[0])
                rstep(dve.tensor_tensor(CHO[:, c, :], OH[:, 0, c, :], OH[:, 1, c, :], ALU.add))
                n = ROWS[c]
                if n < P:
                    rstep(dve.tensor_copy(CUM[:, c + 1, :], CUM[:, c, :]))
                rstep(dve.tensor_tensor(CUM[0:n, c + 1, :], CUM[0:n, c, :], CHO[0:n, c, :], ALU.add))

            for c in range(NT + 1):
                if c < NT:
                    for half in range(2):
                        ps = await_ps(dve, ("op", c, half))
                        x = X[0:ROWS[c], c, half * 512:(half + 1) * 512]
                        read(dve.tensor_tensor(x, ps[0:ROWS[c], :], x, ALU.add), ("op", c, half))
                if c > 0:
                    evac_xt("x2t", c - 1, G2)
                if c < NT:
                    dve.wait_ge(s_rstd, 3 + 2 * c)
                    dve.reciprocal(RSTD[0:ROWS[c], c:c + 1], RSTD[0:ROWS[c], c:c + 1]).then_inc(s_rstd, 1)
                if c > 0:
                    ps = await_ps(dve, ("lg", c - 1))
                    n = ROWS[c - 1]
                    read(dve.tensor_tensor(LG[0:n, c - 1, :], ps[0:n, 0:GROUPS + NE], RB[0:n, :], ALU.add), ("lg", c - 1))
                    await_read(dve, ("lg", c - 1))
                    route(c - 1)
            dve.sem_inc(s_oh, 1)

            ps = await_ps(dve, ("pos",))
            pos = ps[:, 0:NT * NE].rearrange("p (i e) -> p i e", i=NT)
            for k in range(2):
                rstep(dve.tensor_tensor(LSEL[:], pos, OH[:, k], ALU.mult))
                rstep(dve.reduce_sum(RANK[:, k, :], LSEL[:], AX_X))
            rstep(dve.reduce_max(CNT[:, 0:1], ps[:, NT * NE:(NT + 1) * NE], AX_X))
            rstep(dve.tensor_scalar(NRND[:], CNT[:, 0:1], CAP - 1.0, None, ALU.add))
            dve.tensor_scalar(NRND[:], NRND[:], 6, None, ALU.arith_shift_right).then_inc(s_rnd, 1)
            dve.wait_ge(s_rnd, 1)
            rounds = dve.value_load(NRND[0:1, 0:1], min_val=1, max_val=MAX_ROUNDS)

            def xgt(n, p):
                dve.wait_ge(s_tw, n + 1)
                for j in range(2):
                    dve.tensor_tensor(XGT[p][:, 4 * j:4 * j + 4, :], PS[j][:, :].rearrange("p (k t) -> p k t", k=4),
                                      bc(G2[:, 4 * j:4 * j + 4], 2, P), ALU.mult).then_inc(s_xgt, 1)

            def gated(n, p):
                dve.wait_ge(s_silu, n + 1)
                dve.tensor_tensor(HG[p], PS[2 + p][:, FE:2 * FE], HS[p], ALU.mult).then_inc(s_hg, 1)

            def y_copy(n, p, scattered):
                dve.wait_ge(s_yw, 2 * n + 2)
                dve.wait_ge(s_ys[p], 16 * scattered + 16)
                dve.tensor_copy(YO[p][:, 512:1024], PS[6][:, :]).then_inc(s_yd, 1)

            dve.wait_ge(s_hp, 16 * NH)
            dve.sem_inc(s_xgt, 1)
            dve.sem_inc(s_yd, 1)
            with dve.Fori(0, rounds) as r:
                base = r * NPAIR
                dve.wait_ge(s_rdone, r + 1)
                for j in range(2 * NT):
                    i, k = j // 2, j % 2
                    dve.wait_ge(s_pmu, r * (2 * NT) + max(j - NPM + 1, 0) + 1)
                    dve.tensor_scalar(PM[:, j % NPM, :], iota_s, RANK[:, k, i:i + 1], None, ALU.is_equal).then_inc(s_pm, 1)
                dve.wait_ge(s_tab, r + 1)
                by_pair = PS[B_O][:, 0:NE].rearrange("p (q two) -> p q two", two=2)
                for two in range(2):
                    part = slice(two * CAP, (two + 1) * CAP)
                    dve.tensor_scalar(DSTI[part, 0:NPAIR], by_pair[part, :, two], float(BIG), None, ALU.add).then_inc(s_tabs, 1)
                dve.tensor_scalar(RANK[:], RANK[:], float(-CAP), None, ALU.add).then_inc(s_tabs, 1)
                dve.wait_ge(s_tabs, 3 * r + 3)
                dve.tensor_scalar(SRCI[:, 0:NPAIR], DSTI[:, 0:NPAIR], 1, None, ALU.arith_shift_right).then_inc(s_tabr, 1)
                xgt(base, 0)
                xgt(base + 1, 1)
                gated(base, 0)
                with dve.Fori(0, NPAIR // 2 - 1) as i:
                    for j in range(2):
                        q = base + i * 2 + 1 + j
                        p = 1 - j
                        xgt(q + 1, 1 - p)
                        gated(q, p)
                        y_copy(q - 1, 1 - p, r * (NPAIR // 2) + i)
                q = base + NPAIR - 1
                gated(q, 1)
                y_copy(q - 1, 0, r * (NPAIR // 2) + NPAIR // 2 - 1)
                y_copy(q, 1, r * (NPAIR // 2) + NPAIR // 2 - 1)

            dve.wait_ge(s_rexp, 2 * NT + 2)
            rstep(dve.reduce_sum(PTOP[:], GEX[:], AX_X))
            rstep(dve.reciprocal(PTOP[:], PTOP[:]))
            rstep(dve.tensor_scalar(WK[:, 0, :], WK[:, 1, :], 1.0, None, ALU.add))
            rstep(dve.reciprocal(WK[:, 0, :], WK[:, 0, :]))
            rstep(dve.tensor_tensor(WK[:, 0, :], WK[:, 0, :], PTOP[:], ALU.mult))
            rstep(dve.tensor_tensor(WK[:, 1, :], WK[:, 1, :], WK[:, 0, :], ALU.mult))

            dve.wait_ge(s_fg, 16)
            for c in range(NT + 1):
                if c < NT:
                    n = ROWS[c]
                    dve.wait_ge(s_ye[c], 16)
                    for k in range(2):
                        dve.scalar_tensor_tensor(out=X[0:n, c, :], in0=YE[c][0:n, k, :], scalar=WK[0:n, k, c:c + 1],
                                                 in1=X[0:n, c, :], op0=ALU.mult, op1=ALU.add).then_inc(s_cmb, 1)
                        dve.wait_ge(s_cmb, 2 * c + k + 1)
                if c > 0:
                    n = ROWS[c - 1]
                    dve.wait_ge(s_froot, c)
                    dve.reciprocal(RSTD[0:n, c - 1:c], RSTD[0:n, c - 1:c]).then_inc(s_frstd, 1)
                    dve.wait_ge(s_frstd, c)
                    dve.scalar_tensor_tensor(out=OUT[c - 1][0:n], in0=X[0:n, c - 1, :], scalar=RSTD[0:n, c - 1:c],
                                             in1=FGB[0:n], op0=ALU.mult, op1=ALU.mult).then_inc(s_fin, 1)

        @block.tensor
        def _(pe):
            pe.wait_ge(s_const, 1)

            def transpose_rows(name, c):
                n = ROWS[c]
                xv = XS[0:n, c % 2, :].rearrange("t (p k) -> t k p", k=KD)
                for j in range(2):
                    ps = claim(pe, (name, c, j))
                    for k in range(4):
                        ins = pe.transpose(ps[:, k * P:k * P + n], xv[:, 4 * j + k, :], IDENT[0:n, 0:n])
                    written(ins, (name, c, j))

            for i in range(NT):
                pe.wait_ge(s_xs, i + 1)
                transpose_rows("xt", i)
                bank, use = ROT[("xt", i, 1)]
                pe.wait_ge(s_written[bank], use + 1)
                pe.sem_inc(s_xst, 1)
            pe.wait_ge(s_par, 16 * 9)
            ps = claim(pe, ("par", 0))
            written(pe.transpose(ps[:, 0:NPAR], PROW[:], IDENT[0:NPAR, 0:NPAR]), ("par", 0))
            ps = claim(pe, ("par", 1))
            written(pe.transpose(ps[:, 0:NS * 3 * NH], CROW[:], IDENT[0:NS * 3 * NH, 0:NS * 3 * NH]), ("par", 1))
            await_read(pe, ("xt", NT - 1, 1))

            def project(name, j, m):
                for hf in range(2):
                    ps = claim(pe, (name, m, hf))
                    for k in range(KD):
                        ins = pe.matmul(ps[:, 0:HALF], WC[:, j % 2, k, m * P:(m + 1) * P],
                                        XNT[:, k, hf * HALF:(hf + 1) * HALF], start=(k == 0), stop=(k == KD - 1))
                    written(ins, (name, m, hf))

            def chunk(j):
                pe.wait_ge(s_wc[j % 2], 16 * (j // 2 + 1))

            def chunk_done(name):
                b, u = ROT[name]
                pe.wait_ge(s_written[b], u + 1)
                pe.sem_inc(s_wc_free, 1)

            for j, name in ((0, "xr"), (1, "fx")):
                chunk(j)
                for m in range(NH):
                    project(name, j, m)
                chunk_done((name, NH - 1, 1))
            chunk(2)
            pe.wait_ge(s_bd, 16 * 4)
            for m in range(NH):
                project("q", 2, m)
                if m == 0:
                    pe.wait_ge(s_conv, 16 + 8)
                for name, w in (("gx", BDX), ("ga", BDA)):
                    for hf in range(2):
                        ps = claim(pe, (name, m, hf))
                        written(pe.matmul(ps[:, 0:HALF], w[:, m, :], XCt[:, m, hf * HALF:(hf + 1) * HALF],
                                          start=True, stop=True), (name, m, hf))
            chunk_done(("q", NH - 1, 1))
            chunk(3)
            for c in range(NT):
                ps = claim(pe, ("v", c))
                for k in range(KD):
                    ins = pe.matmul(ps[0:ROWS[c], :], XNT[:, k, c * P:c * P + ROWS[c]], WC[:, 1, k, :],
                                    start=(k == 0), stop=(k == KD - 1))
                written(ins, ("v", c))
            chunk_done(("v", NT - 1))
            ps = claim(pe, ("xtail",))
            for m in range(NH):
                ins = pe.transpose(ps[0:11, m * P:(m + 1) * P], XRt[:, m, SEQ:TOK + 3], IDENT[:])
            written(ins, ("xtail",))

            def head_scores(h):
                t = T[:, h % 2]
                pe.wait_ge(s_qk, 8 * (h + 1))
                if h >= 1:
                    pe.wait_ge(s_sc, 4 * h)
                for c in range(CH):
                    at = c * P
                    pe.matmul(PS[B_SD][:, at:at + P], t[:, 2, at:at + P], t[:, 4, at:at + P], start=True, stop=True)
                for c in range(CH):
                    at = c * P
                    for j, s0, n in ((0, 0, 64), (1, 0, 32), (1, 64, 32)):
                        ins = pe.matmul(PS[B_SL][s0:s0 + n, at + s0 + n:at + s0 + 2 * n], t[:, j, at + s0:at + s0 + n],
                                        t[:, j, at + s0 + n:at + s0 + 2 * n], start=True, stop=True,
                                        tile_position=(0, s0), skip_group_check=True)
                ins.then_inc(s_scores, 1)
                if h >= 1:
                    pe.wait_ge(s_s, CH * h)
                for c in range(CH):
                    ins = pe.transpose(PS[B_KV][:, c * P:(c + 1) * P], t[:, 3, c * P:(c + 1) * P], IDENT[:])
                ins.then_inc(s_kt_ps, 1)

            def head_kv(h):
                pe.wait_ge(s_kt, h + 1)
                for c in range(CH):
                    ins = pe.matmul(PS[B_KV][:, c * P:(c + 1) * P], KT[:, c, :], Vt[:, c, h * P:(h + 1) * P], start=True, stop=True)
                ins.then_inc(s_kv, 1)

            def head_o(h):
                pe.wait_ge(s_sc, 4 * (h + 1))
                pe.wait_ge(s_s, CH * (h + 1))
                if h >= 1:
                    pe.wait_ge(s_yn, h)
                for c in range(CH):
                    o = PS[B_O][:, c * P:(c + 1) * P]
                    ins = pe.matmul(o, Vt[:, c, h * P:(h + 1) * P], SC[:, h % 2, c, :], start=True, stop=(c == 0))
                    if c > 0:
                        ins = pe.matmul(o, S[:, h % 2, c - 1, :], T[:, h % 2, 5, c * P:(c + 1) * P], start=False, stop=True)
                ins.then_inc(s_o, 1)

            def head_mean(h):
                ps = claim(pe, ("mean", h))
                pe.wait_ge(s_osq, h + 1)
                written(pe.matmul(ps[:, :], MEAN128[:], NB, start=True, stop=True), ("mean", h))

            def sample_o(b):
                pe.wait_ge(s_sst, b + 1)
                for h in range(NH):
                    at = h * NS + b
                    ins = pe.matmul(PS[B_OS][:, at:at + 1], SST[:, b % 2, h * P:(h + 1) * P], Qt[:, h, SEQ + b:SEQ + b + 1],
                                    start=True, stop=True)
                ins.then_inc(s_osw, 1)

            pe.wait_ge(s_const, 2)
            for s in range(8):
                h = s // 2
                if s % 4 == 0:
                    chunk(4 + s // 4)
                name = "gr" if s < 4 else "g"
                project(name, 4 + s // 4, s % 4)
                if s % 2 == 0:
                    head_scores(h)
                    if h >= 1:
                        head_o(h - 1)
                else:
                    head_kv(h)
                    if s >= 3:
                        head_mean((s - 3) // 2)
                if s >= 1:
                    sample_o(s - 1)
                ps = claim(pe, ("vb", s))
                written(pe.matmul(ps[:, :], IDENT[0:NS, s:s + 1].to_broadcast([NS, P]), Vs[:], start=True, stop=True), ("vb", s))
                if s % 4 == 3:
                    chunk_done((name, NH - 1, 1))
            head_o(NH - 1)
            sample_o(NS - 1)
            head_mean(NH - 1)
            ps = claim(pe, ("mean", 4))
            pe.wait_ge(s_oss, 2)
            written(pe.matmul(ps[:, 0:NH * NS], MEAN128[:], OSB[:], start=True, stop=True), ("mean", 4))
            ps = claim(pe, ("htail",))
            pe.wait_ge(s_h, NH + 1)
            for m in range(NH):
                ins = pe.transpose(ps[0:9, m * P:(m + 1) * P], XCt[:, m, SEQ - 1:TOK], IDENT[:])
            written(ins, ("htail",))

            chunk(6)
            chunk(7)
            pe.wait_ge(s_yb, NH)
            pe.wait_ge(s_y, NH + 1)
            for c in range(NT + 1):
                if c < NT:
                    n = ROWS[c]
                    for half in range(2):
                        ps = claim(pe, ("op", c, half))
                        for j in range(2 * NH):
                            m = (j + NH) % (2 * NH)
                            ins = pe.matmul(ps[0:n, :], GY[:, m, c * P:c * P + n], WC[:, half, m, :],
                                            start=(j == 0), stop=(j == 2 * NH - 1))
                        written(ins, ("op", c, half))
                if c > 0:
                    pe.wait_ge(s_xs, NT + c)
                    transpose_rows("x2t", c - 1)
                    b, u = ROT[("x2t", c - 1, 1)]
                    pe.wait_ge(s_written[b], u + 1)
                    pe.sem_inc(s_xst, 1)
                    n = ROWS[c - 1]
                    ps = claim(pe, ("lg", c - 1))
                    await_read(pe, ("x2t", c - 1, 1))
                    for k in range(KD):
                        ins = pe.matmul(ps[0:n, 0:GROUPS + NE], XNT[:, k, (c - 1) * P:(c - 1) * P + n], WR[:, k, :],
                                        start=(k == 0), stop=(k == KD - 1))
                    written(ins, ("lg", c - 1))

            ps = claim(pe, ("pos",))
            pe.wait_ge(s_oh, 1)
            for lhs, src, first in ((LTRI, CHO, True), (ONES, CUM, False)):
                ins = pe.matmul(ps[:, 0:(NT + 1) * NE], lhs[:], src[:, :, :].rearrange("p i e -> p (i e)"), start=first, stop=not first)
            written(ins, ("pos",))
            pe.wait_ge(s_rnd, 1)
            rounds = pe.value_load(NRND[0:1, 0:1], min_val=1, max_val=MAX_ROUNDS)

            def turn(n, p, use):
                pe.wait_ge(s_xg[p], 16 * (use + 1))
                pe.wait_ge(s_xgt, 2 * n + 1)
                xv = XG[p].rearrange("t (p k) -> t k p", k=KD)
                for k in range(KD):
                    ins = pe.transpose(PS[k // 4][:, (k % 4) * P:(k % 4 + 1) * P], xv[:, k, :], IDENT[:])
                ins.then_inc(s_tw, 1)

            def up(n, p, use):
                pe.wait_ge(s_xgt, 2 * n + 3)
                for two in range(2):
                    pe.wait_ge(s_w13[2 * p + two], 32 * (use + 1))
                    at = two * CAP
                    for k in range(KD):
                        ins = pe.matmul(PS[2 + p][at:at + CAP, :], XGT[p][:, k, at:at + CAP], W13[2 * p + two][:, k, :],
                                        start=(k == 0), stop=(k == KD - 1), tile_position=(0, at))
                    ins.then_inc(s_hw, 1)

            def turn_h(n, p):
                pe.wait_ge(s_hg, n + 1)
                pe.wait_ge(s_ht, n + 1)
                hv = HG[p].rearrange("t (p j) -> t j p", j=2)
                for j in range(2):
                    ins = pe.transpose(PS[4][:, j * P:(j + 1) * P], hv[:, j, :], IDENT[:])
                ins.then_inc(s_htw, 1)

            def down(n, p, use):
                pe.wait_ge(s_ht, n + 2)
                pe.wait_ge(s_ya, n + 1)
                pe.wait_ge(s_yd, n + 1)
                for two in range(2):
                    pe.wait_ge(s_w2[2 * p + two], 16 * (use + 1))
                    at = two * CAP
                    for half in range(2):
                        for j in range(2):
                            ins = pe.matmul(PS[5 + half][at:at + CAP, :], HT[p][:, j, at:at + CAP],
                                            W2[2 * p + two][:, j, half * 512:(half + 1) * 512],
                                            start=(j == 0), stop=(j == 1), tile_position=(0, at))
                    ins.then_inc(s_yw, 1)

            pe.sem_inc(s_pmu, 1)
            with pe.Fori(0, rounds) as r:
                base = r * NPAIR
                for j in range(2 * NT):
                    i, k = j // 2, j % 2
                    pe.wait_ge(s_pm, r * (2 * NT) + j + 1)
                    ins = pe.matmul(PS[B_O][:, 0:NE], PM[0:ROWS[i], j % NPM, :], OHV[0:ROWS[i], k, i, :],
                                    start=(j == 0), stop=(j == 2 * NT - 1))
                    if j < 2 * NT - 1:
                        ins.then_inc(s_pmu, 1)
                ins.then_inc(s_tab, 1)
                pe.wait_ge(s_tab, r + 1)
                pe.sem_inc(s_pmu, 1)
                half_n = r * (NPAIR // 2)
                turn(base, 0, half_n)
                turn(base + 1, 1, half_n)
                up(base, 0, half_n)
                turn_h(base, 0)
                with pe.Fori(0, NPAIR // 2 - 1) as i:
                    for j in range(2):
                        q = base + i * 2 + 1 + j
                        p = 1 - j
                        turn(q + 1, 1 - p, half_n + i + 1)
                        up(q, p, half_n + i + j)
                        down(q - 1, 1 - p, half_n + i)
                        turn_h(q, p)
                q = base + NPAIR - 1
                up(q, 1, half_n + NPAIR // 2 - 1)
                down(q - 1, 0, half_n + NPAIR // 2 - 1)
                turn_h(q, 1)
                down(q, 1, half_n + NPAIR // 2 - 1)


_INS = ["x_prompt", "x_sample", "state_hgrn", "state_rglru", "state_conv", "lower_bounds", "ln1_g", "w_in",
        "hgrn_norm_g", "conv_w", "conv_b", "lru_wx", "lru_bx", "lru_wa", "lru_ba", "lru_lambda", "w_out", "ln2_g",
        "router_wg", "router_bg", "router_we", "router_be", "exp_w1", "exp_w3", "exp_w2", "final_g"]
_OUTS = [(1, SEQ, D), (NS, 1, D), (1, 1, NH, P, P), (1, 1, 512), (1, 1, 3, 512),
         (1, NS, NH, P, P), (1, NS, 512), (1, NS, 3, 512)]


def kernel(**inputs):
    import numpy as _np
    import concourse.bacc as _bacc
    from concourse.bass_utils import run_bass_kernel_spmd as _run

    nc = _bacc.Bacc("TRN2", target_bir_lowering=False, num_devices=1)
    arrays, args = {}, []
    for name in _INS:
        a = _np.ascontiguousarray(inputs[name])
        arrays[f"in_{name}"] = a
        args.append(nc.dram_tensor(f"in_{name}", a.shape, F32, kind="ExternalInput").ap())
    for i, shape in enumerate(_OUTS):
        args.append(nc.dram_tensor(f"out_{i}", shape, F32, kind="ExternalOutput").ap())
    build(nc, *args)
    r = _run(nc, [arrays], core_ids=[0])
    return tuple(r.results[0][f"out_{i}"] for i in range(len(_OUTS)))
```

```python
from contextlib import ExitStack
from math import pi, sqrt

import concourse.bass as bass
from concourse import mybir

F32 = mybir.dt.float32
I32 = mybir.dt.int32
U32 = mybir.dt.uint32
ALU = mybir.AluOpType
ACT = mybir.ActivationFunctionType
AX_X = mybir.AxisListType.X

P = 128
D = 1024
SEQ, NS = 512, 8
TOK = SEQ + NS
HALF = TOK // 2
KD = D // P
NH = 4
CH = SEQ // P
NT = CH + 1
ROWS = [P] * CH + [NS]
TILE_ORDER = [0, CH] + list(range(1, CH))
GROUPS, PER_GROUP = 4, 8
NE = GROUPS * PER_GROUP
FE = 256
CAP = 64
NPAIR = NE // 2
MAX_ROUNDS = -(-TOK // CAP)
POOL_TILES = (0, 1, 2)
KEPT = NE - 3
NPM = 4
NR = 3
BIG = 4096
EPS = 1e-6
SUB = 32

LB, HGG, CW, CB, BX, BA, LAM, H0 = 0, 8, 12, 28, 32, 36, 40, 44
NPAR = H0 + NS * NH
V_FA, V_FB, V_NFB, V_C, V_NC, V_BX, V_BA, V_HG, V_T0, V_T1, V_T2, V_T3 = range(0, 48, 4)

XR, FX, Q, V, GR, G = 4, 1, 0, 2, 5, 3
ORDER = [XR, FX, Q, V, GR, G]


def rotation():
    r = []
    for i in range(NT):
        r += [("xt", i, 0), ("xt", i, 1)]
    for name in ("xr", "fx"):
        for m in range(NH):
            r += [(name, m, 0), (name, m, 1)]
            if (name, m) == ("xr", 0):
                r += [("par", 0), ("par", 1)]
    for m in range(NH):
        r += [("q", m, 0), ("q", m, 1)]
        r += [(g, m, h) for g in ("gx", "ga") for h in range(2)]
    r += [("v", c) for c in TILE_ORDER]
    r += [("xtail",)]
    for s in range(8):
        r += [("gr" if s < 4 else "g", s % 4, 0), ("gr" if s < 4 else "g", s % 4, 1)]
        if s % 2 and s >= 3:
            r += [("mean", (s - 3) // 2)]
        if s == 6:
            r += [("ost", 0)]
    r += [("mean", 3), ("ost", 1), ("mean", 4), ("htail",)]
    for i in range(NT + 2):
        if i > 1:
            r += [("lg", i - 2)]
        if 1 <= i <= NT:
            r += [("x2t", i - 1, 0), ("x2t", i - 1, 1)]
    r += [("pos",)]
    return {name: (n % NR, n // NR) for n, name in enumerate(r)}


ROT = rotation()


def build(nc, x_prompt, x_sample, state_hgrn, state_rglru, state_conv, lower_bounds, ln1_g, w_in,
          hgrn_norm_g, conv_w, conv_b, lru_wx, lru_bx, lru_wa, lru_ba, lru_lambda, w_out, ln2_g,
          router_wg, router_bg, router_we, router_be, exp_w1, exp_w3, exp_w2, final_g,
          y_prompt, y_sample, hgrn_p, rglru_p, conv_p, hgrn_s, rglru_s, conv_s):
    xn_dram = nc.dram_tensor("xn_rows", (TOK, D), F32).ap()
    vs_dram = nc.dram_tensor("sample_v", (NS, 512), F32).ap()
    ye_dram = nc.dram_tensor("expert_rows", (2 * TOK, D), F32).ap()

    def x_rows(i):
        return x_prompt[0, i * P:(i + 1) * P, :] if i < CH else x_sample.rearrange("b s d -> (b s) d")

    def y_rows(i):
        return y_prompt[0, i * P:(i + 1) * P, :] if i < CH else y_sample.rearrange("b s d -> (b s) d")

    with ExitStack() as ctx:
        def sb(name, shape, dt=F32):
            return ctx.enter_context(nc.sbuf_tensor(name, shape, dt))

        def sem(name):
            return ctx.enter_context(nc.semaphore(name))

        X = sb("X", [P, NT, D])
        XS = sb("XS", [P, 2, D])
        XNT = sb("XNT", [P, KD, TOK])
        WC = sb("WC", [P, 2, KD, 512])
        SLOT0 = sb("SLOT0", [P, 6144])
        GXt = SLOT0[:, 0:NH * TOK].rearrange("p (m t) -> p m t", m=NH)
        GAt = SLOT0[:, NH * TOK:2 * NH * TOK].rearrange("p (m t) -> p m t", m=NH)
        XRC = sb("XRC", [P, NH * (2 * TOK + 3)])
        XRt = XRC[:, 0:NH * (TOK + 3)].rearrange("p (m t) -> p m t", m=NH)
        XCt = XRC[:, NH * (TOK + 3):].rearrange("p (m t) -> p m t", m=NH)
        SLOT1 = sb("SLOT1", [P, 3 * NH * TOK])
        Ft = SLOT1[:, 0:NH * TOK].rearrange("p (m t) -> p m t", m=NH)
        Kt = SLOT1[:, NH * TOK:2 * NH * TOK].rearrange("p (m t) -> p m t", m=NH)
        Qt = SLOT1[:, 2 * NH * TOK:3 * NH * TOK].rearrange("p (m t) -> p m t", m=NH)
        GY = sb("GY", [P, 2 * NH, TOK])
        Vt = sb("Vt", [P, CH, 512])
        Vs = sb("Vs", [NS, 512])
        T = sb("T", [P, 2, 6, 512])
        TN = T[:, 1, 0:5, :].rearrange("p a t -> p (a t)")[:, 0:NH * TOK].rearrange("p (m t) -> p m t", m=NH)
        A2 = T[:, 0, 0:5, :].rearrange("p a t -> p (a t)")[:, 0:NH * TOK].rearrange("p (m t) -> p m t", m=NH)
        SC = SLOT0[:, 0:1024].rearrange("p (a c t) -> p a c t", a=2, c=CH)
        S = SLOT0[:, 1024:2048].rearrange("p (a c t) -> p a c t", a=2, c=CH)
        KT = SLOT0[:, 2048:2560].rearrange("p (c t) -> p c t", c=CH)
        NB = SLOT0[:, 2560:3072]
        SST = XS[:, 1, :].rearrange("p (a t) -> p a t", a=2)
        VB = XS[:, 0, :].rearrange("p (a t) -> p a t", a=2)
        OX = SLOT0[:, 3072:3584]
        QS = sb("QS", [P, NH * NS])
        OS = sb("OS", [P, NH * NS])
        OSB = sb("OSB", [P, NH * NS])
        AC = sb("AC", [P, NH, CH])
        PROW = sb("PROW", [NPAR, P])
        CROW = sb("CROW", [NS * 3 * NH, P])
        PARAM = sb("PARAM", [P, NPAR])
        CVT = sb("CVT", [P, NS * 3 * NH])
        VEC = sb("VEC", [P, 48])
        G1 = sb("G1", [P, KD])
        G2 = sb("G2", [P, KD])
        BDX = sb("BDX", [P, NH, P])
        BDA = sb("BDA", [P, NH, P])
        TAIL = BDX[0:11, :, :].rearrange("p m t -> p (m t)")
        HTAIL = BDA[0:9, :, :].rearrange("p m t -> p (m t)")
        SSQ = sb("SSQ", [P, NT])
        RSTD = sb("RSTD", [P, NT])
        EPSC = sb("EPSC", [P, 1])
        UNUSED = sb("UNUSED", [P, 1])
        IDENT = sb("IDENT", [P, P])
        MEAN128 = sb("MEAN128", [P, P])
        ONES = sb("ONES", [P, P])
        LTRI = sb("LTRI", [P, P])
        CMASK = sb("CMASK", [P, P])
        RESET = sb("RESET", [P, CH, P])
        SCR = sb("SCR", [P, 8, NS])
        V_FLAT = Vt[:, :, :].rearrange("p c t -> p (c t)")
        used = [0]

        def over_v(shape):
            n = 1
            for x in shape[1:]:
                n *= x
            v = V_FLAT[:, used[0]:used[0] + n]
            used[0] += n
            if len(shape) == 3:
                return v.rearrange("p (a b) -> p a b", a=shape[1])
            return v.rearrange("p (k a b) -> p k a b", k=shape[1], a=shape[2])

        WGt = sb("WGt", [P, KD * GROUPS])
        WEt = sb("WEt", [P, GROUPS, KD * PER_GROUP])
        WR = sb("WR", [P, KD, GROUPS + NE])
        RB = sb("RB", [P, GROUPS + NE])
        LG = over_v([P, NT, GROUPS + NE])
        L8 = over_v([P, NT, 8])
        TOP = over_v([P, NT, 8])
        TIX = sb("TIX", [P, NT, 8], U32)
        GIX = sb("GIX", [P, NT])
        GEX = over_v([P, NT, GROUPS])
        PTOP = sb("PTOP", [P, NT])
        LSEL = over_v([P, NT, NE])
        LMSK = over_v([P, 1, NE])
        CHO = over_v([P, NT + 1, NE])
        CUM = over_v([P, NT + 1, NE])
        EIX = sb("EIX", [P, NT, 2])
        OH = over_v([P, 2, NT, NE])
        OHV = over_v([P, 2, NT, NE])
        RANK = sb("RANK", [P, 2, NT])
        WK = sb("WK", [P, 2, NT])
        CNT = sb("CNT", [P, 2])
        NRND = sb("NRND", [P, 1], I32)
        IOI = SLOT1[:, 2 * NH * TOK:2 * NH * TOK + 2 * NE + CAP + 2 * NT].bitcast(I32)
        IOF = sb("IOF", [P, NE + NE + CAP + 2 * NT])
        iota_e, iota_g = IOF[:, 0:NE], IOF[:, NE:2 * NE]
        iota_s = IOF[:, 2 * NE:2 * NE + CAP]
        token_code = IOF[:, 2 * NE + CAP:].rearrange("p (i k) -> p k i", k=2)
        PM = over_v([P, NPM, CAP])
        DSTI = sb("DSTI", [P, NPAIR], I32)
        SRCI = sb("SRCI", [P, NPAIR], I32)
        GIDX = sb("GIDX", [P, 2, 1], I32)
        SIDX = sb("SIDX", [P, 2, 1], I32)
        SQUARES = [T[:, j, 0:2, :].rearrange("p a t -> p (a t)") for j in range(2)]
        XG = [T[:, j, 0:2, :].rearrange("p a t -> p (a t)") for j in range(2)]
        YO = [T[:, j, 2:4, :].rearrange("p a t -> p (a t)") for j in range(2)]
        XGT = [XRC[:, 1024 * j:1024 * (j + 1)].rearrange("p (k t) -> p k t", k=KD) for j in range(2)]
        HS = [XRC[:, 2048 + FE * j:2048 + FE * (j + 1)] for j in range(2)]
        HG = [XRC[:, 2560 + FE * j:2560 + FE * (j + 1)] for j in range(2)]
        HT = [XRC[:, 3072 + FE * j:3072 + FE * (j + 1)].rearrange("p (j t) -> p j t", j=2) for j in range(2)]
        GYF = GY[:, :, :].rearrange("p m t -> p (m t)")
        WCF = WC[:, :, :, :].rearrange("p a k t -> p (a k t)")
        W13 = [s[:, 0:4096].rearrange("p (k f) -> p k f", k=KD) for s in (SLOT0, SLOT1, WCF, GYF)]
        W2 = [s.rearrange("p (j d) -> p j d", j=2)
              for s in (SLOT0[:, 4096:6144], SLOT1[:, 4096:6144], WCF[:, 4096:6144], WCF[:, 6144:8192])]
        XNF = XNT[:, :, :].rearrange("p k t -> p (k t)")
        YE = [b.rearrange("p (k d) -> p k d", k=2) for b in
              (XNF[:, 0:2048], XNF[:, 2048:4096], SLOT0[:, 0:2048], SLOT0[:, 2048:4096], SLOT0[:, 4096:6144])]
        OUT = [SLOT1[:, D * c:D * (c + 1)] for c in range(NT)]
        W13_KEPT = XNF[:, 0:4096].rearrange("p (k f) -> p k f", k=KD)
        W2_KEPT = XS[:, :, :]
        FGB = T[:, 0, 4:6, :].rearrange("p a t -> p (a t)")

        PS = [ctx.enter_context(nc.psum_tensor(f"ps{b}", [P, 512], F32)) for b in range(8)]
        B_OS, B_SD, B_SL, B_KV, B_O = 3, 4, 5, 6, 7
        OP = [(PS[B_SD], PS[B_SL]), (PS[B_KV], PS[B_O])]

        s_x = [sem(f"x_in{i}") for i in range(NT)]
        s_wc = [sem(f"wc_in{i}") for i in range(2)]
        s_wc_free = sem("wc_free")
        s_par = sem("param_rows_in")
        s_gain = [sem(f"gain{i}_in") for i in (1, 2)]
        s_bd = sem("gate_weights_in")
        s_rt = sem("router_weights_in")
        s_written = [sem(f"rot_written{i}") for i in range(NR)]
        s_read = [sem(f"rot_read{i}") for i in range(NR)]
        s_const = sem("constants_made")
        s_init = sem("scratch_initialised")
        s_pool = sem("pool_step")
        s_zero = sem("zeroed")
        s_zero_sc = sem("scores_zeroed")
        s_ssq = sem("squares_summed")
        s_root = sem("root_ready")
        s_unused = sem("table_loaded")
        s_rstd = sem("rstd_ready")
        s_xs = sem("rows_scaled")
        s_xst = sem("rows_transposed")
        s_param = sem("param_ready")
        s_vec = sem("vec_step")
        s_vexp = sem("vec_exp")
        s_conv = sem("conv_step")
        s_f = sem("f_ready")
        s_gt = sem("gate_tanh_ready")
        s_a = sem("decay_a_ready")
        s_m2 = sem("mult_squared_ready")
        s_mu = sem("mult_ready")
        s_vs = sem("sample_v_step")
        s_u = sem("u_step")
        s_h = sem("h_ready")
        s_k = sem("k_ready")
        s_lf = sem("logf_ready")
        s_b = sem("cumulated_ready")
        s_d = sem("exponents_ready")
        s_e = sem("decays_ready")
        s_ac = sem("chunk_decay_ready")
        s_qk = sem("decayed_qk_ready")
        s_scores = sem("scores_written")
        s_kt_ps = sem("kt_written")
        s_kt = sem("kt_ready")
        s_sc = sem("scores_ready")
        s_kv = sem("kv_written")
        s_s = sem("states_ready")
        s_o = sem("o_written")
        s_osq = sem("o_squared")
        s_rs = sem("head_rstd_step")
        s_yn = sem("y_normed")
        s_gel = sem("gelu_step")
        s_gela = sem("gelu_act")
        s_yb = sem("y_b_ready")
        s_tg = sem("g_tanh_ready")
        s_sg = sem("silu_ready")
        s_y = sem("y_a_ready")
        s_skv = sem("sample_kv_step")
        s_sst = sem("sample_state_ready")
        s_sin = [sem(f"sample_state_in{i}") for i in range(2)]
        s_sout = [sem(f"sample_state_out{i}") for i in range(2)]
        s_vsd = sem("sample_v_in_dram")
        s_vb = [sem(f"sample_v_in{i}") for i in range(2)]
        s_qs = sem("sample_q_ready")
        s_osw = sem("sample_pair_written")
        s_ox = sem("sample_products_copied")
        s_oss = sem("sample_o_step")
        s_tail = sem("tails_ready")
        s_small_out = sem("small_outputs_written")
        s_hp = sem("hgrn_state_written")
        s_op = sem("out_product_written")
        s_opr = sem("out_product_read")
        s_xn = [sem(f"xn_rows_written{i}") for i in range(2)]
        s_r = sem("router_step")
        s_rexp = sem("router_exp")
        s_oh = sem("onehots_ready")
        s_rnd = sem("rounds_known")
        s_pm = sem("slot_onehot_ready")
        s_pmu = sem("slot_onehot_used")
        s_tab = sem("table_written")
        s_tabr = sem("table_ready")
        s_tabs = sem("table_step")
        s_turn = sem("pool_turns")
        s_gi = sem("gather_index_copied")
        s_si = sem("scatter_index_copied")
        s_xg = [sem(f"rows_gathered{i}") for i in range(2)]
        s_ys = [sem(f"rows_scattered{i}") for i in range(2)]
        s_w13 = [sem(f"w13_in{i}") for i in range(5)]
        s_w2 = [sem(f"w2_in{i}") for i in range(5)]
        s_tw = sem("xg_transposed")
        s_xgt = sem("xgt_ready")
        s_hw = sem("h_written")
        s_silu = sem("silu_done")
        s_hg = sem("h_gated")
        s_htw = sem("h_transposed")
        s_ht = sem("ht_ready")
        s_yw = sem("y_written")
        s_ya = sem("y_half_a_read")
        s_yd = sem("y_half_b_read")
        s_rdone = sem("round_done")
        s_fg = sem("final_gain_in")
        s_ye = [sem(f"expert_rows_in{i}") for i in range(NT)]
        s_cmb = sem("combine_step")
        s_fr = sem("final_squares_summed")
        s_froot = sem("final_root_ready")
        s_frstd = sem("final_rstd_ready")
        s_fscaled = sem("final_rows_scaled")
        s_fin = [sem(f"final_ready{i}") for i in range(NT)]
        s_out = sem("y_out")

        def claim(pe, name):
            bank, use = ROT[name]
            if use > 0:
                pe.wait_ge(s_read[bank], use)
            return PS[bank]

        def written(ins, name):
            ins.then_inc(s_written[ROT[name][0]], 1)

        def await_ps(eng, name):
            bank, use = ROT[name]
            eng.wait_ge(s_written[bank], use + 1)
            return PS[bank]

        def read(ins, name):
            ins.then_inc(s_read[ROT[name][0]], 1)

        def await_read(eng, name):
            eng.wait_ge(s_read[ROT[name][0]], ROT[name][1] + 1)

        def bc(ap, axis, n):
            ap = ap.unsqueeze(axis)
            shape = list(ap.shape)
            shape[axis] = n
            return ap.to_broadcast(shape)

        def col(v, m):
            return VEC[:, v + m:v + m + 1]

        def load_w2(eng, e, slot):
            eng.dma_start(W2[slot], exp_w2[0, e].rearrange("(p j) d -> p j d", j=2)).then_inc(s_w2[slot], 16)

        def weights_of(p, two, kept):
            if kept and two:
                return W13_KEPT, W2_KEPT, 4
            return W13[2 * p + two], W2[2 * p + two], 2 * p + two

        def loads(slot, r, n):
            if slot == 4:
                return 1
            return r * (NPAIR // 2 - (slot == KEPT % 4)) + n

        block = ctx.enter_context(nc.Block())

        @block.sync
        def _(sp):
            sp.dma_start(X[:, 0, :], x_rows(0)).then_inc(s_x[0], 16)
            for i in range(1, NT):
                sp.dma_start(X[0:ROWS[i], i, :], x_rows(i)).then_inc(s_x[i], 16)
            w_in_v = w_in[0].rearrange("(p k) n -> p k n", k=KD)
            w_out_v = w_out[0].rearrange("(m p) n -> p m n", p=P)
            sp.dma_start(G1[:], ln1_g[0].rearrange("(p k) -> p k", k=KD)).then_inc(s_gain[0], 16)
            rows = [(lower_bounds, LB, 8), (hgrn_norm_g, HGG, 4), (conv_w[0], CW, 16), (conv_b, CB, 4), (lru_bx, BX, 4),
                    (lru_ba, BA, 4), (lru_lambda, LAM, 4), (state_rglru[0], H0, NS * NH)]
            for j in range(8):
                if j >= 2:
                    sp.wait_ge(s_wc_free, j - 1)
                src = w_in_v[:, :, ORDER[j] * 512:(ORDER[j] + 1) * 512] if j < 6 else w_out_v[:, :, (j - 6) * 512:(j - 5) * 512]
                sp.dma_start(WC[:, j % 2, :, :], src).then_inc(s_wc[j % 2], 16)
                if j == 0:
                    for src, at, n in rows:
                        sp.dma_start(PROW[at:at + n, :], src.rearrange("a (m p) -> (a m) p", p=P)).then_inc(s_par, 16)
                    sp.dma_start(CROW[:], state_conv[0].rearrange("b w (m p) -> (b w m) p", p=P)).then_inc(s_par, 16)
                if j == 1:
                    sp.dma_start(G2[:], ln2_g[0].rearrange("(p k) -> p k", k=KD)).then_inc(s_gain[1], 16)
                    sp.dma_start(WGt[:], router_wg[0].rearrange("(p k) g -> p (k g)", k=KD)).then_inc(s_rt, 16)
                    sp.dma_start(WEt[:], router_we[0].rearrange("g (p k) e -> p g (k e)", k=KD)).then_inc(s_rt, 16)
                    sp.dma_start(RB[:, 0:GROUPS], router_bg[0:1, :].to_broadcast([P, GROUPS])).then_inc(s_rt, 16)
                    sp.dma_start(RB[:, GROUPS:], router_be.rearrange("a g e -> a (g e)").to_broadcast([P, NE])).then_inc(s_rt, 16)

            def load_w13(e, slot, w13=None):
                w13 = W13[slot] if w13 is None else w13
                for half, w in enumerate((exp_w1, exp_w3)):
                    sp.dma_start(w13[:, :, half * FE:(half + 1) * FE],
                                 w[0, e].rearrange("(p k) f -> p k f", k=KD)).then_inc(s_w13[slot], 16)

            sp.wait_ge(s_y, NH + 1)
            sp.wait_ge(s_hp, 16 * NH)
            for e in range(2):
                load_w13(e, e)
                load_w2(sp, e, e)

            for i, c in enumerate(TILE_ORDER):
                sp.wait_ge(s_xs, NT + i + 1)
                sp.dma_start(xn_dram[c * P:c * P + ROWS[c], :], XS[0:ROWS[c], i % 2, :]).then_inc(s_xn[i % 2], 16)
            sp.dma_start(FGB, final_g.rearrange("(a d) -> a d", a=1).partition_broadcast(P)).then_inc(s_fg, 16)

            sp.wait_ge(s_opr, 2 * NT)
            for e in range(2, 4):
                load_w13(e, e)
                load_w2(sp, e, e)
            await_read(sp, ("lg", NT - 1))
            for i in range(2):
                sp.wait_ge(s_xg[i], 16)
            load_w13(KEPT, 4, W13_KEPT)
            for i in range(2):
                sp.wait_ge(s_xn[i], 16 * ((NT + 1 - i) // 2))
            sp.dma_start(W2_KEPT, exp_w2[0, KEPT].rearrange("(p j) d -> p j d", j=2)).then_inc(s_w2[4], 16)

            sp.wait_ge(s_rnd, 1)
            rounds = sp.value_load(NRND[0:1, 0:1], min_val=1, max_val=MAX_ROUNDS)
            with sp.Fori(0, rounds) as r:
                with sp.If(r > 0):
                    sp.wait_ge(s_yw, r * NE)
                    for e in range(4):
                        load_w13(e, e)
                        load_w2(sp, e, e)
                with sp.Fori(0, NE // 4 - 2) as i:
                    for slot in range(4):
                        sp.wait_ge(s_hw, r * NE + i * 4 + slot + 1)
                        load_w13(i * 4 + slot + 4, slot)
                for slot in range(4):
                    if NE - 4 + slot != KEPT:
                        sp.wait_ge(s_hw, r * NE + NE - 8 + slot + 1)
                        load_w13(NE - 4 + slot, slot)

            sp.wait_ge(s_rdone, rounds + 1)
            ye_v = ye_dram.rearrange("(t k) d -> t k d", k=2)
            for c in range(NT):
                sp.dma_start(YE[c][0:ROWS[c]], ye_v[c * P:c * P + ROWS[c]]).then_inc(s_ye[c], 16)
            for c in range(NT):
                sp.wait_ge(s_fin[c], 1)
                sp.dma_start(y_rows(c), OUT[c][0:ROWS[c]]).then_inc(s_out, 16)
            sp.wait_ge(s_out, 16 * NT)

        @block.gpsimd
        def _(pool):
            step = [0]

            def chain(ins):
                step[0] += 1
                ins.then_inc(s_pool, 1)
                pool.wait_ge(s_pool, step[0])

            chain(pool.memset(IDENT[:], 0.0))
            pool.affine_select(out=IDENT[:], in_=IDENT[:], compare_op=ALU.not_equal, fill=1.0, base=0,
                               pattern=[[-1, P]], channel_multiplier=1).then_inc(s_const, 1)
            chain(pool.memset(BDX[:], 0.0))
            chain(pool.memset(BDA[:], 0.0))
            for bd, w in ((BDX, lru_wx), (BDA, lru_wa)):
                wv = w[0].rearrange("(m two) c d -> two c m d", two=2)
                for two in range(2):
                    pool.dma_start(bd[64 * two:64 * two + 64, :, 64 * two:64 * two + 64], wv[two]).then_inc(s_bd, 16)
            st_v = state_hgrn[0].rearrange("b h d e -> b d h e")
            so_v = hgrn_s[0].rearrange("b h d e -> b d h e")

            def load_state(b):
                pool.dma_start(SST[:, b % 2, :].rearrange("p (h e) -> p h e", h=NH), st_v[b]).then_inc(s_sin[b % 2], 16)

            pool.memset(ONES[:], 1.0).then_inc(s_pool, 1)
            pool.memset(MEAN128[:], 1.0 / P).then_inc(s_pool, 1)
            pool.memset(LTRI[:], 1.0).then_inc(s_pool, 1)
            pool.memset(CMASK[:], 1.0).then_inc(s_pool, 1)
            step[0] += 4
            pool.wait_ge(s_pool, step[0])
            chain(pool.affine_select(out=LTRI[:], in_=LTRI[:], compare_op=ALU.is_gt, fill=0.0, base=0,
                                     pattern=[[1, P]], channel_multiplier=-1))
            chain(pool.affine_select(out=CMASK[:], in_=CMASK[:], compare_op=ALU.is_ge, fill=0.0, base=0,
                                     pattern=[[1, P]], channel_multiplier=-1))
            for blk in range(P // SUB):
                part = CMASK[SUB * blk:SUB * (blk + 1), :]
                chain(pool.affine_select(out=part, in_=part, compare_op=ALU.is_ge, fill=0.0, base=SUB * (blk + 1) - 1,
                                         pattern=[[-1, P]], channel_multiplier=0))
            chain(pool.iota(IOI[:, 0:NE], [[1, NE]], base=0, channel_multiplier=0))
            chain(pool.iota(IOI[:, NE:2 * NE], [[1, GROUPS], [0, PER_GROUP]], base=0, channel_multiplier=0))
            chain(pool.iota(IOI[:, 2 * NE:2 * NE + CAP], [[1, CAP]], base=0, channel_multiplier=0))
            pool.iota(IOI[:, 2 * NE + CAP:], [[2 * P, NT], [1, 2]], base=-BIG, channel_multiplier=2).then_inc(s_const, 1)

            pool.wait_ge(s_xst, NT)
            load_state(0)
            load_state(1)

            def load_v(b):
                pool.dma_start(VB[:, b % 2, :], vs_dram[b:b + 1, :].to_broadcast([P, 512])).then_inc(s_vb[b % 2], 16)

            await_read(pool, ("v", CH))
            pool.dma_start(vs_dram, Vs[:]).then_inc(s_vsd, 16)
            pool.wait_ge(s_vsd, 16)
            load_v(0)
            load_v(1)

            pool.dma_start(conv_s[0, :, 0:2, :], state_conv[0, :, 1:3, :]).then_inc(s_small_out, 16)
            pool.wait_ge(s_tail, 1)
            pool.dma_start(conv_p[0, 0], TAIL[0:3, :]).then_inc(s_small_out, 16)
            pool.dma_start(conv_s[0, :, 2, :], TAIL[3:11, :]).then_inc(s_small_out, 16)
            for h in range(NH):
                pair = (2 * h, 2 * h + 1)
                for b in pair:
                    pool.wait_ge(s_sst, b + 1)
                    pool.dma_start(so_v[b], SST[:, b % 2, :].rearrange("p (h e) -> p h e", h=NH)).then_inc(s_sout[b % 2], 16)
                pool.wait_ge(s_s, CH * (h + 1))
                pool.dma_start(hgrn_p[0, 0, h], S[:, h % 2, CH - 1, :]).then_inc(s_hp, 16)
                if h + 1 < NH:
                    for b in pair:
                        load_v(b + 2)
                    pool.wait_ge(s_osw, h + 1)
                    for b in pair:
                        pool.wait_ge(s_sout[b % 2], 16 * (h + 1))
                        load_state(b + 2)
            pool.wait_ge(s_tail, 2)
            pool.dma_start(rglru_p[0], HTAIL[0:1, :]).then_inc(s_ys[0], 16)
            pool.dma_start(rglru_s[0], HTAIL[1:9, :]).then_inc(s_ys[1], 16)

            pool.wait_ge(s_hp, 16 * NH)
            pool.wait_ge(s_y, NH + 1)
            pool.memset(XG[0], 0.0).then_inc(s_zero, 1)
            pool.memset(XG[1], 0.0).then_inc(s_zero, 1)
            pool.wait_ge(s_zero, 2)
            pool.wait_ge(s_xn[0], 16 * 3)
            pool.wait_ge(s_xn[1], 16 * 2)
            pool.wait_ge(s_rnd, 1)
            rounds = pool.value_load(NRND[0:1, 0:1], min_val=1, max_val=MAX_ROUNDS)

            def gather(n, q, p):
                pool.wait_ge(s_tw, n - 1)
                pool.sem_inc(s_turn, 1)
                pool.tensor_copy(GIDX[:, p, :], SRCI[:, q]).then_inc(s_gi, 1)
                pool.wait_ge(s_gi, n + 1)
                pool.sem_inc(s_turn, 1)
                pool.indirect_dma_start(out=XG[p], out_offset=None, in_=xn_dram,
                                        in_offset=bass.IndirectOffsetOnAxis(ap=GIDX[:, p, :].bitcast(U32), axis=0),
                                        bounds_check=TOK - 1, oob_is_err=False).then_inc(s_xg[p], 16)

            def scatter(n, q, p, use):
                pool.wait_ge(s_ys[p], 16 * use + 16)
                pool.sem_inc(s_turn, 1)
                pool.tensor_copy(SIDX[:, p, :], DSTI[:, q]).then_inc(s_si, 1)
                pool.wait_ge(s_si, n + 1)
                pool.wait_ge(s_ya, n + 2)
                pool.wait_ge(s_yd, n + 2)
                pool.sem_inc(s_turn, 1)
                pool.indirect_dma_start(out=ye_dram, out_offset=bass.IndirectOffsetOnAxis(ap=SIDX[:, p, :].bitcast(U32), axis=0),
                                        in_=YO[p], in_offset=None,
                                        bounds_check=2 * TOK - 1, oob_is_err=False).then_inc(s_ys[p], 16)

            pool.sem_inc(s_rdone, 1)
            with pool.Fori(0, rounds) as r:
                base = r * NPAIR
                pool.wait_ge(s_tabr, r + 1)
                pool.sem_inc(s_turn, 1)
                for q in range(2):
                    pool.tensor_copy(GIDX[:, q, :], SRCI[:, q:q + 1]).then_inc(s_gi, 1)
                    pool.wait_ge(s_gi, base + q + 1)
                    pool.sem_inc(s_turn, 1)
                    pool.indirect_dma_start(out=XG[q], out_offset=None, in_=xn_dram,
                                            in_offset=bass.IndirectOffsetOnAxis(ap=GIDX[:, q, :].bitcast(U32), axis=0),
                                            bounds_check=TOK - 1, oob_is_err=False).then_inc(s_xg[q], 16)
                gather(base + 2, slice(2, 3), 0)
                with pool.Fori(0, NPAIR // 2 - 2) as i:
                    for p in range(2):
                        q = i * 2 + p
                        gather(base + q + 3, bass.ds(q + 3, 1), 1 - p)
                        scatter(base + q, bass.ds(q, 1), p, r * (NPAIR // 2) + i)
                gather(base + NPAIR - 1, slice(NPAIR - 1, NPAIR), 1)
                for q in range(NPAIR - 4, NPAIR):
                    scatter(base + q, slice(q, q + 1), q % 2, r * (NPAIR // 2) + q // 2)
                pool.wait_ge(s_ys[0], (r + 1) * (NPAIR // 2 * 16) + 16)
                pool.wait_ge(s_ys[1], (r + 1) * (NPAIR // 2 * 16) + 16)
                pool.sem_inc(s_rdone, 1)
            pool.wait_ge(s_fg, 16)
            for n, c in enumerate(POOL_TILES):
                pool.wait_ge(s_fscaled, n + 1)
                pool.tensor_tensor(OUT[c], OUT[c], FGB, ALU.mult).then_inc(s_fin[c], 1)
            pool.wait_ge(s_small_out, 16 * 3)
            pool.wait_ge(s_sout[0], 16 * 4)
            pool.wait_ge(s_sout[1], 16 * 4)

        @block.scalar
        def _(act):
            act.wait_ge(s_init, 1)
            act.activation(UNUSED[:], EPSC[:], ACT.Sqrt).then_inc(s_unused, 1)
            for i in range(NT + 1):
                if i < NT:
                    n = ROWS[i]
                    act.wait_ge(s_x[i], 16)
                    if i >= 2:
                        act.wait_ge(s_ssq, i - 1)
                    act.activation(SQUARES[i % 2][0:n, :], X[0:n, i, :], ACT.Square, accum_out=SSQ[0:n, i:i + 1]).then_inc(s_ssq, 1)
                    act.wait_ge(s_ssq, i + 1)
                    act.activation(RSTD[0:n, i:i + 1], SSQ[0:n, i:i + 1], ACT.Sqrt, scale=1.0 / D, bias=EPSC[0:n, :]).then_inc(s_root, 1)
                if i >= 1:
                    n = ROWS[i - 1]
                    act.wait_ge(s_rstd, i)
                    if i >= 3:
                        act.wait_ge(s_xst, i - 2)
                    act.activation(XS[0:n, (i - 1) % 2, :], X[0:n, i - 1, :], ACT.Copy, scale=RSTD[0:n, i - 1:i]).then_inc(s_xs, 1)

            def halves(name, m, dst, off, func, **kw):
                for h in range(2):
                    ps = await_ps(act, (name, m, h))
                    read(act.activation(dst[:, m, off + h * HALF:off + (h + 1) * HALF], ps[:, 0:HALF], func, **kw),
                         (name, m, h))

            for m in range(NH):
                halves("xr", m, XRt, 3, ACT.Copy)
                if m == 0:
                    act.wait_ge(s_vec, 2)
                    act.activation(VEC[:, V_T0:V_T0 + 8], VEC[:, V_T0:V_T0 + 8], ACT.Exp).then_inc(s_vexp, 1)
            for m in range(NH):
                halves("fx", m, Kt, 0, ACT.Tanh, scale=0.5)
            act.wait_ge(s_param, 1)
            for m in range(NH):
                halves("gx", m, GXt, 0, ACT.Tanh, scale=0.5, bias=col(V_BX, m))
                halves("ga", m, GAt, 0, ACT.Tanh, scale=0.5, bias=col(V_BA, m))
                await_read(act, ("ga", m, 1))
                act.activation(TN[:, m, :], GAt[:, m, :], ACT.Tanh, scale=col(V_NC, m), bias=col(V_NC, m)).then_inc(s_gt, 1)
                act.activation(GAt[:, m, :], GAt[:, m, :], ACT.Exp, scale=col(V_C, m), bias=col(V_C, m)).then_inc(s_a, 1)
                act.wait_ge(s_a, m + 1)
                act.activation(A2[:, m, :], GAt[:, m, :], ACT.Square).then_inc(s_gt, 1)
            for m in range(NH):
                act.wait_ge(s_m2, 2 * (m + 1))
                act.activation(TN[:, m, :], TN[:, m, :], ACT.Ln, scale=0.25).then_inc(s_mu, 1)
            act.wait_ge(s_f, NH)
            for h in range(NH):
                act.activation(Ft[:, h, 0:SEQ], Ft[:, h, 0:SEQ], ACT.Ln).then_inc(s_lf, 1)
            for m in range(NH):
                act.wait_ge(s_mu, m + 1)
                act.activation(TN[:, m, :], TN[:, m, :], ACT.Exp, scale=0.5).then_inc(s_mu, 1)

            def decays(h):
                t = T[:, h % 2]
                act.wait_ge(s_d, 4 * (h + 1))
                for j, half in ((0, 64), (1, 32)):
                    v = t[:, j, :].rearrange("p (n two l) -> p n two l", two=2, l=half)
                    act.activation(v[:, :, 1, :], v[:, :, 1, :], ACT.Exp).then_inc(s_e, 1)
                    act.activation(v[:, :, 0, :], v[:, :, 0, :], ACT.Exp, scale=-1.0).then_inc(s_e, 1)
                act.activation(t[:, 4, :], t[:, 2, :], ACT.Exp).then_inc(s_e, 1)
                act.activation(t[:, 2, :], t[:, 2, :], ACT.Exp, scale=-1.0).then_inc(s_e, 1)
                act.activation(t[:, 5, :], Ft[:, h, 0:SEQ], ACT.Exp).then_inc(s_e, 1)
                act.activation(t[:, 3, :], t[:, 3, :], ACT.Exp).then_inc(s_e, 1)
                act.activation(AC[:, h, :], Ft[:, h, 0:SEQ].rearrange("p (c t) -> p c t", c=CH)[:, :, P - 1], ACT.Exp).then_inc(s_ac, 1)

            def square_o(h):
                act.wait_ge(s_o, h + 1)
                if h >= 1:
                    act.wait_ge(s_rs, 2 * h)
                    act.wait_ge(s_yn, h)
                act.activation(NB, PS[B_O][:, :], ACT.Square).then_inc(s_osq, 1)

            def head_log(h):
                ps = await_ps(act, ("mean", h))
                read(act.activation(NB, ps[:, :], ACT.Ln, bias=EPSC[:]), ("mean", h))

            def head_rstd(h):
                await_read(act, ("mean", h))
                act.activation(NB, NB, ACT.Exp, scale=-0.5).then_inc(s_rs, 2)

            decays(0)
            for s in range(8):
                name, m = ("gr" if s < 4 else "g"), s % 4
                halves(name, m, GY[:, NH:, :] if s < 4 else GY[:, 0:NH, :], 0, ACT.Copy)
                if s < 4:
                    await_read(act, (name, m, 1))
                    act.wait_ge(s_tail, 1)
                    act.activation(XRt[:, m, 0:TOK], GY[:, NH + m, :], ACT.Square).then_inc(s_gela, 1)
                if s % 2 == 0:
                    h = s // 2
                    act.wait_ge(s_kt_ps, h + 1)
                    if h == 0:
                        act.wait_ge(s_h, NH + 1)
                    if h >= 1:
                        act.wait_ge(s_kv, h)
                    act.activation(KT, PS[B_KV][:, :].rearrange("p (c t) -> p c t", c=CH), ACT.Copy).then_inc(s_kt, 1)
                    if h >= 1:
                        square_o(h - 1)
                    if h + 1 < NH:
                        decays(h + 1)
                elif s >= 3:
                    head_log((s - 3) // 2)
                    head_rstd((s - 3) // 2)
                if s == 5:
                    for m2 in range(NH):
                        act.wait_ge(s_gel, 2 * (m2 + 1))
                        act.activation(XRt[:, m2, 0:TOK], XRt[:, m2, 0:TOK], ACT.Tanh, scale=sqrt(2 / pi)).then_inc(s_gela, 1)
            for m in range(NH):
                await_read(act, ("g", m, 1))
                act.wait_ge(s_yb, m + 1)
                act.activation(XRt[:, m, 0:TOK], GY[:, m, :], ACT.Tanh, scale=0.5).then_inc(s_tg, 1)
            square_o(NH - 1)
            head_log(NH - 1)
            act.wait_ge(s_oss, 1)
            act.activation(OSB[:], OS[:], ACT.Square).then_inc(s_oss, 1)
            ps = await_ps(act, ("mean", 4))
            act.wait_ge(s_oss, 2)
            read(act.activation(OSB[:], ps[:, 0:NH * NS], ACT.Ln, bias=EPSC[:]), ("mean", 4))
            head_rstd(NH - 1)
            await_read(act, ("mean", 4))
            act.activation(OSB[:], OSB[:], ACT.Exp, scale=-0.5).then_inc(s_oss, 1)

            act.wait_ge(s_unused, 1)
            act.activation(UNUSED[:], EPSC[:], ACT.Sqrt).then_inc(s_unused, 1)
            for i, c in enumerate(TILE_ORDER):
                n = ROWS[c]
                act.wait_ge(s_opr, 2 * i + 2)
                if i == 0:
                    act.wait_ge(s_sout[0], 16 * 4)
                    act.wait_ge(s_sout[1], 16 * 4)
                if i >= 2:
                    act.wait_ge(s_xst, NT + i - 1)
                    act.wait_ge(s_xn[i % 2], 16 * (i // 2))
                act.activation(XS[0:n, i % 2, :], X[0:n, c, :], ACT.Square, accum_out=SSQ[0:n, c:c + 1]).then_inc(s_ssq, 1)
                act.wait_ge(s_ssq, NT + i + 1)
                act.activation(RSTD[0:n, c:c + 1], SSQ[0:n, c:c + 1], ACT.Sqrt, scale=1.0 / D, bias=EPSC[0:n, :]).then_inc(s_root, 1)
                act.wait_ge(s_rstd, NT + i + 1)
                act.activation(XS[0:n, i % 2, :], X[0:n, c, :], ACT.Copy, scale=RSTD[0:n, c:c + 1]).then_inc(s_xs, 1)

            act.wait_ge(s_rexp, 2 * NT)
            act.activation(GEX[:], GEX[:], ACT.Exp).then_inc(s_rexp, 1)
            act.activation(WK[:, 1, :], WK[:, 1, :], ACT.Exp).then_inc(s_rexp, 1)

            act.wait_ge(s_rnd, 1)
            rounds = act.value_load(NRND[0:1, 0:1], min_val=1, max_val=MAX_ROUNDS)

            def silu(n, p):
                act.wait_ge(s_hw, 2 * n + 2)
                act.activation(HS[p], PS[2 + p][:, 0:FE], ACT.Silu).then_inc(s_silu, 1)

            def ht_copy(n, p):
                act.wait_ge(s_htw, n + 1)
                act.activation(HT[p], PS[4][:, 0:2 * P].rearrange("p (j t) -> p j t", j=2), ACT.Copy).then_inc(s_ht, 1)

            def y_copy(n, p, scattered, load=None, last=False):
                act.wait_ge(s_yw, 2 * n + 2)
                if load is not None:
                    for slot in (2 * p, 2 * p + 1):
                        if slot != KEPT % 4 or not last:
                            load_w2(act, load + slot, slot)
                act.wait_ge(s_ys[p], 16 * scattered + 16)
                act.activation(YO[p][:, 0:512], PS[5][:, :], ACT.Copy).then_inc(s_ya, 1)

            act.sem_inc(s_ht, 1)
            act.sem_inc(s_ya, 1)
            with act.Fori(0, rounds) as r:
                base = r * NPAIR
                silu(base, 0)
                ht_copy(base, 0)

                def two_pairs(i, last=False):
                    for j in range(2):
                        q = base + i * 2 + 1 + j
                        p = 1 - j
                        silu(q, p)
                        y_copy(q - 1, 1 - p, r * (NPAIR // 2) + i, load=i * 4 + 4, last=last)
                        ht_copy(q, p)

                with act.Fori(0, NPAIR // 2 - 2) as i:
                    two_pairs(i)
                two_pairs(NPAIR // 2 - 2, last=True)
                q = base + NPAIR - 1
                silu(q, 1)
                y_copy(q - 1, 0, r * (NPAIR // 2) + NPAIR // 2 - 1)
                ht_copy(q, 1)
                y_copy(q, 1, r * (NPAIR // 2) + NPAIR // 2 - 1)

            act.wait_ge(s_unused, 2)
            act.activation(UNUSED[:], EPSC[:], ACT.Sqrt).then_inc(s_unused, 1)
            for c in range(NT):
                n = ROWS[c]
                act.wait_ge(s_cmb, 2 * (c + 1))
                act.activation(OUT[c][0:n], X[0:n, c, :], ACT.Square, accum_out=SSQ[0:n, c:c + 1]).then_inc(s_fr, 1)
                act.wait_ge(s_fr, c + 1)
                act.activation(RSTD[0:n, c:c + 1], SSQ[0:n, c:c + 1], ACT.Sqrt, scale=1.0 / D, bias=EPSC[0:n, :]).then_inc(s_froot, 1)
                if c in POOL_TILES:
                    act.wait_ge(s_frstd, c + 1)
                    act.activation(OUT[c][0:n], X[0:n, c, :], ACT.Copy, scale=RSTD[0:n, c:c + 1]).then_inc(s_fscaled, 1)

        @block.vector
        def _(dve):
            vec = [0]

            def vstep(ins):
                vec[0] += 1
                ins.then_inc(s_vec, 1)
                dve.wait_ge(s_vec, vec[0])

            dve.memset(EPSC[:], EPS).then_inc(s_init, 1)
            dve.memset(XRt[:, :, 0:3], 0.0).then_inc(s_init, 1)
            dve.memset(RESET[:], 1.0).then_inc(s_init, 1)
            dve.wait_ge(s_init, 3)
            dve.memset(RESET[:, :, 0:1], 0.0).then_inc(s_init, 1)

            def evac_xt(name, i, gain, c=None):
                c = i if c is None else c
                n = ROWS[c]
                for j in range(2):
                    ps = await_ps(dve, (name, i, j))
                    src = ps[:, :].rearrange("p (k t) -> p k t", k=4)[:, :, 0:n]
                    read(dve.tensor_tensor(XNT[:, 4 * j:4 * j + 4, c * P:c * P + n], src, bc(gain[:, 4 * j:4 * j + 4], 2, n), ALU.mult),
                         (name, i, j))

            def invert_root(i, c):
                dve.wait_ge(s_root, i + 1)
                dve.reciprocal(RSTD[0:ROWS[c], c:c + 1], RSTD[0:ROWS[c], c:c + 1]).then_inc(s_rstd, 1)

            invert_root(0, 0)
            dve.wait_ge(s_gain[0], 16)
            for i in range(NT):
                if i + 1 < NT:
                    invert_root(i + 1, i + 1)
                evac_xt("xt", i, G1)
            ps = await_ps(dve, ("par", 0))
            read(dve.tensor_copy(PARAM[:], ps[:, 0:NPAR]), ("par", 0))
            ps = await_ps(dve, ("par", 1))
            read(dve.tensor_copy(CVT[:], ps[:, 0:NS * 3 * NH]), ("par", 1))
            await_read(dve, ("par", 0))
            await_read(dve, ("par", 1))
            dve.wait_ge(s_const, 2)
            dve.tensor_copy(IOF[:], IOI[:, :]).then_inc(s_init, 1)

            def v4(at):
                return VEC[:, at:at + 4]

            def p4(at):
                return PARAM[:, at:at + 4]

            vstep(dve.tensor_tensor(v4(V_T0), p4(LB + 4), p4(LB), ALU.subtract))
            vstep(dve.scalar_tensor_tensor(out=v4(V_T1), in0=p4(LAM), scalar=-1.0, in1=p4(LAM), op0=ALU.mult, op1=ALU.min))
            dve.wait_ge(s_vexp, 1)
            vstep(dve.tensor_scalar(v4(V_T0), v4(V_T0), 1.0, None, ALU.add))
            vstep(dve.reciprocal(v4(V_T0), v4(V_T0)))
            vstep(dve.tensor_scalar(v4(V_FB), v4(V_T0), -0.5, 0.5, ALU.mult, ALU.add))
            vstep(dve.tensor_scalar(v4(V_NFB), v4(V_FB), -1.0, None, ALU.mult))
            vstep(dve.tensor_tensor(v4(V_FA), v4(V_T0), v4(V_FB), ALU.add))
            vstep(dve.tensor_scalar(v4(V_T2), v4(V_T1), 2.0, None, ALU.add))
            vstep(dve.reciprocal(v4(V_T2), v4(V_T2)))
            vstep(dve.tensor_tensor(v4(V_T1), v4(V_T1), v4(V_T2), ALU.mult))
            vstep(dve.tensor_tensor(v4(V_T2), v4(V_T1), v4(V_T1), ALU.mult))
            vstep(dve.tensor_scalar(v4(V_T3), v4(V_T2), 1.0 / 17, None, ALU.mult))
            for odd in (15, 13, 11, 9, 7, 5, 3):
                vstep(dve.scalar_tensor_tensor(out=v4(V_T3), in0=v4(V_T3), scalar=1.0 / odd, in1=v4(V_T2), op0=ALU.add, op1=ALU.mult))
            vstep(dve.scalar_tensor_tensor(out=v4(V_T3), in0=v4(V_T3), scalar=1.0, in1=v4(V_T1), op0=ALU.add, op1=ALU.mult))
            vstep(dve.tensor_scalar(v4(V_T1), p4(LAM), -1.0, 0.0, ALU.mult, ALU.max))
            vstep(dve.scalar_tensor_tensor(out=v4(V_T3), in0=v4(V_T3), scalar=2.0, in1=v4(V_T1), op0=ALU.mult, op1=ALU.add))
            vstep(dve.tensor_scalar(v4(V_C), v4(V_T3), -4.0, None, ALU.mult))
            vstep(dve.tensor_scalar(v4(V_NC), v4(V_T3), 4.0, None, ALU.mult))
            vstep(dve.tensor_scalar(v4(V_BX), p4(BX), 0.5, None, ALU.mult))
            vstep(dve.tensor_scalar(v4(V_BA), p4(BA), 0.5, None, ALU.mult))
            dve.tensor_scalar(v4(V_HG), p4(HGG), 0.5, None, ALU.mult).then_inc(s_param, 1)

            conv = [0]

            def cstep(ins):
                conv[0] += 1
                ins.then_inc(s_conv, 1)
                dve.wait_ge(s_conv, conv[0])

            dve.wait_ge(s_param, 1)
            for m in range(NH):
                await_read(dve, ("xr", m, 1))
                cstep(dve.tensor_scalar(XCt[:, m, 0:SEQ], XRt[:, m, 0:SEQ], PARAM[:, CW + m:CW + m + 1],
                                        PARAM[:, CB + m:CB + m + 1], ALU.mult, ALU.add))
                for w in range(1, 4):
                    cstep(dve.scalar_tensor_tensor(out=XCt[:, m, 0:SEQ], in0=XRt[:, m, w:w + SEQ],
                                                   scalar=PARAM[:, CW + 4 * w + m:CW + 4 * w + m + 1],
                                                   in1=XCt[:, m, 0:SEQ], op0=ALU.mult, op1=ALU.add))
            xs_c = XCt[:, :, SEQ:TOK]
            hist = CVT[:, :].rearrange("p (b w m) -> p w m b", b=NS, w=3)
            cstep(dve.tensor_tensor(xs_c, XRt[:, :, SEQ + 3:TOK + 3], bc(p4(CW + 12), 2, NS), ALU.mult))
            cstep(dve.tensor_tensor(xs_c, xs_c, bc(p4(CB), 2, NS), ALU.add))
            for w in range(3):
                cstep(dve.tensor_tensor(SCR[:, 0:NH, :], hist[:, w], bc(p4(CW + 4 * w), 2, NS), ALU.mult))
                cstep(dve.tensor_tensor(xs_c, xs_c, SCR[:, 0:NH, :], ALU.add))

            for h in range(NH):
                await_read(dve, ("fx", h, 1))
                dve.tensor_scalar(Ft[:, h, :], Kt[:, h, :], col(V_FB, h), col(V_FA, h), ALU.mult, ALU.add).then_inc(s_f, 1)
                dve.tensor_scalar(Kt[:, h, :], Kt[:, h, :], col(V_NFB, h), col(V_FB, h), ALU.mult, ALU.add).then_inc(s_k, 1)

            def mult_squared(m):
                dve.wait_ge(s_gt, 2 * (m + 1))
                dve.scalar_tensor_tensor(out=TN[:, m, :], in0=A2[:, m, :], scalar=1.0, in1=TN[:, m, :],
                                         op0=ALU.add, op1=ALU.mult).then_inc(s_m2, 1)
                dve.wait_ge(s_m2, 2 * m + 1)
                dve.tensor_scalar(TN[:, m, :], TN[:, m, :], 1e-18, None, ALU.max).then_inc(s_m2, 1)

            for m in range(NH):
                for hf in range(2):
                    ps = await_ps(dve, ("q", m, hf))
                    read(dve.tensor_copy(Qt[:, m, hf * HALF:(hf + 1) * HALF], ps[:, 0:HALF]), ("q", m, hf))
                if m >= 1:
                    mult_squared(m - 1)
            mult_squared(NH - 1)
            def exponents(h):
                t = T[:, h % 2]
                if h >= 2:
                    dve.wait_ge(s_o, h - 1)
                dve.wait_ge(s_lf, h + 1)
                b = Ft[:, h, 0:SEQ]
                dve.tensor_tensor_scan(b, RESET[:, :, :].rearrange("p c t -> p (c t)"), b, 0.0, ALU.mult, ALU.add).then_inc(s_b, 1)
                dve.wait_ge(s_b, h + 1)
                for j, size, at in ((0, P, 63), (1, 64, 31), (2, SUB, SUB // 2 - 1)):
                    bv = b.rearrange("p (n l) -> p n l", l=size)
                    tv = t[:, j, :].rearrange("p (n l) -> p n l", l=size)
                    dve.tensor_tensor(tv, bv, bc(bv[:, :, at], 2, size), ALU.subtract).then_inc(s_d, 1)
                bv = b.rearrange("p (n l) -> p n l", l=P)
                dve.tensor_tensor(t[:, 3, :].rearrange("p (n l) -> p n l", l=P), bc(bv[:, :, P - 1], 2, P), bv,
                                  ALU.subtract).then_inc(s_d, 1)

            def decayed_qk(h):
                t = T[:, h % 2]
                dve.wait_ge(s_e, 8 * (h + 1))
                q, k = Qt[:, h, 0:SEQ], Kt[:, h, 0:SEQ]
                for j, half in ((0, 64), (1, 32)):
                    tv = t[:, j, :].rearrange("p (n two l) -> p n two l", two=2, l=half)
                    for two, x in ((1, q), (0, k)):
                        xv = x.rearrange("p (n two l) -> p n two l", two=2, l=half)
                        dve.tensor_tensor(tv[:, :, two, :], tv[:, :, two, :], xv[:, :, two, :], ALU.mult).then_inc(s_qk, 1)
                for j, x in ((4, q), (2, k), (5, q), (3, k)):
                    dve.tensor_tensor(t[:, j, :], t[:, j, :], x, ALU.mult).then_inc(s_qk, 1)

            def v_out(c):
                ps = await_ps(dve, ("v", c))
                if c < CH:
                    read(dve.tensor_copy(Vt[:, c, :], ps[:, :]), ("v", c))
                    return
                dve.tensor_copy(Vs[:], ps[0:NS, :]).then_inc(s_vs, 1)
                for g in range(1, 4):
                    dve.wait_ge(s_vs, g)
                    ins = dve.tensor_tensor(Vs[:], Vs[:], ps[32 * g:32 * g + NS, :], ALU.add)
                    if g < 3:
                        ins.then_inc(s_vs, 1)
                read(ins, ("v", c))

            ustep_n = [0]

            def ustep(ins):
                ustep_n[0] += 1
                ins.then_inc(s_u, 1)
                dve.wait_ge(s_u, ustep_n[0])

            def recur(m):
                ustep(dve.scalar_tensor_tensor(out=GXt[:, m, :], in0=GXt[:, m, :], scalar=1.0, in1=XCt[:, m, :],
                                               op0=ALU.add, op1=ALU.mult))
                ustep(dve.tensor_tensor(GXt[:, m, :], GXt[:, m, :], TN[:, m, :], ALU.mult))
                dve.tensor_tensor_scan(XCt[:, m, 0:SEQ], GAt[:, m, 0:SEQ], GXt[:, m, 0:SEQ], 0.0, ALU.mult, ALU.add).then_inc(s_h, 1)

            dve.tensor_copy(QS[:, :].rearrange("p (h b) -> p h b", h=NH), Qt[:, :, SEQ:TOK]).then_inc(s_qs, 1)
            v_out(CH)
            exponents(0)
            v_out(0)
            dve.wait_ge(s_mu, 2 * NH)
            ustep(dve.memset(TN[:, :, 0:1], 0.5))
            recur(0)
            recur(1)
            v_out(1)
            decayed_qk(0)
            v_out(2)
            recur(2)
            recur(3)
            h0 = PARAM[:, H0:NPAR].rearrange("p (b m) -> p m b", b=NS)
            ustep(dve.tensor_tensor(SCR[:, 0:NH, :], GAt[:, :, SEQ:TOK], h0, ALU.mult))
            dve.tensor_tensor(XCt[:, :, SEQ:TOK], SCR[:, 0:NH, :], GXt[:, :, SEQ:TOK], ALU.add).then_inc(s_h, 1)
            v_out(3)
            ps = await_ps(dve, ("xtail",))
            read(dve.tensor_copy(TAIL[:], ps[0:11, :]), ("xtail",))
            await_read(dve, ("xtail",))
            dve.sem_inc(s_tail, 1)

            def scores(h):
                dve.wait_ge(s_scores, h + 1)
                if h >= 2:
                    dve.wait_ge(s_o, h - 1)
                sc = SC[:, h % 2]
                sd = PS[B_SD][:, :].rearrange("p (c t) -> p c t", c=CH)
                sl = PS[B_SL][:, :].rearrange("p (c t) -> p c t", c=CH)
                dve.copy_predicated(sc, bc(CMASK[:].bitcast(I32), 1, CH), sd).then_inc(s_sc, 1)
                dve.wait_ge(s_sc, 4 * h + 1)
                for s0, n in ((0, 64), (0, 32), (64, 32)):
                    dve.tensor_copy(sc[s0:s0 + n, :, s0 + n:s0 + 2 * n], sl[s0:s0 + n, :, s0 + n:s0 + 2 * n]).then_inc(s_sc, 1)

            def states(h):
                dve.wait_ge(s_kv, h + 1)
                dve.wait_ge(s_ac, h + 1)
                if h >= 2:
                    dve.wait_ge(s_hp, 16 * (h - 1))
                    dve.wait_ge(s_o, h - 1)
                kv = PS[B_KV][:, :].rearrange("p (c t) -> p c t", c=CH)
                dve.tensor_copy(S[:, h % 2, 0, :], kv[:, 0, :]).then_inc(s_s, 1)
                for c in range(1, CH):
                    dve.wait_ge(s_s, CH * h + c)
                    dve.scalar_tensor_tensor(out=S[:, h % 2, c, :], in0=S[:, h % 2, c - 1, :], scalar=AC[:, h, c:c + 1],
                                             in1=kv[:, c, :], op0=ALU.mult, op1=ALU.add).then_inc(s_s, 1)

            def normed(h):
                dve.wait_ge(s_rs, 2 * (h + 1))
                dve.scalar_tensor_tensor(out=Kt[:, h, 0:SEQ], in0=PS[B_O][:, :], scalar=col(V_HG, h), in1=NB,
                                         op0=ALU.mult, op1=ALU.mult).then_inc(s_yn, 1)

            def sample_state(b):
                kv = VB[:, b % 2, :].rearrange("p (h e) -> p h e", h=NH)
                dve.wait_ge(s_vb[b % 2], 16 * (b // 2 + 1))
                dve.tensor_tensor(kv, kv, bc(Kt[:, :, SEQ + b], 2, P), ALU.mult).then_inc(s_skv, 1)
                dve.wait_ge(s_sin[b % 2], 16 * (b // 2 + 1))
                st = SST[:, b % 2, :].rearrange("p (h e) -> p h e", h=NH)
                dve.tensor_tensor(st, st, bc(Ft[:, :, SEQ + b], 2, P), ALU.mult).then_inc(s_skv, 1)
                dve.wait_ge(s_skv, 2 * b + 2)
                dve.tensor_tensor(st, st, kv, ALU.add).then_inc(s_sst, 1)

            def copy_ox(g):
                dve.wait_ge(s_osw, 2 * g + 2)
                dve.tensor_copy(OX, PS[B_OS][:, :]).then_inc(s_ox, 1)

            def pick_os(g):
                ps = await_ps(dve, ("ost", g))
                for h in range(NH):
                    at = h * (P + NS) + 4 * g
                    ins = dve.tensor_copy(OS[:, h * NS + 4 * g:h * NS + 4 * g + 4], ps[:, at:at + 3 * 33 + 1:33])
                read(ins, ("ost", g))

            gel = [0]

            def gelu_argument(m):
                dve.wait_ge(s_gela, m + 1)
                dve.tensor_scalar(XRt[:, m, 0:TOK], XRt[:, m, 0:TOK], 0.044715, 1.0, ALU.mult, ALU.add).then_inc(s_gel, 1)
                dve.wait_ge(s_gel, 2 * m + 1)
                dve.tensor_tensor(XRt[:, m, 0:TOK], XRt[:, m, 0:TOK], GY[:, NH + m, :], ALU.mult).then_inc(s_gel, 1)

            dve.wait_ge(s_h, NH + 1)
            dve.memset(SC, 0.0).then_inc(s_zero_sc, 1)
            dve.wait_ge(s_zero_sc, 1)
            dve.wait_ge(s_const, 2)
            for s in range(8):
                h = s // 2
                if s == 5:
                    copy_ox(0)
                if s == 7:
                    pick_os(0)
                if s % 2 == 0:
                    scores(h)
                else:
                    states(h)
                    if s >= 3:
                        normed((s - 3) // 2)
                    sample_state(s - 1)
                    sample_state(s)
                if s % 2 == 0 and h + 1 < NH:
                    exponents(h + 1)
                    decayed_qk(h + 1)
                if s < 4:
                    gelu_argument(s)
                if s == 6:
                    for m in range(NH):
                        dve.wait_ge(s_gela, NH + m + 1)
                        yb = GY[:, NH + m, :]
                        dve.scalar_tensor_tensor(out=yb, in0=XRt[:, m, 0:TOK], scalar=1.0, in1=yb,
                                                 op0=ALU.add, op1=ALU.mult).then_inc(s_gel, 1)
                        dve.wait_ge(s_gel, 2 * NH + m + 1)
                        dve.scalar_tensor_tensor(out=yb, in0=yb, scalar=0.5, in1=XCt[:, m, :],
                                                 op0=ALU.mult, op1=ALU.mult).then_inc(s_yb, 1)
            copy_ox(1)
            pick_os(1)
            await_read(dve, ("ost", 0))
            await_read(dve, ("ost", 1))
            dve.sem_inc(s_oss, 1)
            for m in range(NH):
                dve.wait_ge(s_tg, m + 1)
                dve.scalar_tensor_tensor(out=GY[:, m, :], in0=XRt[:, m, 0:TOK], scalar=1.0, in1=GY[:, m, :],
                                         op0=ALU.add, op1=ALU.mult).then_inc(s_sg, 1)
            normed(NH - 1)
            dve.wait_ge(s_sg, NH)
            for h in range(NH):
                dve.wait_ge(s_yn, h + 1)
                dve.tensor_tensor(GY[:, h, 0:SEQ], GY[:, h, 0:SEQ], Kt[:, h, 0:SEQ], ALU.mult).then_inc(s_y, 1)
            dve.wait_ge(s_oss, 3)
            dve.tensor_tensor(OS[:], OS[:], OSB[:], ALU.mult).then_inc(s_oss, 1)
            dve.wait_ge(s_oss, 4)
            os_v = OS[:, :].rearrange("p (h b) -> p h b", h=NH)
            dve.tensor_tensor(os_v, os_v, bc(v4(V_HG), 2, NS), ALU.mult).then_inc(s_oss, 1)
            dve.wait_ge(s_oss, 5)
            dve.tensor_tensor(GY[:, 0:NH, SEQ:TOK], GY[:, 0:NH, SEQ:TOK], os_v, ALU.mult).then_inc(s_y, 1)
            ps = await_ps(dve, ("htail",))
            read(dve.tensor_copy(HTAIL[:], ps[0:9, :]), ("htail",))
            await_read(dve, ("htail",))
            dve.sem_inc(s_tail, 1)

            rt = [0]

            def rstep(ins):
                rt[0] += 1
                ins.then_inc(s_r, 1)
                dve.wait_ge(s_r, rt[0])

            dve.wait_ge(s_rt, 16 * 4)
            dve.tensor_copy(WR[:, :, 0:GROUPS], WGt[:, :].rearrange("p (k g) -> p k g", k=KD)).then_inc(s_r, 1)
            for g in range(GROUPS):
                dve.tensor_copy(WR[:, :, GROUPS + PER_GROUP * g:GROUPS + PER_GROUP * (g + 1)],
                                WEt[:, g, :].rearrange("p (k e) -> p k e", k=KD)).then_inc(s_r, 1)
            dve.memset(LG[:], 0.0).then_inc(s_r, 1)
            dve.memset(L8[:], -3e38).then_inc(s_r, 1)
            dve.memset(CHO[:, NT, :], 0.0).then_inc(s_r, 1)
            dve.memset(CUM[:, 0, :], 0.0).then_inc(s_r, 1)
            rt[0] += 5 + GROUPS
            dve.wait_ge(s_r, rt[0])

            def route(c, tile):
                rstep(dve.tensor_copy(L8[:, c, 0:GROUPS], LG[:, c, 0:GROUPS]))
                rstep(dve.max(TOP[:, c, :], L8[:, c, :]))
                rstep(dve.max_index(TIX[:, c, :], TOP[:, c, :], L8[:, c, :]))
                rstep(dve.tensor_copy(GIX[:, c:c + 1], TIX[:, c, 0:1]))
                dve.tensor_tensor(GEX[:, c, :], LG[:, c, 0:GROUPS], TOP[:, c, 0:1].to_broadcast([P, GROUPS]),
                                  ALU.subtract).then_inc(s_rexp, 1)
                rstep(dve.tensor_scalar(LMSK[:, 0, :], iota_g, GIX[:, c:c + 1], 3e38, ALU.is_equal, ALU.mult))
                rstep(dve.scalar_tensor_tensor(out=LSEL[:, c, :], in0=LMSK[:, 0, :], scalar=-3e38, in1=LG[:, c, GROUPS:],
                                               op0=ALU.add, op1=ALU.add))
                dve.wait_ge(s_rexp, 2 * c + 1)
                rstep(dve.max(TOP[:, c, :], LSEL[:, c, :]))
                rstep(dve.max_index(TIX[:, c, :], TOP[:, c, :], LSEL[:, c, :]))
                rstep(dve.tensor_copy(EIX[:, c, :], TIX[:, c, 0:2]))
                dve.tensor_tensor(WK[:, 1, c:c + 1], TOP[:, c, 1:2], TOP[:, c, 0:1], ALU.subtract).then_inc(s_rexp, 1)
                for k in range(2):
                    dve.tensor_scalar(OH[:, k, c, :], iota_e, EIX[:, c, k:k + 1], None, ALU.is_equal).then_inc(s_r, 1)
                    dve.tensor_scalar(OHV[:, k, c, :], iota_e, EIX[:, c, k:k + 1], token_code[:, k, tile:tile + 1],
                                      ALU.is_equal, ALU.mult).then_inc(s_r, 1)
                rt[0] += 4
                dve.wait_ge(s_r, rt[0])
                rstep(dve.tensor_tensor(CHO[:, c, :], OH[:, 0, c, :], OH[:, 1, c, :], ALU.add))
                n = ROWS[tile]
                if n < P:
                    rstep(dve.tensor_copy(CUM[:, c + 1, :], CUM[:, c, :]))
                rstep(dve.tensor_tensor(CUM[0:n, c + 1, :], CUM[0:n, c, :], CHO[0:n, c, :], ALU.add))

            def residual(i, half):
                c = TILE_ORDER[i]
                dve.wait_ge(s_op, 2 * i + half + 1)
                ps = OP[i % 2][half]
                x = X[0:ROWS[c], c, half * 512:(half + 1) * 512]
                if c < CH:
                    dve.tensor_tensor(x, ps[:, :], x, ALU.add).then_inc(s_opr, 1)
                    return
                for g in range(4):
                    ins = dve.tensor_tensor(x, ps[32 * g:32 * g + NS, :], x, ALU.add)
                    if g < 3:
                        rstep(ins)
                ins.then_inc(s_opr, 1)

            dve.wait_ge(s_gain[1], 16)
            for i in range(NT + 2):
                if i < NT:
                    residual(i, 0)
                if i > 1:
                    ps = await_ps(dve, ("lg", i - 2))
                    n = ROWS[TILE_ORDER[i - 2]]
                    read(dve.tensor_tensor(LG[0:n, i - 2, :], ps[0:n, 0:GROUPS + NE], RB[0:n, :], ALU.add), ("lg", i - 2))
                if i < NT:
                    residual(i, 1)
                if 1 <= i <= NT:
                    evac_xt("x2t", i - 1, G2, TILE_ORDER[i - 1])
                if i < NT:
                    invert_root(NT + i, TILE_ORDER[i])
                if i > 1:
                    await_read(dve, ("lg", i - 2))
                    route(i - 2, TILE_ORDER[i - 2])
            dve.sem_inc(s_oh, 1)

            ps = await_ps(dve, ("pos",))
            pos = ps[:, 0:NT * NE].rearrange("p (i e) -> p i e", i=NT)
            rstep(dve.tensor_tensor(OH[:], OH[:], bc(pos, 1, 2), ALU.mult))
            rstep(dve.reduce_sum(RANK[:], OH[:], AX_X))
            rstep(dve.reduce_max(CNT[:, 0:1], ps[:, NT * NE:(NT + 1) * NE], AX_X))
            rstep(dve.tensor_scalar(NRND[:], CNT[:, 0:1], CAP - 1.0, None, ALU.add))
            dve.tensor_scalar(NRND[:], NRND[:], CAP.bit_length() - 1, None, ALU.arith_shift_right).then_inc(s_rnd, 1)
            dve.wait_ge(s_rnd, 1)
            rounds = dve.value_load(NRND[0:1, 0:1], min_val=1, max_val=MAX_ROUNDS)

            def xgt(n, p):
                dve.wait_ge(s_tw, n + 1)
                for j in range(2):
                    dve.tensor_tensor(XGT[p][:, 4 * j:4 * j + 4, :], PS[j][:, :].rearrange("p (k t) -> p k t", k=4),
                                      bc(G2[:, 4 * j:4 * j + 4], 2, P), ALU.mult).then_inc(s_xgt, 1)

            def gated(n, p):
                dve.wait_ge(s_silu, n + 1)
                dve.tensor_tensor(HG[p], PS[2 + p][:, FE:2 * FE], HS[p], ALU.mult).then_inc(s_hg, 1)

            def y_copy(n, p, scattered):
                dve.wait_ge(s_yw, 2 * n + 2)
                dve.wait_ge(s_ys[p], 16 * scattered + 16)
                dve.tensor_copy(YO[p][:, 512:1024], PS[6][:, :]).then_inc(s_yd, 1)

            dve.wait_ge(s_hp, 16 * NH)
            dve.sem_inc(s_xgt, 1)
            dve.sem_inc(s_yd, 1)
            with dve.Fori(0, rounds) as r:
                base = r * NPAIR
                dve.wait_ge(s_rdone, r + 1)
                for j in range(2 * NT):
                    i, k = j // 2, j % 2
                    dve.wait_ge(s_pmu, r * (2 * NT) + max(j - NPM + 1, 0) + 1)
                    dve.tensor_scalar(PM[:, j % NPM, :], iota_s, RANK[:, k, i:i + 1], None, ALU.is_equal).then_inc(s_pm, 1)
                dve.wait_ge(s_tab, r + 1)
                dve.tensor_scalar(DSTI[:, 0:NPAIR], PS[B_O][:, 0:NPAIR], float(BIG), None, ALU.add).then_inc(s_tabs, 1)
                dve.tensor_scalar(RANK[:], RANK[:], float(-CAP), None, ALU.add).then_inc(s_tabs, 1)
                dve.wait_ge(s_tabs, 2 * r + 2)
                dve.tensor_scalar(SRCI[:, 0:NPAIR], DSTI[:, 0:NPAIR], 1, None, ALU.arith_shift_right).then_inc(s_tabr, 1)
                xgt(base, 0)
                xgt(base + 1, 1)
                gated(base, 0)
                with dve.Fori(0, NPAIR // 2 - 1) as i:
                    for j in range(2):
                        q = base + i * 2 + 1 + j
                        p = 1 - j
                        xgt(q + 1, 1 - p)
                        gated(q, p)
                        y_copy(q - 1, 1 - p, r * (NPAIR // 2) + i)
                q = base + NPAIR - 1
                gated(q, 1)
                y_copy(q - 1, 0, r * (NPAIR // 2) + NPAIR // 2 - 1)
                y_copy(q, 1, r * (NPAIR // 2) + NPAIR // 2 - 1)

            dve.wait_ge(s_rexp, 2 * NT + 2)
            rstep(dve.reduce_sum(PTOP[:], GEX[:], AX_X))
            rstep(dve.reciprocal(PTOP[:], PTOP[:]))
            rstep(dve.tensor_scalar(WK[:, 0, :], WK[:, 1, :], 1.0, None, ALU.add))
            rstep(dve.reciprocal(WK[:, 0, :], WK[:, 0, :]))
            rstep(dve.tensor_tensor(WK[:, 0, :], WK[:, 0, :], PTOP[:], ALU.mult))
            rstep(dve.tensor_tensor(WK[:, 1, :], WK[:, 1, :], WK[:, 0, :], ALU.mult))

            dve.wait_ge(s_fg, 16)
            for c in range(NT + 1):
                if c < NT:
                    n = ROWS[c]
                    dve.wait_ge(s_ye[c], 16)
                    at = TILE_ORDER.index(c)
                    for k in range(2):
                        dve.scalar_tensor_tensor(out=X[0:n, c, :], in0=YE[c][0:n, k, :], scalar=WK[0:n, k, at:at + 1],
                                                 in1=X[0:n, c, :], op0=ALU.mult, op1=ALU.add).then_inc(s_cmb, 1)
                        dve.wait_ge(s_cmb, 2 * c + k + 1)
                if c > 0:
                    n = ROWS[c - 1]
                    dve.wait_ge(s_froot, c)
                    dve.reciprocal(RSTD[0:n, c - 1:c], RSTD[0:n, c - 1:c]).then_inc(s_frstd, 1)
                    if c - 1 in POOL_TILES:
                        continue
                    dve.wait_ge(s_frstd, c)
                    dve.scalar_tensor_tensor(out=OUT[c - 1][0:n], in0=X[0:n, c - 1, :], scalar=RSTD[0:n, c - 1:c],
                                             in1=FGB[0:n], op0=ALU.mult, op1=ALU.mult).then_inc(s_fin[c - 1], 1)

        @block.tensor
        def _(pe):
            pe.wait_ge(s_const, 1)

            def transpose_rows(name, i, c):
                n = ROWS[c]
                xv = XS[0:n, i % 2, :].rearrange("t (p k) -> t k p", k=KD)
                for j in range(2):
                    ps = claim(pe, (name, i, j))
                    for k in range(4):
                        ins = pe.transpose(ps[:, k * P:k * P + n], xv[:, 4 * j + k, :], IDENT[0:n, 0:n])
                    written(ins, (name, i, j))

            for i in range(NT):
                pe.wait_ge(s_xs, i + 1)
                transpose_rows("xt", i, i)
                bank, use = ROT[("xt", i, 1)]
                pe.wait_ge(s_written[bank], use + 1)
                pe.sem_inc(s_xst, 1)
            await_read(pe, ("xt", NT - 1, 1))

            def project(name, j, m):
                for hf in range(2):
                    ps = claim(pe, (name, m, hf))
                    for k in range(KD):
                        ins = pe.matmul(ps[:, 0:HALF], WC[:, j % 2, k, m * P:(m + 1) * P],
                                        XNT[:, k, hf * HALF:(hf + 1) * HALF], start=(k == 0), stop=(k == KD - 1))
                    written(ins, (name, m, hf))

            def short_tile(ps, products):
                for i, (rows, weights) in enumerate(products):
                    at = 32 * (i % 4)
                    ins = pe.matmul(ps[at:at + NS, :], rows, weights, start=(i < 4), stop=(i >= len(products) - 4),
                                    tile_position=(0, at), skip_group_check=True)
                return ins

            def chunk(j):
                pe.wait_ge(s_wc[j % 2], 16 * (j // 2 + 1))

            def chunk_done(name):
                b, u = ROT[name]
                pe.wait_ge(s_written[b], u + 1)
                pe.sem_inc(s_wc_free, 1)

            for j, name in ((0, "xr"), (1, "fx")):
                chunk(j)
                for m in range(NH):
                    project(name, j, m)
                    if (name, m) == ("xr", 0):
                        pe.wait_ge(s_par, 16 * 9)
                        ps = claim(pe, ("par", 0))
                        written(pe.transpose(ps[:, 0:NPAR], PROW[:], IDENT[0:NPAR, 0:NPAR]), ("par", 0))
                        ps = claim(pe, ("par", 1))
                        written(pe.transpose(ps[:, 0:NS * 3 * NH], CROW[:], IDENT[0:NS * 3 * NH, 0:NS * 3 * NH]), ("par", 1))
                chunk_done((name, NH - 1, 1))
            chunk(2)
            pe.wait_ge(s_bd, 16 * 4)
            for m in range(NH):
                project("q", 2, m)
                if m == 0:
                    pe.wait_ge(s_conv, 16 + 8)
                for name, w in (("gx", BDX), ("ga", BDA)):
                    for hf in range(2):
                        ps = claim(pe, (name, m, hf))
                        written(pe.matmul(ps[:, 0:HALF], w[:, m, :], XCt[:, m, hf * HALF:(hf + 1) * HALF],
                                          start=True, stop=True), (name, m, hf))
            chunk_done(("q", NH - 1, 1))
            chunk(3)
            for c in TILE_ORDER:
                ps = claim(pe, ("v", c))
                if c < CH:
                    for k in range(KD):
                        ins = pe.matmul(ps[:, :], XNT[:, k, c * P:(c + 1) * P], WC[:, 1, k, :],
                                        start=(k == 0), stop=(k == KD - 1))
                else:
                    ins = short_tile(ps, [(XNT[:, k, SEQ:TOK], WC[:, 1, k, :]) for k in range(KD)])
                written(ins, ("v", c))
            chunk_done(("v", TILE_ORDER[-1]))
            ps = claim(pe, ("xtail",))
            for m in range(NH):
                ins = pe.transpose(ps[0:11, m * P:(m + 1) * P], XRt[:, m, SEQ:TOK + 3], IDENT[:])
            written(ins, ("xtail",))

            def head_scores(h):
                t = T[:, h % 2]
                pe.wait_ge(s_qk, 8 * (h + 1))
                if h >= 1:
                    pe.wait_ge(s_sc, 4 * h)
                for c in range(CH):
                    at = c * P
                    pe.matmul(PS[B_SD][:, at:at + P], t[:, 2, at:at + P], t[:, 4, at:at + P], start=True, stop=True)
                for c in range(CH):
                    at = c * P
                    for j, s0, n in ((0, 0, 64), (1, 0, 32), (1, 64, 32)):
                        ins = pe.matmul(PS[B_SL][s0:s0 + n, at + s0 + n:at + s0 + 2 * n], t[:, j, at + s0:at + s0 + n],
                                        t[:, j, at + s0 + n:at + s0 + 2 * n], start=True, stop=True,
                                        tile_position=(0, s0), skip_group_check=True)
                ins.then_inc(s_scores, 1)
                if h >= 1:
                    pe.wait_ge(s_s, CH * h)
                for c in range(CH):
                    ins = pe.transpose(PS[B_KV][:, c * P:(c + 1) * P], t[:, 3, c * P:(c + 1) * P], IDENT[:])
                ins.then_inc(s_kt_ps, 1)

            def head_kv(h):
                pe.wait_ge(s_kt, h + 1)
                for c in range(CH):
                    ins = pe.matmul(PS[B_KV][:, c * P:(c + 1) * P], KT[:, c, :], Vt[:, c, h * P:(h + 1) * P], start=True, stop=True)
                ins.then_inc(s_kv, 1)

            def head_o(h):
                pe.wait_ge(s_sc, 4 * (h + 1))
                pe.wait_ge(s_s, CH * (h + 1))
                if h >= 1:
                    pe.wait_ge(s_yn, h)
                for c in range(CH):
                    o = PS[B_O][:, c * P:(c + 1) * P]
                    ins = pe.matmul(o, Vt[:, c, h * P:(h + 1) * P], SC[:, h % 2, c, :], start=True, stop=(c == 0))
                    if c > 0:
                        ins = pe.matmul(o, S[:, h % 2, c - 1, :], T[:, h % 2, 5, c * P:(c + 1) * P], start=False, stop=True)
                ins.then_inc(s_o, 1)

            def head_mean(h):
                ps = claim(pe, ("mean", h))
                pe.wait_ge(s_osq, h + 1)
                written(pe.matmul(ps[:, :], MEAN128[:], NB, start=True, stop=True), ("mean", h))

            def sample_pair(j):
                pe.wait_ge(s_sst, 2 * j + 2)
                if j == 2:
                    pe.wait_ge(s_ox, 1)
                for b in (2 * j, 2 * j + 1):
                    at = 32 * (b % 4)
                    ins = pe.matmul(PS[B_OS][at:at + 32, :], QS[:], SST[:, b % 2, :], start=True, stop=True,
                                    tile_position=(0, at), skip_group_check=True)
                ins.then_inc(s_osw, 1)

            def sample_turn(g):
                ps = claim(pe, ("ost", g))
                pe.wait_ge(s_ox, g + 1)
                for h in range(NH):
                    ins = pe.transpose(ps[:, h * P:(h + 1) * P], OX[:, h * P:(h + 1) * P], IDENT[:])
                written(ins, ("ost", g))

            pe.wait_ge(s_qs, 1)
            pe.wait_ge(s_const, 2)
            for s in range(8):
                h = s // 2
                if s % 4 == 0:
                    chunk(4 + s // 4)
                name = "gr" if s < 4 else "g"
                project(name, 4 + s // 4, s % 4)
                if s % 2 == 0:
                    head_scores(h)
                    if h >= 1:
                        head_o(h - 1)
                else:
                    head_kv(h)
                    if s >= 3:
                        head_mean((s - 3) // 2)
                if s % 2 == 0 and s >= 2:
                    sample_pair(s // 2 - 1)
                if s == 6:
                    sample_turn(0)
                if s % 4 == 3:
                    chunk_done((name, NH - 1, 1))
            def out_rows(i, half, part=None):
                c = TILE_ORDER[i]
                ps = OP[i % 2][half]
                if i >= 2 and half == 0:
                    pe.wait_ge(s_opr, 2 * i - 2)
                if i == 1:
                    pe.wait_ge(s_s, CH * NH)
                    pe.wait_ge(s_yn, NH)
                order = list(range(NH, 2 * NH)) + list(range(NH))
                products = [(GY[:, m, c * P:c * P + ROWS[c]], WC[:, half, m, :]) for m in order]
                if c < CH:
                    for j in range(2 * NH) if part is None else range(NH * part, NH * (part + 1)):
                        rows, weights = products[j]
                        ins = pe.matmul(ps[:, :], rows, weights, start=(j == 0), stop=(j == 2 * NH - 1), skip_group_check=True)
                else:
                    ins = short_tile(ps, products)
                if part != 0:
                    ins.then_inc(s_op, 1)

            chunk(6)
            pe.wait_ge(s_yb, NH)
            pe.wait_ge(s_sc, 4 * NH)
            out_rows(0, 0, part=0)
            head_o(NH - 1)
            sample_pair(3)
            head_mean(NH - 1)
            sample_turn(1)
            ps = claim(pe, ("mean", 4))
            pe.wait_ge(s_oss, 2)
            written(pe.matmul(ps[:, 0:NH * NS], MEAN128[:], OSB[:], start=True, stop=True), ("mean", 4))
            chunk(7)
            out_rows(0, 1, part=0)
            ps = claim(pe, ("htail",))
            pe.wait_ge(s_h, NH + 1)
            for m in range(NH):
                ins = pe.transpose(ps[0:9, m * P:(m + 1) * P], XCt[:, m, SEQ - 1:TOK], IDENT[:])
            written(ins, ("htail",))

            pe.wait_ge(s_y, NH + 1)
            out_rows(0, 0, part=1)
            out_rows(0, 1, part=1)
            for i in range(NT + 2):
                if 0 < i < NT:
                    out_rows(i, 0)
                if i > 1:
                    c = TILE_ORDER[i - 2]
                    n = ROWS[c]
                    ps = claim(pe, ("lg", i - 2))
                    await_read(pe, ("x2t", i - 2, 1))
                    for k in range(KD):
                        ins = pe.matmul(ps[0:n, 0:GROUPS + NE], XNT[:, k, c * P:c * P + n], WR[:, k, :],
                                        start=(k == 0), stop=(k == KD - 1))
                    written(ins, ("lg", i - 2))
                if 0 < i < NT:
                    out_rows(i, 1)
                if 1 <= i <= NT:
                    pe.wait_ge(s_xs, NT + i)
                    transpose_rows("x2t", i - 1, TILE_ORDER[i - 1])
                    bank, use = ROT[("x2t", i - 1, 1)]
                    pe.wait_ge(s_written[bank], use + 1)
                    pe.sem_inc(s_xst, 1)

            ps = claim(pe, ("pos",))
            pe.wait_ge(s_oh, 1)
            for lhs, src, first in ((LTRI, CHO, True), (ONES, CUM, False)):
                ins = pe.matmul(ps[:, 0:(NT + 1) * NE], lhs[:], src[:, :, :].rearrange("p i e -> p (i e)"), start=first, stop=not first)
            written(ins, ("pos",))
            pe.wait_ge(s_rnd, 1)
            rounds = pe.value_load(NRND[0:1, 0:1], min_val=1, max_val=MAX_ROUNDS)

            def turn(n, p, use):
                pe.wait_ge(s_xg[p], 16 * (use + 1))
                pe.wait_ge(s_xgt, 2 * n + 1)
                xv = XG[p].rearrange("t (p k) -> t k p", k=KD)
                for k in range(KD):
                    ins = pe.transpose(PS[k // 4][:, (k % 4) * P:(k % 4 + 1) * P], xv[:, k, :], IDENT[:])
                ins.then_inc(s_tw, 1)

            def up(n, p, r, use, kept=False):
                pe.wait_ge(s_xgt, 2 * n + 3)
                weights = [weights_of(p, two, kept) for two in range(2)]
                for w13, _, slot in weights:
                    pe.wait_ge(s_w13[slot], 32 * loads(slot, r, use + 1))
                for k in range(KD):
                    for two in range(2):
                        at = two * CAP
                        ins = pe.matmul(PS[2 + p][at:at + CAP, :], XGT[p][:, k, at:at + CAP], weights[two][0][:, k, :],
                                        start=(k == 0), stop=(k == KD - 1), tile_position=(0, at), skip_group_check=True)
                        if k == KD - 1:
                            ins.then_inc(s_hw, 1)

            def turn_h(n, p):
                pe.wait_ge(s_hg, n + 1)
                pe.wait_ge(s_ht, n + 1)
                hv = HG[p].rearrange("t (p j) -> t j p", j=2)
                for j in range(2):
                    ins = pe.transpose(PS[4][:, j * P:(j + 1) * P], hv[:, j, :], IDENT[:])
                ins.then_inc(s_htw, 1)

            def down(n, p, r, use, kept=False):
                pe.wait_ge(s_ht, n + 2)
                pe.wait_ge(s_ya, n + 1)
                pe.wait_ge(s_yd, n + 1)
                weights = [weights_of(p, two, kept) for two in range(2)]
                for _, w2, slot in weights:
                    pe.wait_ge(s_w2[slot], 16 * loads(slot, r, use + 1))
                for half in range(2):
                    for j in range(2):
                        for two in range(2):
                            at = two * CAP
                            ins = pe.matmul(PS[5 + half][at:at + CAP, :], HT[p][:, j, at:at + CAP],
                                            weights[two][1][:, j, half * 512:(half + 1) * 512],
                                            start=(j == 0), stop=(j == 1), tile_position=(0, at), skip_group_check=True)
                            if half == 1 and j == 1:
                                ins.then_inc(s_yw, 1)

            pe.sem_inc(s_pmu, 1)
            with pe.Fori(0, rounds) as r:
                base = r * NPAIR
                for j in range(2 * NT):
                    i, k = j // 2, j % 2
                    n = ROWS[TILE_ORDER[i]]
                    pe.wait_ge(s_pm, r * (2 * NT) + j + 1)
                    by_pair = OHV[0:n, k, i, :].rearrange("p (q two) -> p q two", two=2)
                    for two in range(2):
                        at = two * CAP
                        ins = pe.matmul(PS[B_O][at:at + CAP, 0:NPAIR], PM[0:n, j % NPM, :], by_pair[:, :, two], start=(j == 0),
                                        stop=(j == 2 * NT - 1), tile_position=(0, at), skip_group_check=True)
                    if j < 2 * NT - 1:
                        ins.then_inc(s_pmu, 1)
                ins.then_inc(s_tab, 1)
                pe.wait_ge(s_tab, r + 1)
                pe.sem_inc(s_pmu, 1)
                half_n = r * (NPAIR // 2)
                turn(base, 0, half_n)
                turn(base + 1, 1, half_n)
                up(base, 0, r, 0)
                turn_h(base, 0)

                def two_pairs(i, last=False):
                    for j in range(2):
                        q = base + i * 2 + 1 + j
                        p = 1 - j
                        turn(q + 1, 1 - p, half_n + i + 1)
                        up(q, p, r, i + j, kept=last and j == 1)
                        down(q - 1, 1 - p, r, i)
                        turn_h(q, p)

                with pe.Fori(0, NPAIR // 2 - 2) as i:
                    two_pairs(i)
                two_pairs(NPAIR // 2 - 2, last=True)
                q = base + NPAIR - 1
                up(q, 1, r, NPAIR // 2 - 1)
                down(q - 1, 0, r, NPAIR // 2 - 1, kept=True)
                turn_h(q, 1)
                down(q, 1, r, NPAIR // 2 - 1)


_INS = ["x_prompt", "x_sample", "state_hgrn", "state_rglru", "state_conv", "lower_bounds", "ln1_g", "w_in",
        "hgrn_norm_g", "conv_w", "conv_b", "lru_wx", "lru_bx", "lru_wa", "lru_ba", "lru_lambda", "w_out", "ln2_g",
        "router_wg", "router_bg", "router_we", "router_be", "exp_w1", "exp_w3", "exp_w2", "final_g"]
_OUTS = [(1, SEQ, D), (NS, 1, D), (1, 1, NH, P, P), (1, 1, 512), (1, 1, 3, 512),
         (1, NS, NH, P, P), (1, NS, 512), (1, NS, 3, 512)]


def kernel(**inputs):
    import numpy as _np
    import concourse.bacc as _bacc
    from concourse.bass_utils import run_bass_kernel_spmd as _run

    nc = _bacc.Bacc("TRN2", target_bir_lowering=False, num_devices=1)
    arrays, args = {}, []
    for name in _INS:
        a = _np.ascontiguousarray(inputs[name])
        arrays[f"in_{name}"] = a
        args.append(nc.dram_tensor(f"in_{name}", a.shape, F32, kind="ExternalInput").ap())
    for i, shape in enumerate(_OUTS):
        args.append(nc.dram_tensor(f"out_{i}", shape, F32, kind="ExternalOutput").ap())
    build(nc, *args)
    r = _run(nc, [arrays], core_ids=[0])
    return tuple(r.results[0][f"out_{i}"] for i in range(len(_OUTS)))
```
